# Optimizing a Trainium2 kernel written in Bass

```python
import math
import jax, jax.numpy as jnp
from jax import lax
import numpy as np

D_MODEL = 1024
BATCH = 1
SEQ = 1024
DEPTH = 1

MEM_LEN = 256
ML_HEADS = 4
ML_DHEAD = 128
SB_HEADS = 4
SB_DHEAD = 128
ML_WIDTH = ML_HEADS * ML_DHEAD
SB_WIDTH = SB_HEADS * SB_DHEAD
D_MIX = ML_WIDTH + SB_WIDTH
CONV_W = 4
ML_CHUNK = 128
SB_BLOCK = 128
IN_SIZES = (ML_WIDTH, ML_WIDTH, ML_WIDTH, ML_WIDTH, ML_HEADS, ML_HEADS, SB_WIDTH, SB_WIDTH, SB_WIDTH)
D_IN = 4 * ML_WIDTH + 2 * ML_HEADS + 3 * SB_WIDTH
XA_HEADS = 4
XA_DHEAD = D_MODEL // XA_HEADS
N_GROUPS = 4
EXP_PER_GROUP = 4
TOP_K = 2
D_EXPERT = 512
EPS = 1e-6

kernel_name = 'hybrid_mlstm_stickbreak_hmoe'

def rmsnorm(x, g):
    x32 = x.astype(jnp.float32)
    y = x32 * lax.rsqrt(jnp.mean(x32 * x32, axis=-1, keepdims=True) + EPS)
    return y.astype(x.dtype) * g

def head_rmsnorm(y, g):
    H, d = y.shape[-2], y.shape[-1]
    y32 = y.astype(jnp.float32)
    y32 = y32 * lax.rsqrt(jnp.mean(y32 * y32, axis=-1, keepdims=True) + EPS)
    return y32.astype(g.dtype) * g.reshape(H, d)

def causal_conv(x, w, b):
    S = x.shape[1]
    xp = jnp.pad(x, ((0, 0), (CONV_W - 1, 0), (0, 0)))
    y = b
    for tap in range(CONV_W):
        y = y + xp[:, tap:tap + S] * w[tap]
    return y

def mlstm_chunkwise(q, k, v, i_pre, f_pre):
    B, S, H, d = q.shape
    L = ML_CHUNK
    nc = S // L
    f32 = jnp.float32

    def chunks(t):
        return t.astype(f32).reshape(B, nc, L, H, d).transpose(1, 0, 3, 2, 4)

    def gchunks(t):
        return t.astype(f32).reshape(B, nc, L, H).transpose(1, 0, 3, 2)

    qc = chunks(q)
    kc = chunks(k) * (d ** -0.5)
    vc = chunks(v)
    ic = gchunks(i_pre)
    bc = jnp.cumsum(jax.nn.log_sigmoid(gchunks(f_pre)), axis=-1)
    causal = jnp.tril(jnp.ones((L, L), dtype=bool))

    def step(carry, inp):
        C, n, m = carry
        q_, k_, v_, i_, b_ = inp
        logd = b_[..., :, None] - b_[..., None, :] + i_[..., None, :]
        logd = jnp.where(causal, logd, -jnp.inf)
        inter = b_ + m[..., None]
        m_t = jnp.maximum(inter, jnp.max(logd, axis=-1))
        s = jnp.einsum('bhtd,bhsd->bhts', q_, k_) * jnp.exp(logd - m_t[..., None])
        w_inter = jnp.exp(inter - m_t)
        num = jnp.einsum('bhts,bhsd->bhtd', s, v_) + w_inter[..., None] * jnp.einsum('bhvk,bhtk->bhtv', C, q_)
        den = jnp.sum(s, axis=-1) + w_inter * jnp.einsum('bhk,bhtk->bht', n, q_)
        h = num / jnp.maximum(jnp.abs(den), jnp.exp(-m_t))[..., None]
        b_last = b_[..., -1]
        end_log = b_last[..., None] - b_ + i_
        m_new = jnp.maximum(b_last + m, jnp.max(end_log, axis=-1))
        w_old = jnp.exp(b_last + m - m_new)
        w_s = jnp.exp(end_log - m_new[..., None])
        C_new = w_old[..., None, None] * C + jnp.einsum('bhs,bhsv,bhsk->bhvk', w_s, v_, k_)
        n_new = w_old[..., None] * n + jnp.einsum('bhs,bhsk->bhk', w_s, k_)
        return (C_new, n_new, m_new), h

    init = (jnp.zeros((B, H, d, d), f32), jnp.zeros((B, H, d), f32), jnp.zeros((B, H), f32))
    _, hc = lax.scan(step, init, (qc, kc, vc, ic, bc))
    return hc.transpose(1, 0, 3, 2, 4).reshape(B, S, H, d)

def stick_breaking(q, k, v):
    B, S, H, d = q.shape
    f32 = jnp.float32
    qh = q.astype(f32).transpose(0, 2, 1, 3) * (d ** -0.5)
    kh = k.astype(f32).transpose(0, 2, 1, 3)
    vh = v.astype(f32).transpose(0, 2, 1, 3)
    outs = []
    for blk in range(S // SB_BLOCK):
        t0 = blk * SB_BLOCK
        t1 = t0 + SB_BLOCK
        z = jnp.einsum('bhtd,bhsd->bhts', qh[:, :, t0:t1], kh[:, :, :t1])
        t_idx = t0 + jnp.arange(SB_BLOCK)[:, None]
        s_idx = jnp.arange(t1)[None, :]
        mask = s_idx < t_idx
        log_1m = jnp.where(mask, jax.nn.log_sigmoid(-z), 0.0)
        tail = lax.cumsum(log_1m, axis=3, reverse=True) - log_1m
        a = jnp.where(mask, jnp.exp(jax.nn.log_sigmoid(z) + tail), 0.0)
        outs.append(jnp.einsum('bhts,bhsd->bhtd', a, vh[:, :, :t1]))
    o = jnp.concatenate(outs, axis=2)
    return o.transpose(0, 2, 1, 3)

def parallel_mixer(h, w_in, conv_w, conv_b, i_bias, f_bias, ml_head_g, sb_head_g, w_out):
    B, S, _ = h.shape
    proj = h @ w_in
    cuts = []
    acc = 0
    for sz in IN_SIZES[:-1]:
        acc += sz
        cuts.append(acc)
    mq, mk, mv, mo, mi, mf, sq, sk, sv = jnp.split(proj, cuts, axis=-1)
    qk = jax.nn.silu(causal_conv(jnp.concatenate([mq, mk], axis=-1), conv_w, conv_b))
    mq, mk = qk[..., :ML_WIDTH], qk[..., ML_WIDTH:]
    hs = (B, S, ML_HEADS, ML_DHEAD)
    h_ml = mlstm_chunkwise(mq.reshape(hs), mk.reshape(hs), mv.reshape(hs), mi + i_bias, mf + f_bias)
    h_ml = jax.nn.sigmoid(mo).reshape(hs) * head_rmsnorm(h_ml.astype(h.dtype), ml_head_g)
    ss = (B, S, SB_HEADS, SB_DHEAD)
    h_sb = stick_breaking(sq.reshape(ss), sk.reshape(ss), sv.reshape(ss))
    h_sb = head_rmsnorm(h_sb.astype(h.dtype), sb_head_g)
    y = jnp.concatenate([h_ml.reshape(B, S, ML_WIDTH), h_sb.reshape(B, S, SB_WIDTH)], axis=-1)
    return y @ w_out

def memory_attention(h, m, w_mq, w_mk, w_mv, w_mo):
    B, S, D = h.shape
    M = m.shape[1]
    q = (h @ w_mq).reshape(B, S, XA_HEADS, XA_DHEAD)
    k = (m @ w_mk).reshape(B, M, XA_HEADS, XA_DHEAD)
    v = (m @ w_mv).reshape(B, M, XA_HEADS, XA_DHEAD)
    s = jnp.einsum('bshd,bmhd->bhsm', q, k).astype(jnp.float32) * (XA_DHEAD ** -0.5)
    p = jax.nn.softmax(s, axis=-1).astype(v.dtype)
    o = jnp.einsum('bhsm,bmhd->bshd', p, v).reshape(B, S, D)
    return o @ w_mo

def hier_moe(h, w_rg, b_rg, w_re, b_re, w_e1, w_e3, w_e2):
    B, S, D = h.shape
    t = h.reshape(-1, D)
    n_tok = t.shape[0]
    p_g = jax.nn.softmax((t @ w_rg + b_rg).astype(jnp.float32), axis=-1)
    onehot_g = jax.nn.one_hot(jnp.argmax(p_g, axis=-1), N_GROUPS, dtype=jnp.float32)
    p_sel = jnp.sum(p_g * onehot_g, axis=-1)
    e_logits = (t @ w_re + b_re).astype(jnp.float32).reshape(n_tok, N_GROUPS, EXP_PER_GROUP)
    e_sel = jnp.einsum('nge,ng->ne', e_logits, onehot_g)
    top_w, top_i = lax.top_k(jax.nn.softmax(e_sel, axis=-1), TOP_K)
    top_w = top_w / jnp.sum(top_w, axis=-1, keepdims=True)
    e_gate = jnp.sum(jax.nn.one_hot(top_i, EXP_PER_GROUP, dtype=jnp.float32) * top_w[..., None], axis=1)
    gate = (onehot_g[:, :, None] * (p_sel[:, None] * e_gate)[:, None, :]).astype(h.dtype)
    y = jnp.zeros((n_tok, D), h.dtype)
    for g in range(N_GROUPS):
        a = jnp.einsum('nd,edf->nef', t, w_e1[g])
        u = jnp.einsum('nd,edf->nef', t, w_e3[g])
        y = y + jnp.einsum('nef,efd->nd', jax.nn.silu(a) * u * gate[:, g, :, None], w_e2[g])
    return y.reshape(B, S, D)

def setup_inputs(seed: int = 0) -> dict:
    key = jax.random.key(seed)
    ks = jax.random.split(key, 32)
    nrm = jax.random.normal
    f32 = jnp.float32
    G, E, F = N_GROUPS, EXP_PER_GROUP, D_EXPERT
    return {
        'x': nrm(ks[0], (BATCH, SEQ, D_MODEL), f32),
        'mem': nrm(ks[1], (BATCH, MEM_LEN, D_MODEL), f32),
        'ln_mix': 1.0 + 0.02 * nrm(ks[2], (DEPTH, D_MODEL), f32),
        'w_in': nrm(ks[3], (DEPTH, D_MODEL, D_IN), f32) * D_MODEL ** -0.5,
        'conv_w': nrm(ks[4], (DEPTH, CONV_W, 2 * ML_WIDTH), f32) * CONV_W ** -0.5,
        'conv_b': 0.02 * nrm(ks[5], (DEPTH, 2 * ML_WIDTH), f32),
        'i_bias': 0.1 * nrm(ks[6], (DEPTH, ML_HEADS), f32),
        'f_bias': jnp.linspace(3.0, 6.0, ML_HEADS, dtype=f32)[None, :] + 0.1 * nrm(ks[7], (DEPTH, ML_HEADS), f32),
        'ml_head_g': 1.0 + 0.02 * nrm(ks[8], (DEPTH, ML_WIDTH), f32),
        'sb_head_g': 1.0 + 0.02 * nrm(ks[9], (DEPTH, SB_WIDTH), f32),
        'w_out': nrm(ks[10], (DEPTH, D_MIX, D_MODEL), f32) * D_MIX ** -0.5,
        'ln_mem': 1.0 + 0.02 * nrm(ks[11], (DEPTH, D_MODEL), f32),
        'ln_memkv': 1.0 + 0.02 * nrm(ks[12], (DEPTH, D_MODEL), f32),
        'w_mq': nrm(ks[13], (DEPTH, D_MODEL, D_MODEL), f32) * D_MODEL ** -0.5,
        'w_mk': nrm(ks[14], (DEPTH, D_MODEL, D_MODEL), f32) * D_MODEL ** -0.5,
        'w_mv': nrm(ks[15], (DEPTH, D_MODEL, D_MODEL), f32) * D_MODEL ** -0.5,
        'w_mo': nrm(ks[16], (DEPTH, D_MODEL, D_MODEL), f32) * D_MODEL ** -0.5,
        'ln_ffn': 1.0 + 0.02 * nrm(ks[17], (DEPTH, D_MODEL), f32),
        'w_rg': nrm(ks[18], (DEPTH, D_MODEL, G), f32) * D_MODEL ** -0.5,
        'b_rg': 0.01 * nrm(ks[19], (DEPTH, G), f32),
        'w_re': nrm(ks[20], (DEPTH, D_MODEL, G * E), f32) * D_MODEL ** -0.5,
        'b_re': 0.01 * nrm(ks[21], (DEPTH, G * E), f32),
        'w_e1': nrm(ks[22], (DEPTH, G, E, D_MODEL, F), f32) * D_MODEL ** -0.5,
        'w_e3': nrm(ks[23], (DEPTH, G, E, D_MODEL, F), f32) * D_MODEL ** -0.5,
        'w_e2': nrm(ks[24], (DEPTH, G, E, F, D_MODEL), f32) * F ** -0.5,
        'ln_final': 1.0 + 0.02 * nrm(ks[25], (D_MODEL,), f32),
    }

def reference(x, mem, ln_mix, w_in, conv_w, conv_b, i_bias, f_bias, ml_head_g, sb_head_g, w_out,
              ln_mem, ln_memkv, w_mq, w_mk, w_mv, w_mo, ln_ffn, w_rg, b_rg, w_re, b_re,
              w_e1, w_e3, w_e2, ln_final):
    for l in range(DEPTH):
        h = rmsnorm(x, ln_mix[l])
        x = x + parallel_mixer(h, w_in[l], conv_w[l], conv_b[l], i_bias[l], f_bias[l],
                               ml_head_g[l], sb_head_g[l], w_out[l])
        h = rmsnorm(x, ln_mem[l])
        m = rmsnorm(mem, ln_memkv[l])
        x = x + memory_attention(h, m, w_mq[l], w_mk[l], w_mv[l], w_mo[l])
        h = rmsnorm(x, ln_ffn[l])
        x = x + hier_moe(h, w_rg[l], b_rg[l], w_re[l], b_re[l], w_e1[l], w_e3[l], w_e2[l])
    return rmsnorm(x, ln_final)


_drawn_inputs = setup_inputs


def setup_inputs(seed=0):
    import zlib

    import numpy as np

    out = dict(_drawn_inputs(seed))
    spreads = {}
    factors = {'conv_b': 4.744,
     'i_bias': 64.0,
     'ml_head_g': 4.627,
     'sb_head_g': 3.03,
     'ln_mem': 8.0,
     'ln_memkv': 7.426,
     'ln_ffn': 2.994,
     'b_rg': 6.249,
     'b_re': 18.896,
     'ln_final': 7.882}
    for name, (base, spread) in spreads.items():
        noise = np.random.default_rng([zlib.crc32(name.encode()), seed]).standard_normal(out[name].shape)
        drawn = base * np.exp(spread * noise) if base else spread * noise
        out[name] = __import__('jax').numpy.asarray(drawn.astype(out[name].dtype))
    for name, factor in factors.items():
        out[name] = (out[name] * factor).astype(out[name].dtype)
    return out
```

```python
from contextlib import ExitStack

import concourse.bass as bass
from concourse import mybir

ALU = mybir.AluOpType
ACT = mybir.ActivationFunctionType
AX = mybir.AxisListType
F32 = mybir.dt.float32
F32R = mybir.dt.float32r
I32 = mybir.dt.int32

P = 128
BANK = 512
EPS = 1e-6
NEG = -1.0e30
DUMP = []


def hybrid_layer(nc, t, out, xg, dbg=None):
    SEQ, D = t["x"].shape[1:]
    MEM = t["mem"].shape[1]
    NT = SEQ // P
    KD = D // P
    MT = MEM // P
    MH = t["i_bias"].shape[1]
    DH = P
    MW = MH * DH
    CW = t["conv_w"].shape[1]
    XH = 4
    XD = D // XH
    NG = t["w_e1"].shape[1]
    NE = t["w_e1"].shape[2]
    E = NG * NE
    F = t["w_e1"].shape[4]
    KF = F // P
    HALF = BANK // P
    NH2 = SEQ // BANK
    QSCALE = float(DH) ** -0.5
    XSCALE = float(XD) ** -0.5
    NR = NG + E
    MAXB = (2 * SEQ + E * (P - 1)) // P
    SLOT_BLOCKS = MAXB + 2
    assert MW == BANK and F == BANK and D == 2 * BANK and MH == 4

    x_d = t["x"][0].rearrange("(t p) d -> t p d", p=P)
    mem_d = t["mem"][0].rearrange("(t p) d -> t p d", p=P)
    out_d = out[0].rearrange("(t p) d -> t p d", p=P)

    PC = BANK // 2
    W_IN = t["w_in"][0]
    OFF = dict(mq=0, mk=MW, mv=2 * MW, mo=3 * MW, gates=4 * MW, sq=4 * MW + 2 * MH,
               sk=5 * MW + 2 * MH, sv=6 * MW + 2 * MH)

    def piece_d(name, c0):
        return t[name][0][:, c0:c0 + PC].rearrange("(k p) n -> p k n", p=P)

    pieces = []
    for nm, who in (("mq", "act"), ("mk", "act"), ("mv", "act"), ("mo", "act"), ("sq", "act"),
                    ("sk", "dve"), ("sv", "act")):
        for c in range(2):
            pieces.append((nm, c, piece_d("w_in", OFF[nm] + c * PC), 4, who))
    for nm, n, who in (("w_out", 4, "dve"), ("w_mk", 1, "act"), ("w_mv", 1, "act"), ("w_mq", 4, "act"),
                       ("w_mo", 4, "dve")):
        for c in range(4):
            pieces.append((nm, c, piece_d(nm, c * PC), n, who))
    PIDX = {(x[0], x[1]): i for i, x in enumerate(pieces)}
    NP = len(pieces)

    tiles = [("gates", 0, i, "dve") for i in range(NH2)]
    for nm, c, _, n, who in pieces:
        if (nm, c) == ("w_mo", 0):
            tiles += [("oT", 0, i, "dve") for i in range(2 * KD)]
        tiles += [(nm, c, i, who) for i in range(n)]
    TIDX = {(n, c, i): k for k, (n, c, i, _) in enumerate(tiles)}
    evac_no = []
    seen = {"act": 0, "dve": 0}
    for *_, w in tiles:
        seen[w] += 1
        evac_no.append((w, seen[w]))
    RING = 4

    def piece_end(p):
        nm, c, _, n, _ = pieces[p]
        return TIDX[nm, c, n - 1] + 1

    with ExitStack() as ctx:
        def sb(name, shape, dt=F32):
            return ctx.enter_context(nc.sbuf_tensor(name, shape, dt))

        def sem(name):
            return ctx.enter_context(nc.semaphore(name))

        KB = 256
        fence_base = nc.sbuf_base
        sb("fence", [P, 178 * KB + 128])
        base = -(-fence_base // 32) * 32

        def region(name, at, words, dt=F32):
            return nc.alloc_sbuf_tensor_at(name, [P, words], dt, offset=base + 4 * at)

        RS = 64 * KB
        arena = region("arena", 0, 178 * KB + 128)
        act_split = region("act_split", 0, 64 * KB, F32R)
        RW = RS + 74 * KB + 128
        w_split = region("w_split", RW, 32 * KB, F32R)
        raw = arena[:, RW + 32 * KB:RW + 40 * KB].rearrange("p (k n) -> p k n", k=KD)

        def hi_lo(tensor, at, a, b):
            return [tensor[:, at + i * a * b:at + (i + 1) * a * b].rearrange("p (a b) -> p a b", a=a) for i in range(2)]

        def view(at, *shape):
            n = 1
            for q in shape:
                n *= q
            v = arena[:, at:at + n]
            if len(shape) == 2:
                v = v.rearrange("p (a b) -> p a b", a=shape[0])
            return v

        hS = hi_lo(act_split, 0, KD, SEQ)
        wS = [hi_lo(w_split, i * 16 * KB, KD, PC) for i in range(2)]
        RP = RS
        mqT = view(RP, MH, SEQ)
        mkT = view(RP + 16 * KB, MH, SEQ)
        vaug = arena[:, RP + 32 * KB:RP + 32 * KB + NT * MH * 129].rearrange(
            "p (t h e) -> p t h e", t=NT, h=MH)
        gate_o = view(RP + 49 * KB, NT, MW)
        sqT = view(RP, MH, SEQ)
        skT = view(RP + 16 * KB, MH, SEQ)
        svn = view(RP + 32 * KB, NT, MW)
        kN = view(RW + 16 * KB, NT, MW)
        xs = view(RP, NT, D)
        x1 = view(RP, NT, D)
        qT = view(RP + 32 * KB, KD, SEQ)
        kTm = view(RP + 64 * KB, KD, MEM)
        mS = hi_lo(region("mem_split", RP + 32 * KB, 16 * KB, F32R), 0, KD, MEM)
        mems = view(RP + 48 * KB, MT, D)
        pT = view(RW + 16 * KB, 2 * XH, BANK)

        consts = {n: sb(n, [P, P]) for n in ("ident", "uincl", "ustrict", "ones")}
        ident, uincl, ustrict, ones = (consts[n] for n in ("ident", "uincl", "ustrict", "ones"))
        sel = sb("sel", [MH, MH, P])
        NV = 4 * KD + CW * 2 * MH + 2 * MH + MH
        vec_rows = sb("vec_rows", [NV, P])
        vecT = sb("vecT", [P, NV])
        GW = 3 * 32 + MH
        gbias = sb("gbias", [GW, 1])
        rbias = sb("rbias", [NR, 1])
        mlg = sb("mlg", [P, MW])
        wpad = view(RW + 16 * KB, KD, GW)
        wpadS = hi_lo(region("wpad_split", RW + 20 * KB, 8 * KB, F32R), 0, KD, GW)
        eps_col = sb("eps_col", [P, 1])
        ss = sb("ss", [P, NT])
        rstd = sb("rstd", [P, NT])
        lnt = sb("lnt", [P, NT])
        work = sb("work", [P, 20 * KB])
        htmp = work[:, 0:2 * D].rearrange("p (b d) -> p b d", b=2)
        pnat = htmp
        tt = [work[:, 2 * D + i * BANK:2 * D + (i + 1) * BANK] for i in range(2)]
        vmem = work[:, 3 * D:5 * D].rearrange("p (m d) -> p m d", m=MT)
        cin = work[:, 2 * D:2 * D + 2 * (SEQ + 4)].rearrange("p (b s) -> p b s", b=2)
        psum = ctx.enter_context(nc.psum_tensor("psum", [P, 8, BANK], F32))

        stack = work[:, 0:SEQ]
        R_G, R_F, R_L, R_K, R_M = range(5)
        grow = [work[0:MH, i * SEQ:(i + 1) * SEQ] for i in range(5)]
        mrow = grow[R_M]
        GC = GW
        cols = work[:, SEQ:SEQ + NT * GC].rearrange("p (c g) -> p c g", c=NT)
        gcol, wicol, flcol, wscol = (cols[:, :, 32 * i:32 * i + MH] for i in range(4))
        woldB = work[:, SEQ + NT * GC:SEQ + NT * GC + NT * MH].rearrange("p (h c) -> p h c", h=MH)
        mprev = sb("mprev", [MH, NT])
        wold = sb("wold", [MH, NT])
        S0 = RW
        NZ, NLT, NL, NX, NRB = 4, 2, 3, 4, 3
        bufs = [view(S0 + i * BANK, BANK) for i in range(16)] + [work[:, i * BANK:(i + 1) * BANK] for i in range(4)]
        zs, bufs = bufs[:NZ], bufs[NZ:]
        lt, bufs = bufs[:NLT], bufs[NLT:]
        Lb, bufs = bufs[:NL], bufs[NL:]
        ex, bufs = bufs[:NX], bufs[NX:]
        Rb, bufs = bufs[:NRB], bufs[NRB:]
        osq, ors, of = bufs[:3]
        E1 = DH + 1
        Dm = [view(S0 + i * BANK, BANK) for i in range(2)]
        Pm = [view(S0 + (2 + i) * BANK, BANK) for i in range(2)]
        vsb = [view(S0 + 4 * BANK + i * MH * E1, MH, E1) for i in range(2)]
        inter = view(S0 + 4 * BANK + 2 * MH * E1, MH, E1)
        wk = SEQ + NT * GC + NT * MH
        CT = [work[:, wk + i * MH * E1:wk + (i + 1) * MH * E1].rearrange("p (h e) -> p h e", h=MH) for i in range(2)]
        wk += 2 * MH * E1
        junk = work[:, wk:wk + DH]
        wk += DH
        assert wk <= 4 * SEQ
        mss = sb("mss", [P, NT * MH])
        mden = sb("mden", [P, NT, MH])
        mfac = sb("mfac", [P, NT, MH])

        G_MIX, G_KV, G_MEM, G_FFN = 0, KD, 2 * KD, 3 * KD
        V_CW = 4 * KD
        V_CB = V_CW + CW * 2 * MH
        V_SBG = V_CB + 2 * MH

        vec_in = sem("vec_in")
        x_in = [sem(f"x_in{i}") for i in range(NT)]
        mem_in = sem("mem_in")
        raw_in, w_hi, w_lo = sem("raw_in"), sem("w_hi"), sem("w_lo")
        pad_hi, pad_lo = sem("pad_hi"), sem("pad_lo")
        scaled, hi_part, ym_hi, o_made, o_hi, oT_hi = (
            sem(n) for n in ("scaled", "hi_part", "ym_hi", "o_made", "o_hi", "oT_hi"))
        const_made = sem("const_made")
        pool_chain = sem("pool_chain")
        dve_chain = sem("dve_chain")
        act_chain = sem("act_chain")
        vec_tr = sem("vec_tr")
        vecT_ready = sem("vecT_ready")
        h_made = sem("h_made")
        h_trans = sem("h_trans")
        hT_part = sem("hT_part")
        tile_out = sem("tile_out")
        evac = {"act": sem("evac_act"), "dve": sem("evac_dve")}
        conv_done = sem("conv_done")
        silu_done = sem("silu_done")
        gate_pe = sem("gate_pe")
        gate_dve = sem("gate_dve")
        gate_act = sem("gate_act")
        z_ready, zs_done, ab_done, l1_done, L_done = (sem(n) for n in ("z_ready", "zs_done", "ab_done", "l1_done", "L_done"))
        Lmasked, R_done, tail_ready, ex_done, ex_masked = (
            sem(n) for n in ("Lmasked", "R_done", "tail_ready", "ex_done", "ex_masked"))
        a_done, av_done, osq_done, ossq_ready, ors_done, sb_out = (
            sem(n) for n in ("a_done", "av_done", "osq_done", "ossq_ready", "ors_done", "sb_out"))
        kn_ready, kn_done = sem("kn_ready"), sem("kn_done")
        mb_ready, kq_ready, D_done, D_masked, W_done, Pm_done = (
            sem(n) for n in ("mb_ready", "kq_ready", "D_done", "D_masked", "W_done", "Pm_done"))
        vs_done, num_ready, inter_ready, U_ready, inter_done, num_done, CT_done = (
            sem(n) for n in ("vs_done", "num_ready", "inter_ready", "U_ready", "inter_done", "num_done", "CT_done"))
        mss_done, ml_fac, ml_rs, yn_done, yn_trans, ym_done = (
            sem(n) for n in ("mss_done", "ml_fac", "ml_rs", "yn_done", "yn_trans", "ym_done"))
        gate_scaled = sem("gate_scaled")
        wpad_in, lgT_done = sem("wpad_in"), sem("lgT_done")
        VEC_DMAS = 12
        sc_ready, mx_done, p_done, pn_done, pt_ready, pt_done = (
            sem(n) for n in ("sc_ready", "mx_done", "p_done", "pn_done", "pt_ready", "pt_done"))
        hn = view(RP + 64 * KB, NT, D)
        mslot = [view(RP + (32 + 16 * i) * KB, KD, BANK) for i in range(2)] + [view(16 * i * KB, KD, BANK) for i in range(4)]
        w1s, w3s = [mslot[0], mslot[3]], [mslot[1], mslot[4]]
        w2s = [w.rearrange("p k n -> p (k n)").rearrange("p (k n) -> p k n", k=KF) for w in (mslot[2], mslot[5])]
        RB = RP + 96 * KB
        xb = view(RB, D)
        xTb = view(RB + 4 * KB, KD, P)
        yb = view(RB + 8 * KB, D)
        sg = view(RB + 12 * KB, F)
        hh = view(RB + 14 * KB, F)
        hhT = view(RB + 16 * KB, KF, P)
        zero = view(RP + 61 * KB, D)
        yg_t = [[view(4 * (2 * i + c) * KB, D) for c in range(2)] for i in range(NT)]
        gfin = work[:, 4 * D:5 * D]
        otile = [view(RP + (64 + 4 * i) * KB, D) for i in range(2)]
        rpad = work[:, 2 * D:2 * D + KD * 100].rearrange("p (k r) -> p k r", k=KD)
        rpadS = hi_lo(region("rpad_split", RP + 32 * KB, 8 * KB, F32R), 0, KD, 100)
        lgT = work[0:NR, 3 * D:4 * D]
        carve = {"at": 0}

        def small(*shape):
            n = 1
            for q in shape:
                n *= q
            w = work[:, carve["at"]:carve["at"] + n]
            carve["at"] += n
            names = "abc"[:len(shape)]
            if len(shape) == 1:
                return w
            return w.rearrange("p (%s) -> p %s" % (" ".join(names), " ".join(names)),
                               **{k: q for k, q in zip(names, shape)})

        lg = small(NT, NR)
        elt = lg[:, :, NG:NR].rearrange("p t (g e) -> p t g e", g=NG)
        r4 = {n: small(NT, 4) for n in ("oh", "eq", "es", "t1", "t2", "tmp")}
        r1 = {n: small(NT) for n in ("mx", "left", "psel", "m1", "m2", "w1", "w2", "pos")}
        re = {n: small(NT, NG, NE) for n in ("A1", "A2", "M", "tot", "pos")}
        rc = {n: small(E) for n in ("cnt", "nb", "cum", "one", "base")}
        all_stored = sem("all_stored")
        pmx = sb("pmx", [P, NT, XH])
        psm = sb("psm", [P, NT, XH])
        idx = sb("idx", [P, 2, NT], I32)
        nb_i = sb("nb_i", [1, E], I32)
        cum_i = sb("cum_i", [1, E], I32)
        zero_made, zero_filled, routed, scattered, rt_pe, rt_dve, rt_act = (
            sem(n) for n in ("zero_made", "zero_filled", "routed", "scattered", "rt_pe", "rt_dve", "rt_act"))
        moe_in = [sem(f"moe_in{i}") for i in range(2)]
        xb_in, xt_ready, xT_done, a_ready, u_ready, sg_done, hh_done = (
            sem(n) for n in ("xb_in", "xt_ready", "xT_done", "a_ready", "u_ready", "sg_done", "hh_done"))
        ht_ready, hhT_done, y_ready, y_evac, y_stored = (
            sem(n) for n in ("ht_ready", "hhT_done", "y_ready", "y_evac", "y_stored"))
        gfin_in, moe_added, fin_rs, out_made = (
            sem(n) for n in ("gfin_in", "moe_added", "fin_rs", "out_made"))
        yg_in = [sem(f"yg_in{i}") for i in range(NT)]
        out_stored = [sem(f"out_stored{i}") for i in range(2)]

        dumped = sem("dumped")
        fin = sem("fin")

        steps = []
        for h in range(MH):
            for hf in range(NH2):
                top = HALF * (hf + 1)
                for j in range(top - 1, -1, -1):
                    lo = max(0, j * P - hf * BANK)
                    steps.append(dict(h=h, hf=hf, j=j, lo=lo, w=BANK - lo, first=(j == top - 1), last=(j == 0),
                                      diag=(j >= HALF * hf), g=h * NH2 + hf))
        NS = len(steps)

        def upto_diag(i):
            return sum(s["diag"] for s in steps[:i + 1])

        def upto_R(i):
            return sum(not s["last"] for s in steps[:i + 1])

        last_step = {s["g"]: i for i, s in enumerate(steps) if s["last"]}
        NGRP = MH * NH2

        def wait_evac(eng, n):
            w, c = evac_no[n]
            eng.wait_ge(evac[w], c)

        LATE = {PIDX["sq", 0], PIDX["w_out", 0]}

        def buffer_free(eng, p):
            if p >= 2:
                eng.wait_ge(tile_out, piece_end(p - 2))
            if p == 1:
                eng.wait_ge(tile_out, NH2)
            if p in (PIDX["sq", 0], PIDX["sq", 1]):
                eng.wait_ge(num_ready, NT)
                eng.wait_ge(num_done, NT)
            if p in (PIDX["w_out", 0], PIDX["w_out", 1]):
                eng.wait_ge(sb_out, NGRP)
                eng.wait_ge(av_done, NS)
            if p == PIDX["w_mo", 1]:
                eng.wait_ge(tile_out, TIDX["oT", 0, 2 * KD - 1] + 1)

        block = ctx.enter_context(nc.Block())

        @block.sync
        def _(sp):
            def load_raw(p):
                if p:
                    sp.wait_ge(w_lo, p)
                sp.dma_start(raw, pieces[p][2]).then_inc(raw_in, 16)

            for i in range(NT):
                sp.dma_start(xs[:, i, :], x_d[i]).then_inc(x_in[i], 16)
                if i == 0:
                    load_raw(0)
            xg_b = xg.rearrange("(b p) d -> b p d", p=P)
            for p in range(1, PIDX["mv", 1]):
                load_raw(p)
                if p == 2:
                    sp.wait_ge(zero_made, 1)
                if p >= 2:
                    for b in range(11 * (p - 2), min(11 * (p - 1), SLOT_BLOCKS)):
                        sp.dma_start(xg_b[b], zero).then_inc(zero_filled, 16)
            for p in range(PIDX["mv", 1], PIDX["w_out", 0] + 1):
                load_raw(p)
            sp.wait_ge(w_lo, PIDX["w_out", 0])
            sp.wait_ge(av_done, NS)
            sp.wait_ge(yn_trans, NT)
            for i in range(NT):
                sp.dma_start(x1[:, i, :], x_d[i]).then_inc(x_in[i], 16)
            for i in range(MT):
                sp.dma_start(mems[:, i, :], mem_d[i]).then_inc(mem_in, 16)
            for p in range(PIDX["w_out", 0] + 1, NP):
                load_raw(p)
            sp.wait_ge(tile_out, len(tiles))
            sp.wait_ge(rt_pe, NH2)

            def load_expert(par, e):
                for w, name in ((w1s, "w_e1"), (w3s, "w_e3"), (w2s, "w_e2")):
                    src = t[name][0].rearrange("g e d f -> (g e) d f")[bass.ds(e, 1)].rearrange(
                        "g (k p) n -> p (g k) n", p=P)
                    sp.dma_start(w[par], src).then_inc(moe_in[par], 16)

            for par in range(2):
                load_expert(par, par)
            sp.wait_ge(routed, 1)
            sp.dma_start(gfin, t["ln_final"].rearrange("(a d) -> a d", a=1).broadcast_to([P, D])).then_inc(gfin_in, 16)
            with sp.Fori(1, E // 2) as i:
                for par in range(2):
                    c = sp.value_load(cum_i[0:1, bass.ds(i * 2 + (par - 2), 1)], min_val=0, max_val=MAXB)
                    sp.wait_ge(y_ready, c + 1)
                    load_expert(par, i * 2 + par)
            for i in range(NT):
                sp.wait_ge(out_made, i + 1)
                sp.dma_start(out_d[i], otile[i % 2]).then_inc(out_stored[i % 2], 16)
            for i in range(2):
                sp.wait_ge(out_stored[i], 16 * NT // 2)
            if dbg is not None:
                sp.wait_ge(fin, 1)
                at = 0
                for n, (a0, ln) in enumerate(DUMP):
                    sp.dma_start(dbg[:, at:at + ln], arena[:, a0:a0 + ln]).then_inc(dumped, 16)
                    at += ln
                    sp.wait_ge(dumped, 16 * (n + 1))

        @block.gpsimd
        def _(pool):
            chain = [0]

            def link(ins):
                chain[0] += 1
                ins.then_inc(pool_chain, 1)
                pool.wait_ge(pool_chain, chain[0])

            g = nc.gpsimd
            g.memset(wpad, 0.0).then_inc(pool_chain, 1)
            g.memset(ident[:], 0.0).then_inc(pool_chain, 1)
            g.memset(uincl[:], 1.0).then_inc(pool_chain, 1)
            g.memset(ustrict[:], 1.0).then_inc(pool_chain, 1)
            g.memset(sel[:], 0.0).then_inc(pool_chain, 1)
            chain[0] = 5
            g.memset(ones[:], 1.0).then_inc(const_made, 1)
            g.memset(eps_col[:], EPS).then_inc(const_made, 1)
            pool.wait_ge(pool_chain, 5)
            for c in range(2):
                pool.dma_start(wpad[:, :, 32 * c:32 * c + MH], W_IN[:, OFF["gates"] + c * MH:OFF["gates"] + (c + 1) * MH]
                               .rearrange("(k p) n -> p k n", p=P)).then_inc(wpad_in, 16)
            g.affine_select(out=ident[:], in_=ident[:], compare_op=ALU.not_equal, fill=1.0, base=0,
                            pattern=[[-1, P]], channel_multiplier=1).then_inc(const_made, 1)
            g.affine_select(out=uincl[:], in_=uincl[:], compare_op=ALU.is_ge, fill=0.0, base=0,
                            pattern=[[-1, P]], channel_multiplier=1).then_inc(const_made, 1)
            g.affine_select(out=ustrict[:], in_=ustrict[:], compare_op=ALU.is_gt, fill=0.0, base=0,
                            pattern=[[1, P]], channel_multiplier=-1).then_inc(const_made, 1)
            g.affine_select(out=sel[:], in_=sel[:], compare_op=ALU.not_equal, fill=1.0, base=0,
                            pattern=[[-1, MH], [0, P]], channel_multiplier=1).then_inc(const_made, 1)
            g.memset(zero, 0.0).then_inc(zero_made, 1)

            pool.wait_ge(vec_in, VEC_DMAS * 16)
            for i in range(NT):
                wait_evac(pool, TIDX["mo", 1, i // 2])
                g.tensor_tensor(gate_o[:, i, :], gate_o[:, i, :], mlg[:], ALU.mult).then_inc(gate_scaled, 1)

            for c in range(NT):
                pool.wait_ge(D_done, c + 1)
                v4 = Dm[c % 2].rearrange("p (h s) -> p h s", h=MH)
                g.affine_select(out=v4, in_=v4, compare_op=ALU.is_ge, fill=-NEG, base=0,
                                pattern=[[0, MH], [1, P]], channel_multiplier=-1).then_inc(D_masked, 1)

            for k in range(NS + 3):
                i = k - 1
                if 0 <= i < NS:
                    s = steps[i]
                    lo = s["lo"]
                    L, R, Rn = Lb[i % NL], Rb[i % NRB], Rb[(i + 1) % NRB]
                    pool.wait_ge(L_done, i + 1)
                    if s["diag"]:
                        g.affine_select(out=L[:, lo:lo + P], in_=L[:, lo:lo + P], compare_op=ALU.is_gt,
                                        fill=0.0, base=0, pattern=[[1, P]], channel_multiplier=-1).then_inc(Lmasked, 1)
                        pool.wait_ge(Lmasked, upto_diag(i))
                    if not s["last"]:
                        if i >= 2:
                            pool.wait_ge(tail_ready, i - 1)
                        if i and upto_R(i - 1):
                            pool.wait_ge(R_done, upto_R(i - 1))
                        if lo:
                            link(g.memset(Rn[:, 0:lo], 0.0))
                        if s["first"]:
                            g.tensor_copy(Rn[:, lo:BANK], L[:, lo:BANK]).then_inc(R_done, 1)
                        else:
                            g.tensor_tensor(Rn[:, lo:BANK], R[:, lo:BANK], L[:, lo:BANK], ALU.add).then_inc(R_done, 1)
                i = k - 2
                if 0 <= i < NS and steps[i]["diag"]:
                    lo = steps[i]["lo"]
                    e = ex[i % NX][:, lo:lo + P]
                    pool.wait_ge(ex_done, i + 1)
                    g.affine_select(out=e, in_=e, compare_op=ALU.is_gt, fill=NEG, base=0, pattern=[[1, P]],
                                    channel_multiplier=-1).then_inc(ex_masked, 1)

            pool.wait_ge(tile_out, piece_end(PIDX["w_mq", 3]))
            link(g.memset(rpad, 0.0))
            pool.dma_start(rpad[:, :, 0:NG], t["w_rg"][0].rearrange("(k p) n -> p k n", p=P)).then_inc(wpad_in, 16)
            pool.dma_start(rpad[:, :, NG:NR], t["w_re"][0].rearrange("(k p) n -> p k n", p=P)).then_inc(wpad_in, 16)

            pool.wait_ge(zero_filled, 16 * SLOT_BLOCKS)
            pool.wait_ge(routed, 1)
            for i in range(NT):
                for c in range(2):
                    g.indirect_dma_start(out=xg, out_offset=bass.IndirectOffsetOnAxis(ap=idx[:, c, i:i + 1], axis=0),
                                         in_=hn[:, i, :], in_offset=None).then_inc(scattered, 16)
            pool.wait_ge(scattered, 16 * 2 * NT)
            xg_b = xg.rearrange("(b p) d -> b p d", p=P)
            for b in range(2):
                if b:
                    pool.wait_ge(xt_ready, 1)
                pool.dma_start(xb, xg_b[b]).then_inc(xb_in, 16)
            blk = pool.alloc_register("pool_block")
            pool.reg_mov(blk, 0)
            tot = pool.value_load(cum_i[0:1, E - 1:E], min_val=1, max_val=MAXB)
            with pool.Fori(0, tot) as b:
                pool.wait_ge(xt_ready, b + 2)
                g.dma_start(xb, xg_b[bass.ds(b + 2, 1)].rearrange("a p d -> p (a d)")).then_inc(xb_in, 16)
            pool.wait_ge(y_stored, (tot + 1) * 16)
            pool.sem_inc(all_stored, 1)
            pool.wait_ge(all_stored, 1)
            for i in range(NT):
                for c in range(2):
                    g.indirect_dma_start(out=yg_t[i][c], out_offset=None, in_=xg,
                                         in_offset=bass.IndirectOffsetOnAxis(ap=idx[:, c, i:i + 1], axis=0)).then_inc(yg_in[i], 16)

        @block.scalar
        def _(act):
            chain = [0]
            a = nc.scalar.activation

            def link(ins):
                chain[0] += 1
                ins.then_inc(act_chain, 1)
                act.wait_ge(act_chain, chain[0])

            def split_hi(p):
                act.wait_ge(raw_in, 16 * (p + 1))
                buffer_free(act, p)
                a(wS[p % 2][0], raw, ACT.Copy).then_inc(w_hi, 1)

            def begin_piece(p):
                if p + 1 < NP and p + 1 not in LATE:
                    split_hi(p + 1)

            def out_of(n):
                act.wait_ge(tile_out, n + 1)
                return psum[:, n % RING, :]

            at = 0
            for src, n in ((t["ln_mix"][0], KD), (t["ln_memkv"][0], KD), (t["ln_mem"][0], KD), (t["ln_ffn"][0], KD),
                           (t["conv_w"][0].rearrange("w c -> (w c)"), CW * 2 * MH), (t["conv_b"][0], 2 * MH),
                           (t["sb_head_g"][0], MH)):
                act.dma_start(vec_rows[at:at + n, :], src.rearrange("(k p) -> k p", p=P)).then_inc(vec_in, 16)
                at += n
            act.dma_start(gbias[0:MH, :], t["i_bias"].rearrange("a h -> h a")).then_inc(vec_in, 16)
            act.dma_start(gbias[32:32 + MH, :], t["f_bias"].rearrange("a h -> h a")).then_inc(vec_in, 16)
            act.dma_start(rbias[0:NG, :], t["b_rg"].rearrange("a h -> h a")).then_inc(vec_in, 16)
            act.dma_start(rbias[NG:NR, :], t["b_re"].rearrange("a h -> h a")).then_inc(vec_in, 16)
            act.dma_start(mlg[:], t["ml_head_g"].broadcast_to([P, MW])).then_inc(vec_in, 16)

            def rms_squares(i, src):
                link(a(htmp[:, i % 2, :], src, ACT.Square, accum_out=ss[:, i:i + 1]))

            def rms_scale(n):
                link(a(lnt[:, 0:n], ss[:, 0:n], ACT.Ln, bias=eps_col[:], scale=1.0 / D))
                link(a(rstd[:, 0:n], lnt[:, 0:n], ACT.Exp, scale=-0.5))

            def norm(j0, n, src, dst, natural=None):
                for i in range(n + 1):
                    j = j0 + i
                    if i < n:
                        if natural is None:
                            if j >= 2:
                                act.wait_ge(h_trans, j - 1)
                            o = htmp[:, j % 2, :]
                        else:
                            o = natural[:, i, :]
                        a(o, src[:, i, :], ACT.Copy, scale=rstd[:, i:i + 1]).then_inc(h_made, 1)
                    if i:
                        j -= 1
                        for q in range(2):
                            act.wait_ge(scaled, 2 * j + q + 1)
                            a(dst[0][:, HALF * q:HALF * (q + 1), (i - 1) * P:i * P],
                              tt[q].rearrange("p (k s) -> p k s", k=HALF), ACT.Copy).then_inc(hi_part, 1)

            nc.scalar.preload_act_table_set("natural_log_exp_and_others")
            act.wait_ge(const_made, 2)
            for i in range(NT):
                act.wait_ge(x_in[i], 16)
                rms_squares(i, xs[:, i, :])
            rms_scale(NT)
            split_hi(0)
            act.wait_ge(wpad_in, 32)
            a(wpadS[0], wpad, ACT.Copy).then_inc(pad_hi, 1)
            norm(0, NT, xs, hS)

            for ch in range(2 * MH + 1):
                if ch < 2 * MH:
                    nm, c = ("mq", "mk")[ch // MH], ch % MH
                    if c % 2 == 0:
                        begin_piece(PIDX[nm, c // 2])
                    for hf in range(NH2):
                        if hf == 0 and ch >= 2:
                            act.wait_ge(conv_done, ch - 1)
                        n = TIDX[nm, c // 2, (c % 2) * NH2 + hf]
                        a(cin[:, ch % 2, CW - 1 + hf * BANK:CW - 1 + (hf + 1) * BANK], out_of(n),
                          ACT.Copy).then_inc(evac["act"], 1)
                if ch >= 1:
                    c = ch - 1
                    act.wait_ge(conv_done, c + 1)
                    v = (mqT if c < MH else mkT)[:, c % MH, :]
                    a(v, v, ACT.Silu).then_inc(silu_done, 1)

            def N_evacs(nm, c, dst, func=ACT.Copy):
                begin_piece(PIDX[nm, c])
                for i in range(NT // 2):
                    o = out_of(TIDX[nm, c, i]).rearrange("p (t n) -> p t n", t=2)
                    a(dst[:, 2 * i:2 * i + 2, c * PC:(c + 1) * PC], o, func).then_inc(evac["act"], 1)

            def v_evacs(c):
                begin_piece(PIDX["mv", c])
                for i in range(NT // 2):
                    o = out_of(TIDX["mv", c, i]).rearrange("p (t h e) -> p t h e", t=2, h=2)
                    for q in range(2):
                        ins = a(vaug[:, 2 * i + q, 2 * c:2 * c + 2, 0:DH], o[:, q, :, :], ACT.Copy)
                    ins.then_inc(evac["act"], 1)

            nc.scalar.preload_act_table_set("natural_log_exp_and_others")
            v_evacs(0)
            act.wait_ge(gate_dve, 1)
            link(a(grow[R_L], grow[R_L], ACT.Exp))
            a(grow[R_L], grow[R_L], ACT.Ln, bias=1.0).then_inc(gate_act, 1)
            v_evacs(1)
            act.wait_ge(gate_dve, 2)
            a(stack[32:32 + MH, :], grow[R_L], ACT.Exp).then_inc(gate_act, 1)
            a(stack[64:64 + MH, :], grow[R_F], ACT.Exp, scale=-1.0).then_inc(gate_act, 1)
            a(stack[96:96 + MH, :], grow[R_K], ACT.Exp).then_inc(gate_act, 1)
            a(wold[:], wold[:], ACT.Exp).then_inc(gate_act, 1)
            act.wait_ge(zero_filled, 16 * SLOT_BLOCKS)
            for c in range(2):
                N_evacs("mo", c, gate_o, ACT.Sigmoid)

            nc.scalar.preload_act_table_set("natural_log_exp_and_others")
            for c in range(NT):
                act.wait_ge(kn_ready, c + 1)
                if c == 0:
                    act.wait_ge(tile_out, piece_end(PIDX["mo", 1]))
                a(kN[:, c, :], psum[:, 6 + c % 2, :], ACT.Copy).then_inc(kn_done, 1)
            for c in range(NT + 1):
                if c < NT:
                    act.wait_ge(D_masked, c + 1)
                    a(Dm[c % 2], Dm[c % 2], ACT.Exp, scale=-1.0).then_inc(W_done, 1)
                if c:
                    act.wait_ge(num_done, c)
                    for h in range(MH):
                        n = (c - 1) * MH + h
                        if n:
                            act.wait_ge(mss_done, n)
                        a(junk, vaug[:, c - 1, h, 0:DH], ACT.Square, accum_out=mss[:, n:n + 1]).then_inc(mss_done, 1)
            act.wait_ge(ml_fac, 1)
            link(a(mfac[:], mfac[:], ACT.Ln, bias=eps_col[:]))
            a(mfac[:], mfac[:], ACT.Exp, scale=-0.5).then_inc(ml_rs, 1)

            split_hi(PIDX["sq", 0])
            for c in range(2):
                begin_piece(PIDX["sq", c])
                for i in range(4):
                    o = out_of(TIDX["sq", c, i])
                    a(sqT[:, 2 * c + i // NH2, (i % NH2) * BANK:(i % NH2 + 1) * BANK], o, ACT.Copy,
                      scale=QSCALE).then_inc(evac["act"], 1)
            for c in range(2):
                begin_piece(PIDX["sk", c])
            for c in range(2):
                N_evacs("sv", c, svn)
            for c in range(NT):
                act.wait_ge(yn_trans, c + 1)
                a(hS[0][:, 0:MH, c * P:(c + 1) * P], psum[:, 4 + c % 2, :].rearrange("p (h s) -> p h s", h=MH),
                  ACT.Copy).then_inc(ym_hi, 1)

            for k in range(NS + 12):
                if k < NS:
                    lo = steps[k]["lo"]
                    z, l = zs[k % NZ], lt[k % NLT]
                    act.wait_ge(z_ready, k + 1)
                    if k >= NZ:
                        act.wait_ge(ex_done, k - NZ + 1)
                    a(z[:, lo:BANK], psum[:, k % 2, lo:BANK], ACT.Copy).then_inc(zs_done, 1)
                    act.wait_ge(ab_done, k + 1)
                    link(a(l[:, lo:BANK], l[:, lo:BANK], ACT.Exp))
                    a(l[:, lo:BANK], l[:, lo:BANK], ACT.Ln, bias=1.0).then_inc(l1_done, 1)
                i = k - 3
                if 0 <= i < NS:
                    lo = steps[i]["lo"]
                    if steps[i]["diag"]:
                        act.wait_ge(ex_masked, upto_diag(i))
                    act.wait_ge(ex_done, i + 1)
                    a(ex[i % NX][:, lo:BANK], ex[i % NX][:, lo:BANK], ACT.Exp).then_inc(a_done, 1)
                i = k - 5
                if 0 <= i < NS and steps[i]["last"]:
                    gi = steps[i]["g"]
                    act.wait_ge(av_done, i + 1)
                    if gi:
                        act.wait_ge(ossq_ready, gi)
                    a(osq, psum[:, 4 + gi % 2, :], ACT.Square).then_inc(osq_done, 1)
                i = k - 7
                if 0 <= i < NS and steps[i]["last"]:
                    gi = steps[i]["g"]
                    act.wait_ge(ossq_ready, gi + 1)
                    if gi:
                        act.wait_ge(o_made, gi)
                    link(a(ors, psum[:, 6 + gi % 2, :], ACT.Ln, bias=eps_col[:], scale=1.0 / DH))
                    a(ors, ors, ACT.Exp, scale=-0.5).then_inc(ors_done, 1)
                i = k - 8
                if 0 <= i < NS and steps[i]["last"]:
                    s = steps[i]
                    act.wait_ge(o_made, s["g"] + 1)
                    a(hS[0][:, MH + s["h"], s["hf"] * BANK:(s["hf"] + 1) * BANK], of, ACT.Copy).then_inc(o_hi, 1)

            split_hi(PIDX["w_out", 0])
            begin_piece(PIDX["w_out", 0])
            act.wait_ge(mem_in, 16 * MT)
            for i in range(MT):
                rms_squares(i, mems[:, i, :])
            rms_scale(MT)
            norm(NT, MT, mems, mS)
            for c in range(1, 4):
                begin_piece(PIDX["w_out", c])
            act.wait_ge(h_trans, NT + MT)
            for i in range(NT):
                wait_evac(act, TIDX["w_out", 3, i // 2])
                rms_squares(i, x1[:, i, :])
            rms_scale(NT)
            for c in range(4):
                begin_piece(PIDX["w_mk", c])
                o = out_of(TIDX["w_mk", c, 0]).rearrange("p (c m) -> p c m", c=2)
                a(kTm[:, 2 * c:2 * c + 2, :], o, ACT.Copy).then_inc(evac["act"], 1)
            for c in range(4):
                begin_piece(PIDX["w_mv", c])
                o = out_of(TIDX["w_mv", c, 0]).rearrange("p (t n) -> p t n", t=2)
                a(vmem[:, :, c * PC:(c + 1) * PC], o, ACT.Copy).then_inc(evac["act"], 1)
            norm(NT + MT, NT, x1, hS)
            for c in range(4):
                begin_piece(PIDX["w_mq", c])
                for i in range(4):
                    o = out_of(TIDX["w_mq", c, i])
                    a(qT[:, 2 * c + i // NH2, (i % NH2) * BANK:(i % NH2 + 1) * BANK], o,
                      ACT.Copy).then_inc(evac["act"], 1)

            for k in range(NT + 1):
                if k < NT:
                    act.wait_ge(mx_done, k + 1)
                    if k >= 2:
                        act.wait_ge(pt_ready, k - 1)
                    for h in range(XH):
                        a(pnat[:, k % 2, h * MEM:(h + 1) * MEM],
                          psum[:, 4 + 2 * (k % 2) + h // 2, (h % 2) * MEM:(h % 2 + 1) * MEM], ACT.Exp,
                          bias=pmx[:, k, h:h + 1], scale=XSCALE, accum_out=psm[:, k, h:h + 1]).then_inc(p_done, 1)
                if k >= 1:
                    i = k - 1
                    act.wait_ge(pt_ready, i + 1)
                    if i == 0:
                        act.wait_ge(tile_out, piece_end(PIDX["w_mq", 3]))
                    if i == HALF:
                        act.wait_ge(tile_out, TIDX["oT", 0, KD - 1] + 1)
                    for q in range(2):
                        a(pT[:, 4 * q:4 * q + 4, (i % HALF) * P:(i % HALF + 1) * P],
                          psum[:, 4 + 2 * (i % 2) + q, :].rearrange("p (j s) -> p j s", j=4),
                          ACT.Copy).then_inc(pt_done, 1)
                    if i % HALF == HALF - 1:
                        hf = i // HALF
                        for c in range(KD):
                            n = TIDX["oT", 0, hf * KD + c]
                            a(hS[0][:, c, hf * BANK:(hf + 1) * BANK], out_of(n), ACT.Copy).then_inc(oT_hi, 1)
            for c in range(4):
                begin_piece(PIDX["w_mo", c])

            act.wait_ge(wpad_in, 64)
            act.wait_ge(tile_out, TIDX["oT", 0, 2 * KD - 1] + 1)
            a(rpadS[0], rpad, ACT.Copy).then_inc(pad_hi, 1)
            for i in range(NT):
                wait_evac(act, TIDX["w_mo", 3, i // 2])
                rms_squares(i, x1[:, i, :])
            rms_scale(NT)
            act.wait_ge(tile_out, len(tiles))
            norm(2 * NT + MT, NT, x1, hS, hn)
            act.wait_ge(rt_dve, 1)
            a(r4["tmp"], r4["tmp"], ACT.Exp).then_inc(rt_act, 1)
            act.wait_ge(rt_dve, 2)
            a(r1["w2"], r1["w2"], ACT.Exp).then_inc(rt_act, 1)

            act.sem_inc(sg_done, 1)
            act.sem_inc(y_evac, 1)
            act.sem_inc(y_stored, 16)
            act.wait_ge(routed, 1)
            yg_b = xg.rearrange("(b p) d -> b p d", p=P)
            tot = act.value_load(cum_i[0:1, E - 1:E], min_val=1, max_val=MAXB)
            nc.scalar.preload_act_table(ACT.Silu)
            with act.Fori(0, tot) as b:
                act.wait_ge(a_ready, b + 1)
                act.wait_ge(hh_done, b + 1)
                a(sg, psum[:, 0, :], ACT.Silu).then_inc(sg_done, 1)
                act.wait_ge(ht_ready, b + 1)
                a(hhT, psum[:, 6, :].rearrange("p (k s) -> p k s", k=KF), ACT.Copy).then_inc(hhT_done, 1)
                act.wait_ge(y_ready, b + 2)
                act.wait_ge(y_stored, (b + 1) * 16)
                a(yb.rearrange("p (b n) -> p b n", b=2), psum[:, 2:4, :], ACT.Copy).then_inc(y_evac, 1)
                act.wait_ge(y_evac, b + 2)
                act.dma_start(yg_b[bass.ds(b, 1)].rearrange("a p d -> p (a d)"), yb).then_inc(y_stored, 16)
            for i in range(NT):
                act.wait_ge(moe_added, i + 1)
                link(a(otile[i % 2], x1[:, i, :], ACT.Square, accum_out=ss[:, i:i + 1]))
            nc.scalar.preload_act_table_set("natural_log_exp_and_others")
            link(a(lnt[:], ss[:], ACT.Ln, bias=eps_col[:], scale=1.0 / D))
            a(rstd[:], lnt[:], ACT.Exp, scale=-0.5).then_inc(fin_rs, 1)

        @block.vector
        def _(dve):
            chain = [0]
            v = nc.vector

            def link(ins):
                chain[0] += 1
                ins.then_inc(dve_chain, 1)
                dve.wait_ge(dve_chain, chain[0])

            def out_of(n):
                dve.wait_ge(tile_out, n + 1)
                return psum[:, n % RING, :]

            def split_lo(p):
                dve.wait_ge(w_hi, p + 1)
                buffer_free(dve, p)
                dve.wait_ge(raw_in, 16 * (p + 1))
                v.tensor_tensor(wS[p % 2][1], raw, wS[p % 2][0].bitcast(F32), ALU.subtract).then_inc(w_lo, 1)

            def begin_piece(p):
                if p + 1 < NP and p + 1 not in LATE:
                    split_lo(p + 1)

            def norm_parts(j0, n, dst, goff):
                for i in range(n):
                    j = j0 + i
                    dve.wait_ge(h_trans, j + 1)
                    if j:
                        dve.wait_ge(hT_part, 2 * j)
                    for q in range(2):
                        v.tensor_tensor(tt[q].rearrange("p (k s) -> p k s", k=HALF),
                                        psum[:, 4 + 2 * (j % 2) + q, :].rearrange("p (k s) -> p k s", k=HALF),
                                        vecT[:, goff + HALF * q:goff + HALF * (q + 1)].unsqueeze(2).broadcast_to(
                                            [P, HALF, P]), ALU.mult).then_inc(scaled, 1)
                    for q in range(2):
                        sl = (slice(None), slice(HALF * q, HALF * (q + 1)), slice(i * P, (i + 1) * P))
                        dve.wait_ge(hi_part, 2 * j + q + 1)
                        v.tensor_tensor(dst[1][sl], tt[q].rearrange("p (k s) -> p k s", k=HALF),
                                        dst[0][sl].bitcast(F32), ALU.subtract).then_inc(hT_part, 1)

            dve.wait_ge(vec_tr, 1)
            v.tensor_copy(vecT[:], psum[:, 0, 0:NV]).then_inc(vecT_ready, 1)
            dve.wait_ge(vecT_ready, 1)
            split_lo(0)
            dve.wait_ge(pad_hi, 1)
            v.tensor_tensor(wpadS[1], wpad, wpadS[0].bitcast(F32), ALU.subtract).then_inc(pad_lo, 1)
            norm_parts(0, NT, hS, G_MIX)

            dve.wait_ge(h_trans, NT)
            link(v.memset(stack, 0.0))
            for b in range(2):
                link(v.memset(cin[:, b, 0:CW - 1], 0.0))
            for hf in range(NH2):
                o = out_of(TIDX["gates", 0, hf])
                cs = slice(hf * BANK, (hf + 1) * BANK)
                link(v.tensor_scalar(grow[R_G][:, cs], o[0:MH, :], gbias[0:MH, :], None, ALU.add))
                v.tensor_scalar(grow[R_F][:, cs], o[32:32 + MH, :], gbias[32:32 + MH, :], None,
                                ALU.add).then_inc(evac["dve"], 1)
            for ch in range(2 * MH):
                nm, c = ("mq", "mk")[ch // MH], ch % MH
                if c % 2 == 0:
                    begin_piece(PIDX[nm, c // 2])
                wait_evac(dve, TIDX[nm, c // 2, (c % 2) * NH2 + 1])
                o = (mqT if ch < MH else mkT)[:, c, :]
                for tap in range(CW - 1, -1, -1):
                    w = vecT[:, V_CW + tap * 2 * MH + ch:V_CW + tap * 2 * MH + ch + 1]
                    src = cin[:, ch % 2, tap:tap + SEQ]
                    if tap == CW - 1:
                        link(v.tensor_scalar(o, src, w, vecT[:, V_CB + ch:V_CB + ch + 1], ALU.mult, ALU.add))
                    elif tap:
                        link(v.scalar_tensor_tensor(o, src, w, o, ALU.mult, ALU.add))
                    else:
                        v.scalar_tensor_tensor(o, src, w, o, ALU.mult, ALU.add).then_inc(conv_done, 1)
            link(v.memset(vaug[:, :, :, DH:DH + 1], 1.0))

            begin_piece(PIDX["mv", 0])
            chunk = [r.rearrange("p (c s) -> p c s", c=NT) for r in grow]
            mch = chunk[R_M]
            dve.wait_ge(conv_done, 2 * MH)
            wait_evac(dve, TIDX["gates", 0, 1])
            v.scalar_tensor_tensor(grow[R_L], grow[R_F], -1.0, grow[R_F], ALU.mult, ALU.min).then_inc(gate_dve, 1)
            link(v.memset(grow[R_K], 1.0))
            link(v.memset(chunk[R_K][:, :, 0:1], 0.0))
            dve.wait_ge(gate_act, 1)
            link(v.scalar_tensor_tensor(grow[R_L], grow[R_F], 0.0, grow[R_L], ALU.min, ALU.subtract))
            link(v.tensor_tensor_scan(grow[R_F], grow[R_K], grow[R_L], 0.0, ALU.mult, ALU.add))
            link(v.tensor_tensor(grow[R_G], grow[R_G], grow[R_F], ALU.subtract))
            link(v.memset(grow[R_K], 0.0))
            link(v.tensor_copy(chunk[R_K][:, 1:NT, 0:1], chunk[R_F][:, 0:NT - 1, P - 1:P]))
            link(v.tensor_tensor_scan(grow[R_M], grow[R_K], grow[R_G], 0.0, ALU.add, ALU.max))
            link(v.memset(mprev[:], 0.0))
            link(v.tensor_tensor(mprev[:, 1:NT].unsqueeze(2), chunk[R_F][:, 0:NT - 1, P - 1:P],
                                 mch[:, 0:NT - 1, P - 1:P], ALU.add))
            begin_piece(PIDX["mv", 1])
            link(v.tensor_tensor(chunk[R_L], mprev[:].unsqueeze(2).broadcast_to([MH, NT, P]), mch, ALU.subtract))
            link(v.tensor_tensor(grow[R_F], grow[R_F], grow[R_M], ALU.add))
            link(v.tensor_tensor(chunk[R_K], chunk[R_G], mch[:, :, P - 1:P].broadcast_to([MH, NT, P]), ALU.subtract))
            v.tensor_tensor(wold[:].unsqueeze(2), mprev[:].unsqueeze(2), mch[:, :, P - 1:P],
                            ALU.subtract).then_inc(gate_dve, 1)
            dve.wait_ge(gate_dve, 2)
            dve.wait_ge(gate_act, 5)
            v.tensor_scalar(stack[96:96 + MH, :], stack[96:96 + MH, :], QSCALE, None, ALU.mult).then_inc(gate_dve, 1)
            begin_piece(PIDX["mo", 0])
            dve.wait_ge(gate_pe, 1)
            for q in range(2):
                link(v.tensor_copy(cols[:, q * HALF:(q + 1) * HALF, :],
                                   psum[:, 4 + q, 0:HALF * GC].rearrange("p (c g) -> p c g", c=HALF)))
            v.tensor_copy(woldB, psum[:, 6, 0:MH * NT].rearrange("p (h c) -> p h c", h=MH)).then_inc(gate_dve, 1)
            dve.wait_ge(gate_dve, 4)

            def two_banks(b):
                return psum[:, b:b + 2, 0:2 * E1].rearrange("p b (h e) -> p b h e", h=2)

            def pairs(ap):
                return ap.rearrange("p (b h) e -> p b h e", b=2)

            def per_head(col, n):
                return col.rearrange("p (b h) -> p b h", b=2).unsqueeze(3).broadcast_to([P, 2, 2, n])

            def distance(c):
                dve.wait_ge(mb_ready, c + 1)
                if c >= 2:
                    dve.wait_ge(Pm_done, c - 1)
                v.tensor_tensor(Dm[c % 2].rearrange("p (h s) -> p h s", h=MH),
                                psum[:, 0, :].rearrange("p (h s) -> p h s", h=MH),
                                gcol[:, c, :].unsqueeze(2).broadcast_to([P, MH, P]), ALU.subtract).then_inc(D_done, 1)

            def weighted_values(c):
                if c >= 2:
                    dve.wait_ge(U_ready, c - 1)
                v.tensor_tensor(vsb[c % 2], vaug[:, c, :, :], wscol[:, c, :].unsqueeze(2).broadcast_to([P, MH, E1]),
                                ALU.mult).then_inc(vs_done, 1)

            dve.wait_ge(tile_out, piece_end(PIDX["mo", 1]))
            distance(0)
            weighted_values(0)
            for c in range(NT):
                dve.wait_ge(kq_ready, c + 1)
                dve.wait_ge(W_done, c + 1)
                if c >= 2:
                    dve.wait_ge(num_ready, c - 1)
                v.scalar_tensor_tensor(Pm[c % 2], psum[:, 1, :], QSCALE, Dm[c % 2], ALU.mult, ALU.mult).then_inc(Pm_done, 1)
                if c < NT - 1:
                    distance(c + 1)
                    weighted_values(c + 1)
                if c:
                    dve.wait_ge(inter_ready, c)
                    if c > 1:
                        dve.wait_ge(num_done, c)
                    v.tensor_tensor(pairs(inter), two_banks(4), per_head(wicol[:, c, :], E1), ALU.mult).then_inc(inter_done, 1)
                    dve.wait_ge(inter_done, c)
                dve.wait_ge(num_ready, c + 1)
                dve.wait_ge(vs_done, c + 1)
                if c:
                    v.tensor_tensor(pairs(vaug[:, c, :, :]), two_banks(2), pairs(inter), ALU.add).then_inc(num_done, 1)
                else:
                    v.tensor_copy(pairs(vaug[:, c, :, :]), two_banks(2)).then_inc(num_done, 1)
                if c < NT - 1:
                    dve.wait_ge(U_ready, c + 1)
                    if c:
                        dve.wait_ge(CT_done, c)
                        link(v.tensor_tensor(CT[(c + 1) % 2], CT[c % 2],
                                             woldB[:, :, c:c + 1].broadcast_to([P, MH, E1]), ALU.mult))
                        v.tensor_tensor(pairs(CT[(c + 1) % 2]), two_banks(6), pairs(CT[(c + 1) % 2]),
                                        ALU.add).then_inc(CT_done, 1)
                    else:
                        v.tensor_copy(pairs(CT[1]), two_banks(6)).then_inc(CT_done, 1)

            dve.wait_ge(mss_done, NT * MH)
            dve.wait_ge(num_done, NT)
            link(v.tensor_copy(mden[:].unsqueeze(3), vaug[:, :, :, DH:E1]))
            link(v.scalar_tensor_tensor(mfac[:], mden[:], -1.0, mden[:], ALU.mult, ALU.max))
            link(v.tensor_tensor(mden[:], mfac[:], flcol, ALU.max))
            link(v.reciprocal(mden[:], mden[:]))
            ms3 = mss[:].rearrange("p (c h) -> p c h", c=NT)
            link(v.tensor_tensor(mfac[:], mden[:], mden[:], ALU.mult))
            v.scalar_tensor_tensor(mfac[:], mfac[:], 1.0 / DH, ms3, ALU.mult, ALU.mult).then_inc(ml_fac, 1)
            split_lo(PIDX["sq", 0])
            dve.wait_ge(ml_rs, 1)
            link(v.tensor_tensor(mfac[:], mfac[:], mden[:], ALU.mult))
            dve.wait_ge(gate_scaled, NT)
            for c in range(NT):
                link(v.tensor_tensor(vaug[:, c, :, 0:DH], vaug[:, c, :, 0:DH],
                                     mfac[:, c, :].unsqueeze(2).broadcast_to([P, MH, DH]), ALU.mult))
                v.tensor_tensor(gate_o[:, c, :].rearrange("p (h e) -> p h e", h=MH), vaug[:, c, :, 0:DH],
                                gate_o[:, c, :].rearrange("p (h e) -> p h e", h=MH), ALU.mult).then_inc(yn_done, 1)

            for c in range(2):
                begin_piece(PIDX["sq", c])
            for c in range(2):
                begin_piece(PIDX["sk", c])
                for i in range(4):
                    o = out_of(TIDX["sk", c, i])
                    v.tensor_copy(skT[:, 2 * c + i // NH2, (i % NH2) * BANK:(i % NH2 + 1) * BANK],
                                  o).then_inc(evac["dve"], 1)
            for c in range(2):
                begin_piece(PIDX["sv", c])
            for c in range(NT):
                dve.wait_ge(ym_hi, c + 1)
                sl = (slice(None), slice(0, MH), slice(c * P, (c + 1) * P))
                v.tensor_tensor(hS[1][sl], psum[:, 4 + c % 2, :].rearrange("p (h s) -> p h s", h=MH),
                                hS[0][sl].bitcast(F32), ALU.subtract).then_inc(ym_done, 1)

            for k in range(NS + 12):
                if k < NS:
                    lo = steps[k]["lo"]
                    z = zs[k % NZ][:, lo:BANK]
                    dve.wait_ge(zs_done, k + 1)
                    if k >= NLT:
                        dve.wait_ge(L_done, k - NLT + 1)
                    v.scalar_tensor_tensor(lt[k % NLT][:, lo:BANK], z, -1.0, z, ALU.mult, ALU.min).then_inc(ab_done, 1)
                i = k - 1
                if 0 <= i < NS:
                    lo = steps[i]["lo"]
                    dve.wait_ge(l1_done, i + 1)
                    if i >= NL:
                        dve.wait_ge(tail_ready, i - NL + 1)
                        if upto_R(i - NL):
                            dve.wait_ge(R_done, upto_R(i - NL))
                    v.scalar_tensor_tensor(Lb[i % NL][:, lo:BANK], zs[i % NZ][:, lo:BANK], 0.0,
                                           lt[i % NLT][:, lo:BANK], ALU.max, ALU.add).then_inc(L_done, 1)
                i = k - 2
                if 0 <= i < NS:
                    lo = steps[i]["lo"]
                    dve.wait_ge(tail_ready, i + 1)
                    if i >= NX:
                        dve.wait_ge(av_done, i - NX + 1)
                    v.tensor_tensor(ex[i % NX][:, lo:BANK], zs[i % NZ][:, lo:BANK], psum[:, 2 + i % 2, lo:BANK],
                                    ALU.subtract).then_inc(ex_done, 1)
                i = k - 7
                if 0 <= i < NS and steps[i]["last"]:
                    s = steps[i]
                    dve.wait_ge(ors_done, s["g"] + 1)
                    if s["g"]:
                        dve.wait_ge(sb_out, s["g"])
                    v.scalar_tensor_tensor(of, psum[:, 4 + s["g"] % 2, :], vecT[:, V_SBG + s["h"]:V_SBG + s["h"] + 1],
                                           ors, ALU.mult, ALU.mult).then_inc(o_made, 1)
                i = k - 8
                if 0 <= i < NS and steps[i]["last"]:
                    s = steps[i]
                    dve.wait_ge(o_hi, s["g"] + 1)
                    sl = (slice(None), MH + s["h"], slice(s["hf"] * BANK, (s["hf"] + 1) * BANK))
                    v.tensor_tensor(hS[1][sl], of, hS[0][sl].bitcast(F32), ALU.subtract).then_inc(sb_out, 1)

            def add_residual(nm, c):
                begin_piece(PIDX[nm, c])
                for i in range(NT // 2):
                    o = out_of(TIDX[nm, c, i]).rearrange("p (t n) -> p t n", t=2)
                    xt = x1[:, 2 * i:2 * i + 2, c * PC:(c + 1) * PC]
                    v.tensor_tensor(xt, xt, o, ALU.add).then_inc(evac["dve"], 1)

            split_lo(PIDX["w_out", 0])
            for i in range(NT):
                dve.wait_ge(x_in[i], 32)
            add_residual("w_out", 0)
            norm_parts(NT, MT, mS, G_KV)
            for c in range(1, 4):
                add_residual("w_out", c)
            for nm in ("w_mk", "w_mv"):
                for c in range(4):
                    begin_piece(PIDX[nm, c])
            dve.wait_ge(tile_out, piece_end(PIDX["w_out", 3]))
            norm_parts(NT + MT, NT, hS, G_MEM)
            for c in range(4):
                begin_piece(PIDX["w_mq", c])
            for k in range(NT + 1):
                if k < NT:
                    dve.wait_ge(sc_ready, k + 1)
                    link(v.tensor_reduce(pmx[:, k, :], psum[:, 4 + 2 * (k % 2):6 + 2 * (k % 2), :].rearrange(
                        "p b (h m) -> p (b h) m", h=2), AX.X, ALU.max))
                    v.tensor_scalar(pmx[:, k, :], pmx[:, k, :], -XSCALE, None, ALU.mult).then_inc(mx_done, 1)
                    dve.wait_ge(p_done, XH * (k + 1))
                    link(v.reciprocal(psm[:, k, :], psm[:, k, :]))
                    pk = pnat[:, k % 2, :].rearrange("p (h m) -> p h m", h=XH)
                    v.tensor_tensor(pk, pk, psm[:, k, :].unsqueeze(2).broadcast_to([P, XH, MEM]),
                                    ALU.mult).then_inc(pn_done, 1)
                if k >= 1 and (k - 1) % HALF == HALF - 1:
                    hf = (k - 1) // HALF
                    for c in range(KD):
                        n = TIDX["oT", 0, hf * KD + c]
                        sl = (slice(None), c, slice(hf * BANK, (hf + 1) * BANK))
                        dve.wait_ge(oT_hi, hf * KD + c + 1)
                        v.tensor_tensor(hS[1][sl], out_of(n), hS[0][sl].bitcast(F32),
                                        ALU.subtract).then_inc(evac["dve"], 1)
            for c in range(4):
                add_residual("w_mo", c)
            dve.wait_ge(pad_hi, 2)
            v.tensor_tensor(rpadS[1], rpad, rpadS[0].bitcast(F32), ALU.subtract).then_inc(pad_lo, 1)
            dve.wait_ge(pad_lo, 2)
            norm_parts(2 * NT + MT, NT, hS, G_FFN)
            for hf in range(NH2):
                dve.wait_ge(rt_pe, hf + 1)
                v.tensor_scalar(lgT[:, hf * BANK:(hf + 1) * BANK], psum[0:NR, hf, :], rbias[:], None,
                                ALU.add).then_inc(lgT_done, 1)
            dve.wait_ge(rt_pe, NH2 + 1)
            link(v.tensor_copy(lg, psum[:, 2, 0:NT * NR].rearrange("p (t r) -> p t r", t=NT)))

            def over4(col):
                return col.unsqueeze(2).broadcast_to([P, NT, 4])

            def first_max(dst, src, mx):
                link(v.tensor_reduce(mx, src, AX.X, ALU.max))
                link(v.tensor_tensor(r4["eq"], src, over4(mx), ALU.is_equal))
                link(v.memset(r1["left"], 1.0))
                for j in range(4):
                    link(v.tensor_tensor(dst[:, :, j], r4["eq"][:, :, j], r1["left"], ALU.mult))
                    if j < 3:
                        link(v.tensor_tensor(r1["left"], r1["left"], dst[:, :, j], ALU.subtract))

            oh, t1, t2, es = (r4[n] for n in ("oh", "t1", "t2", "es"))
            first_max(oh, lg[:, :, 0:NG], r1["mx"])
            v.tensor_tensor(r4["tmp"], lg[:, :, 0:NG], over4(r1["mx"]), ALU.subtract).then_inc(rt_dve, 1)
            M = re["M"]
            link(v.tensor_tensor(M, elt, oh.unsqueeze(3).broadcast_to([P, NT, NG, NE]), ALU.mult))
            link(v.tensor_reduce(es, M.rearrange("p t g e -> p t e g"), AX.X, ALU.add))
            first_max(t1, es, r1["m1"])
            link(v.scalar_tensor_tensor(es, t1, NEG, es, ALU.mult, ALU.add))
            first_max(t2, es, r1["m2"])
            v.tensor_tensor(r1["w2"], r1["m2"], r1["m1"], ALU.subtract).then_inc(rt_dve, 1)
            g4 = [P, NT, NG, NE]
            link(v.tensor_tensor(re["A1"], oh.unsqueeze(3).broadcast_to(g4), t1.unsqueeze(2).broadcast_to(g4), ALU.mult))
            link(v.tensor_tensor(re["A2"], oh.unsqueeze(3).broadcast_to(g4), t2.unsqueeze(2).broadcast_to(g4), ALU.mult))
            v.tensor_tensor(M, re["A1"], re["A2"], ALU.add).then_inc(rt_dve, 1)
            dve.wait_ge(rt_act, 2)
            link(v.tensor_reduce(r1["psel"], r4["tmp"], AX.X, ALU.add))
            link(v.tensor_scalar(r1["w1"], r1["w2"], 1.0, None, ALU.add))
            link(v.tensor_tensor(r1["w1"], r1["w1"], r1["psel"], ALU.mult))
            link(v.reciprocal(r1["w1"], r1["w1"]))
            link(v.tensor_tensor(r1["w2"], r1["w2"], r1["w1"], ALU.mult))
            dve.wait_ge(rt_pe, NH2 + 2)
            flat = [n.rearrange("p t g e -> p t (g e)") for n in (re["tot"], re["pos"])]
            link(v.tensor_copy(flat[0], psum[:, 1, NT * E:2 * NT * E].rearrange("p (t e) -> p t e", t=NT)))
            link(v.tensor_copy(flat[1], psum[:, 1, 0:NT * E].rearrange("p (t e) -> p t e", t=NT)))
            cnt, nb, cum, one, base = (rc[n] for n in ("cnt", "nb", "cum", "one", "base"))
            link(v.tensor_copy(cnt, flat[0][:, 0, :]))
            for i in range(1, NT):
                link(v.tensor_tensor(flat[1][:, i, :], flat[1][:, i, :], cnt, ALU.add))
                link(v.tensor_tensor(cnt, cnt, flat[0][:, i, :], ALU.add))
            link(v.memset(nb, 0.0))
            link(v.memset(one, 1.0))
            for b in range(NT):
                link(v.scalar_tensor_tensor(nb, cnt, float(b * P), nb, ALU.is_gt, ALU.add))
            link(v.tensor_tensor_scan(cum, one, nb, 0.0, ALU.mult, ALU.add))
            link(v.tensor_tensor(base, cum, nb, ALU.subtract))
            link(v.tensor_scalar(base, base, float(P), None, ALU.mult))
            link(v.tensor_tensor(flat[1], flat[1], base.unsqueeze(1).broadcast_to([P, NT, E]), ALU.add))
            for c, A in enumerate((re["A1"], re["A2"])):
                link(v.tensor_tensor(M, A, re["pos"], ALU.mult))
                link(v.tensor_reduce(r1["pos"], M, AX.XY, ALU.add))
                link(v.tensor_copy(idx[:, c, :], r1["pos"]))
            link(v.tensor_copy(nb_i[:], nb[0:1, :]))
            v.tensor_copy(cum_i[:], cum[0:1, :]).then_inc(routed, 1)

            dve.wait_ge(routed, 1)
            dve.sem_inc(hh_done, 1)

            def xT_evac():
                for q in range(2):
                    ins = v.tensor_tensor(xTb[:, HALF * q:HALF * (q + 1), :],
                                          psum[:, 4 + q, :].rearrange("p (k s) -> p k s", k=HALF),
                                          vecT[:, G_FFN + HALF * q:G_FFN + HALF * (q + 1)].unsqueeze(2).broadcast_to(
                                              [P, HALF, P]), ALU.mult)
                ins.then_inc(xT_done, 1)

            dve.wait_ge(xt_ready, 1)
            xT_evac()
            tot = dve.value_load(cum_i[0:1, E - 1:E], min_val=1, max_val=MAXB)
            with dve.Fori(0, tot) as b:
                dve.wait_ge(u_ready, b + 1)
                dve.wait_ge(sg_done, b + 2)
                v.tensor_tensor(hh, sg, psum[:, 1, :], ALU.mult).then_inc(hh_done, 1)
                dve.wait_ge(xt_ready, b + 2)
                xT_evac()
            for i in range(NT):
                dve.wait_ge(yg_in[i], 32)
                link(v.scalar_tensor_tensor(x1[:, i, :], yg_t[i][0], r1["w1"][:, i:i + 1], x1[:, i, :], ALU.mult, ALU.add))
                v.scalar_tensor_tensor(x1[:, i, :], yg_t[i][1], r1["w2"][:, i:i + 1], x1[:, i, :], ALU.mult,
                                       ALU.add).then_inc(moe_added, 1)
            dve.wait_ge(fin_rs, 1)
            dve.wait_ge(gfin_in, 16)
            for i in range(NT):
                if i >= 2:
                    dve.wait_ge(out_stored[i % 2], 16 * (i // 2))
                v.scalar_tensor_tensor(otile[i % 2], x1[:, i, :], rstd[:, i:i + 1], gfin, ALU.mult,
                                       ALU.mult).then_inc(out_made, 1)

        @block.tensor
        def _(pe):
            te = nc.tensor
            pe.wait_ge(vec_in, VEC_DMAS * 16)
            pe.wait_ge(const_made, 6)
            te.transpose(psum[:, 0, 0:NV], vec_rows[:], ident[0:NV, 0:NV]).then_inc(vec_tr, 1)

            def norm_transposes(j, src):
                pe.wait_ge(h_made, j + 1)
                if j >= 2:
                    pe.wait_ge(scaled, 2 * (j - 1))
                for k in range(KD):
                    last = te.transpose(psum[:, 4 + 2 * (j % 2) + k // HALF, (k % HALF) * P:(k % HALF + 1) * P],
                                        src[:, k * P:(k + 1) * P], ident[:])
                last.then_inc(h_trans, 1)

            def open_tile(n):
                if n >= RING:
                    wait_evac(pe, n - RING)
                return psum[:, n % RING, :]

            def product(o, lhs, rhs, n):
                for k in range(n):
                    te.matmul(o, lhs(0, k), rhs(0, k), start=(k == 0), stop=False)
                    te.matmul(o, lhs(0, k), rhs(1, k), start=False, stop=False)
                    last = te.matmul(o, lhs(1, k), rhs(0, k), start=False, stop=(k == n - 1))
                return last

            def T_piece(nm, c, xS, cols=BANK):
                p = PIDX[nm, c]
                w = wS[p % 2]
                pe.wait_ge(w_lo, p + 1)
                per = xS[0].shape[2] // cols
                in_bank = BANK // cols
                for i in range(2 * per // in_bank):
                    n = TIDX[nm, c, i]
                    o = open_tile(n)
                    for q in range(in_bank):
                        ch, part = (i * in_bank + q) // per, (i * in_bank + q) % per
                        last = product(o[:, q * cols:(q + 1) * cols],
                                       lambda z, k: w[z][:, k, ch * P:(ch + 1) * P],
                                       lambda z, k: xS[z][:, k, part * cols:(part + 1) * cols], KD)
                    last.then_inc(tile_out, 1)

            def N_piece(nm, c, xS):
                p = PIDX[nm, c]
                w = wS[p % 2]
                pe.wait_ge(w_lo, p + 1)
                for i in range(xS[0].shape[2] // (2 * P)):
                    n = TIDX[nm, c, i]
                    o = open_tile(n)
                    for q in range(2):
                        tk = 2 * i + q
                        last = product(o[:, q * PC:(q + 1) * PC], lambda z, k: xS[z][:, k, tk * P:(tk + 1) * P],
                                       lambda z, k: w[z][:, k, :], KD)
                    last.then_inc(tile_out, 1)

            for i in range(NT):
                norm_transposes(i, htmp[:, i % 2, :])
            pe.wait_ge(hT_part, 2 * NT)
            pe.wait_ge(vecT_ready, 1)
            pe.wait_ge(pad_lo, 1)
            for hf in range(NH2):
                o = open_tile(TIDX["gates", 0, hf])
                product(o[0:GW, :], lambda z, k: wpadS[z][:, k, :],
                        lambda z, k: hS[z][:, k, hf * BANK:(hf + 1) * BANK], KD).then_inc(tile_out, 1)
            for nm in ("mq", "mk"):
                for c in range(2):
                    T_piece(nm, c, hS)
            for c in range(2):
                N_piece("mv", c, hS)
            N_piece("mo", 0, hS)
            pe.wait_ge(gate_dve, 3)
            pe.wait_ge(gate_act, 5)
            for c in range(NT):
                te.transpose(psum[:, 4 + c // HALF, (c % HALF) * GC:(c % HALF + 1) * GC],
                             stack[0:GC, c * P:(c + 1) * P], ident[0:GC, 0:GC])
            for h in range(MH):
                last = te.matmul(psum[:, 6, h * NT:(h + 1) * NT], sel[:, h, :], wold[:], start=True, stop=True)
            last.then_inc(gate_pe, 1)
            N_piece("mo", 1, hS)

            wait_evac(pe, TIDX["mo", 1, NT // 2 - 1])
            pe.wait_ge(gate_dve, 4)
            pe.wait_ge(silu_done, 2 * MH)
            for c in range(NT):
                if c >= 2:
                    pe.wait_ge(kn_done, c - 1)
                for h in range(MH):
                    last = te.transpose(psum[:, 6 + c % 2, h * P:(h + 1) * P], mkT[:, h, c * P:(c + 1) * P], ident[:])
                last.then_inc(kn_ready, 1)

            def at_head(b, h):
                return psum[:, b + h // 2, (h % 2) * E1:(h % 2 + 1) * E1]

            def max_rows(c):
                if c:
                    pe.wait_ge(D_done, c)
                for h in range(MH):
                    last = te.matmul(psum[:, 0, h * P:(h + 1) * P], sel[:, h, :], mrow[:, c * P:(c + 1) * P],
                                     start=True, stop=True)
                last.then_inc(mb_ready, 1)

            def scores(c):
                if c:
                    pe.wait_ge(Pm_done, c)
                for h in range(MH):
                    last = te.matmul(psum[:, 1, h * P:(h + 1) * P], mkT[:, h, c * P:(c + 1) * P],
                                     mqT[:, h, c * P:(c + 1) * P], start=True, stop=True)
                last.then_inc(kq_ready, 1)

            max_rows(0)
            scores(0)
            pe.wait_ge(kn_done, NT)
            for c in range(NT):
                cs = slice(c * P, (c + 1) * P)
                if c < NT - 1:
                    pe.wait_ge(vs_done, c + 1)
                    if c:
                        pe.wait_ge(CT_done, c)
                    for h in range(MH):
                        last = te.matmul(at_head(6, h), kN[:, c, h * P:(h + 1) * P], vsb[c % 2][:, h, :],
                                         start=True, stop=True)
                    last.then_inc(U_ready, 1)
                    max_rows(c + 1)
                if c:
                    pe.wait_ge(CT_done, c)
                    pe.wait_ge(num_done, c)
                    for h in range(MH):
                        last = te.matmul(at_head(4, h), mqT[:, h, cs], CT[c % 2][:, h, :], start=True, stop=True)
                    last.then_inc(inter_ready, 1)
                pe.wait_ge(Pm_done, c + 1)
                if c:
                    pe.wait_ge(num_done, c)
                for h in range(MH):
                    last = te.matmul(at_head(2, h), Pm[c % 2][:, h * P:(h + 1) * P], vaug[:, c, h, :],
                                     start=True, stop=True)
                last.then_inc(num_ready, 1)
                if c < NT - 1:
                    scores(c + 1)

            for c in range(2):
                T_piece("sq", c, hS)
            for c in range(2):
                T_piece("sk", c, hS)
            for c in range(2):
                N_piece("sv", c, hS)
            for c in range(NT):
                pe.wait_ge(yn_done, c + 1)
                if c >= 2:
                    pe.wait_ge(ym_done, c - 1)
                for h in range(MH):
                    last = te.transpose(psum[:, 4 + c % 2, h * P:(h + 1) * P], gate_o[:, c, h * P:(h + 1) * P], ident[:])
                last.then_inc(yn_trans, 1)

            for i in range(4):
                wait_evac(pe, TIDX["sv", 1, i])
            wait_evac(pe, TIDX["sk", 1, 3])
            pe.wait_ge(ym_done, NT)
            for k in range(NS + 12):
                if k < NS:
                    s = steps[k]
                    lo = s["lo"]
                    if k >= 2:
                        pe.wait_ge(zs_done, k - 1)
                    te.matmul(psum[:, k % 2, lo:BANK], skT[:, s["h"], s["j"] * P:(s["j"] + 1) * P],
                              sqT[:, s["h"], s["hf"] * BANK + lo:(s["hf"] + 1) * BANK],
                              start=True, stop=True).then_inc(z_ready, 1)
                i = k - 2
                if 0 <= i < NS:
                    s = steps[i]
                    lo = s["lo"]
                    if s["diag"]:
                        pe.wait_ge(Lmasked, upto_diag(i))
                    pe.wait_ge(L_done, i + 1)
                    if i >= 2:
                        pe.wait_ge(ex_done, i - 1)
                    if not s["first"]:
                        pe.wait_ge(R_done, upto_R(i - 1))
                        te.matmul(psum[:, 2 + i % 2, lo:BANK], ones[:], Rb[i % NRB][:, lo:BANK], start=True, stop=False)
                    te.matmul(psum[:, 2 + i % 2, lo:BANK], uincl[:], Lb[i % NL][:, lo:BANK],
                              start=s["first"], stop=True).then_inc(tail_ready, 1)
                i = k - 4
                if 0 <= i < NS:
                    s = steps[i]
                    lo = s["lo"]
                    if s["first"] and s["g"] >= 2:
                        pe.wait_ge(o_made, s["g"] - 1)
                    pe.wait_ge(a_done, i + 1)
                    te.matmul(psum[:, 4 + s["g"] % 2, lo:BANK], svn[:, s["j"], s["h"] * DH:(s["h"] + 1) * DH],
                              ex[i % NX][:, lo:BANK], start=s["first"], stop=s["last"],
                              skip_group_check=True).then_inc(av_done, 1)
                i = k - 6
                if 0 <= i < NS and steps[i]["last"]:
                    gi = steps[i]["g"]
                    pe.wait_ge(osq_done, gi + 1)
                    if gi >= 2:
                        pe.wait_ge(ors_done, gi - 1)
                    te.matmul(psum[:, 6 + gi % 2, :], ones[:], osq, start=True, stop=True).then_inc(ossq_ready, 1)

            pe.wait_ge(sb_out, NGRP)
            N_piece("w_out", 0, hS)
            for i in range(MT):
                norm_transposes(NT + i, htmp[:, (NT + i) % 2, :])
            for c in range(1, 4):
                N_piece("w_out", c, hS)
            pe.wait_ge(hT_part, 2 * (NT + MT))
            for c in range(4):
                T_piece("w_mk", c, mS, MEM)
            for c in range(4):
                N_piece("w_mv", c, mS)
            for i in range(NT):
                norm_transposes(NT + MT + i, htmp[:, (NT + MT + i) % 2, :])
            pe.wait_ge(hT_part, 2 * (2 * NT + MT))
            for c in range(4):
                T_piece("w_mq", c, hS)

            wait_evac(pe, TIDX["w_mq", 3, 3])
            JH = XD // P
            for k in range(NT + 1):
                if k < NT:
                    if k >= 2:
                        pe.wait_ge(pt_done, 2 * (k - 1))
                    for h in range(XH):
                        for j in range(JH):
                            last = te.matmul(psum[:, 4 + 2 * (k % 2) + h // 2, (h % 2) * MEM:(h % 2 + 1) * MEM],
                                             qT[:, JH * h + j, k * P:(k + 1) * P], kTm[:, JH * h + j, :],
                                             start=(j == 0), stop=(j == JH - 1))
                    last.then_inc(sc_ready, 1)
                if k >= 1:
                    i = k - 1
                    pe.wait_ge(pn_done, i + 1)
                    for q in range(2 * XH):
                        last = te.transpose(psum[:, 4 + 2 * (i % 2) + q // 4, (q % 4) * P:(q % 4 + 1) * P],
                                            pnat[:, i % 2, q * P:(q + 1) * P], ident[:])
                    last.then_inc(pt_ready, 1)
                    if i % HALF == HALF - 1:
                        hf = i // HALF
                        pe.wait_ge(pt_done, 2 * (i + 1))
                        for c in range(KD):
                            n = TIDX["oT", 0, hf * KD + c]
                            o = open_tile(n)
                            for m in range(MT):
                                last = te.matmul(o, vmem[:, m, c * P:(c + 1) * P], pT[:, MT * (c // JH) + m, :],
                                                 start=(m == 0), stop=(m == MT - 1))
                            last.then_inc(tile_out, 1)
            wait_evac(pe, TIDX["oT", 0, 2 * KD - 1])
            for c in range(4):
                N_piece("w_mo", c, hS)

            pe.wait_ge(pad_lo, 2)
            for i in range(NT):
                norm_transposes(2 * NT + MT + i, hn[:, i, :])
            wait_evac(pe, len(tiles) - 1)
            pe.wait_ge(hT_part, 2 * (3 * NT + MT))
            for hf in range(NH2):
                product(psum[0:100, hf, :], lambda z, k: rpadS[z][:, k, :],
                        lambda z, k: hS[z][:, k, hf * BANK:(hf + 1) * BANK], KD).then_inc(rt_pe, 1)
            for i in range(NT):
                pe.wait_ge(lgT_done, i // HALF + 1)
                last = te.transpose(psum[:, 2, i * NR:(i + 1) * NR], lgT[:, i * P:(i + 1) * P], ident[0:NR, 0:NR])
            last.then_inc(rt_pe, 1)
            pe.wait_ge(rt_dve, 3)
            Mf = re["M"].rearrange("p t g e -> p (t g e)")
            te.matmul(psum[:, 1, 0:NT * E], ustrict[:], Mf, start=True, stop=True)
            te.matmul(psum[:, 1, NT * E:2 * NT * E], ones[:], Mf, start=True, stop=True).then_inc(rt_pe, 1)
            pe.wait_ge(routed, 1)

            def x_transposes():
                for k in range(KD):
                    last = te.transpose(psum[:, 4 + k // HALF, (k % HALF) * P:(k % HALF + 1) * P],
                                        xb[:, k * P:(k + 1) * P], ident[:])
                last.then_inc(xt_ready, 1)

            pe.sem_inc(y_ready, 1)
            pe.wait_ge(xb_in, 16)
            x_transposes()
            blk = pe.alloc_register("pe_block")
            pe.reg_mov(blk, 0)
            with pe.Fori(0, E // 2) as i:
                for par in range(2):
                    pe.wait_ge(moe_in[par], (i + 1) * 48)
                    n_blocks = pe.value_load(nb_i[0:1, bass.ds(i * 2 + par, 1)], min_val=0, max_val=NT)
                    with pe.Fori(0, n_blocks) as _j:
                        b = pe.snap(blk, min_val=0, max_val=MAXB)
                        pe.wait_ge(xT_done, b + 1)
                        pe.wait_ge(sg_done, b + 1)
                        for k in range(KD):
                            last = te.matmul(psum[:, 0, :], xTb[:, k, :], w1s[par][:, k, :], start=(k == 0), stop=(k == KD - 1))
                        last.then_inc(a_ready, 1)
                        pe.wait_ge(hh_done, b + 1)
                        for k in range(KD):
                            last = te.matmul(psum[:, 1, :], xTb[:, k, :], w3s[par][:, k, :], start=(k == 0), stop=(k == KD - 1))
                        last.then_inc(u_ready, 1)
                        pe.wait_ge(xb_in, (b + 2) * 16)
                        x_transposes()
                        pe.wait_ge(hh_done, b + 2)
                        for k in range(KF):
                            last = te.transpose(psum[:, 6, k * P:(k + 1) * P], hh[:, k * P:(k + 1) * P], ident[:])
                        last.then_inc(ht_ready, 1)
                        pe.wait_ge(hhT_done, b + 1)
                        pe.wait_ge(y_evac, b + 1)
                        for c in range(2):
                            for k in range(KF):
                                last = te.matmul(psum[:, 2 + c, :], hhT[:, k, :], w2s[par][:, k, c * BANK:(c + 1) * BANK],
                                                 start=(k == 0), stop=(k == KF - 1))
                        last.then_inc(y_ready, 1)
                        pe.reg_add(blk, blk, 1)



def kernel(**inputs):
    import numpy as np
    import concourse.bacc as bacc
    from concourse.bass_utils import run_bass_kernel_spmd as run

    nc = bacc.Bacc("TRN2", target_bir_lowering=False, num_devices=1)
    arrays, t = {}, {}
    for name in sorted(inputs):
        arrays["in_" + name] = np.ascontiguousarray(inputs[name])
        t[name] = nc.dram_tensor("in_" + name, arrays["in_" + name].shape, F32, kind="ExternalInput").ap()
    shape = tuple(inputs["x"].shape)
    out = nc.dram_tensor("out", shape, F32, kind="ExternalOutput").ap()
    experts = inputs["w_e1"].shape[1] * inputs["w_e1"].shape[2]
    rows = ((2 * shape[1] + experts * (P - 1)) // P + 2) * P
    xg = nc.dram_tensor("token_blocks", (rows, shape[2]), F32).ap()
    hybrid_layer(nc, t, out, xg)
    return run(nc, [arrays], core_ids=[0]).results[0]["out"]
```

```python
from contextlib import ExitStack

import concourse.bass as bass
from concourse import mybir

ALU = mybir.AluOpType
ACT = mybir.ActivationFunctionType
AX = mybir.AxisListType
F32 = mybir.dt.float32
F32R = mybir.dt.float32r
I32 = mybir.dt.int32

P = 128
BANK = 512
EPS = 1e-6
NEG = -1.0e30
DUMP = []


def hybrid_layer(nc, t, out, xg, dbg=None):
    SEQ, D = t["x"].shape[1:]
    MEM = t["mem"].shape[1]
    NT = SEQ // P
    KD = D // P
    MT = MEM // P
    MH = t["i_bias"].shape[1]
    DH = P
    MW = MH * DH
    CW = t["conv_w"].shape[1]
    XH = 4
    XD = D // XH
    NG = t["w_e1"].shape[1]
    NE = t["w_e1"].shape[2]
    E = NG * NE
    F = t["w_e1"].shape[4]
    KF = F // P
    HALF = BANK // P
    NH2 = SEQ // BANK
    QSCALE = float(DH) ** -0.5
    XSCALE = float(XD) ** -0.5
    NR = NG + E
    MAXB = (2 * SEQ + E * (P - 1)) // P
    SLOT_BLOCKS = MAXB + 2
    assert MW == BANK and F == BANK and D == 2 * BANK and MH == 4

    x_d = t["x"][0].rearrange("(t p) d -> t p d", p=P)
    mem_d = t["mem"][0].rearrange("(t p) d -> t p d", p=P)
    x1_d = nc.dram_tensor("x1_rows", (SEQ, D), F32).ap().rearrange("(t p) d -> t p d", p=P)
    out_d = out[0].rearrange("(t p) d -> t p d", p=P)

    PC = BANK // 2
    W_IN = t["w_in"][0]
    OFF = dict(mq=0, mk=MW, mv=2 * MW, mo=3 * MW, gates=4 * MW, sq=4 * MW + 2 * MH,
               sk=5 * MW + 2 * MH, sv=6 * MW + 2 * MH)

    def piece_d(name, c0):
        return t[name][0][:, c0:c0 + PC].rearrange("(k p) n -> p k n", p=P)

    pieces = []
    for nm, who in (("mq", "act"), ("mk", "act"), ("mv", "act"), ("mo", "act"), ("sq", "act"),
                    ("sk", "dve"), ("sv", "act")):
        for c in range(2):
            pieces.append((nm, c, piece_d("w_in", OFF[nm] + c * PC), 4, who))
    for nm, n, who in (("w_out", 4, "dve"), ("w_mk", 1, "act"), ("w_mv", 1, "act"), ("w_mq", 4, "act"),
                       ("w_mo", 4, "dve")):
        for c in range(4):
            pieces.append((nm, c, piece_d(nm, c * PC), n, who))
    PIDX = {(x[0], x[1]): i for i, x in enumerate(pieces)}
    NP = len(pieces)

    tiles = [("gates", 0, i, "dve") for i in range(NH2)]
    for nm, c, _, n, who in pieces:
        if (nm, c) == ("w_mo", 0):
            tiles += [("oT", 0, i, "dve") for i in range(2 * KD)]
        tiles += [(nm, c, i, who) for i in range(n)]
    TIDX = {(n, c, i): k for k, (n, c, i, _) in enumerate(tiles)}
    evac_no = []
    seen = {"act": 0, "dve": 0}
    for *_, w in tiles:
        seen[w] += 1
        evac_no.append((w, seen[w]))
    RING = 4

    def piece_end(p):
        nm, c, _, n, _ = pieces[p]
        return TIDX[nm, c, n - 1] + 1

    with ExitStack() as ctx:
        def sb(name, shape, dt=F32):
            return ctx.enter_context(nc.sbuf_tensor(name, shape, dt))

        def sem(name):
            return ctx.enter_context(nc.semaphore(name))

        KB = 256
        fence_base = nc.sbuf_base
        sb("fence", [P, 178 * KB + 128])
        base = -(-fence_base // 32) * 32

        def region(name, at, words, dt=F32):
            return nc.alloc_sbuf_tensor_at(name, [P, words], dt, offset=base + 4 * at)

        RS = 64 * KB
        arena = region("arena", 0, 178 * KB + 128)
        act_split = region("act_split", 0, 64 * KB, F32R)
        RW = RS + 74 * KB + 128
        w_split = region("w_split", RW, 32 * KB, F32R)
        raws = [arena[:, at:at + 8 * KB].rearrange("p (k n) -> p k n", k=KD) for at in (RW + 32 * KB, RS + 56 * KB)]
        raw_no = [int(p % 2 == 1 and PIDX["w_mk", 0] <= p <= PIDX["w_mq", 1]) for p in range(NP)]

        def hi_lo(tensor, at, a, b):
            return [tensor[:, at + i * a * b:at + (i + 1) * a * b].rearrange("p (a b) -> p a b", a=a) for i in range(2)]

        def view(at, *shape):
            n = 1
            for q in shape:
                n *= q
            v = arena[:, at:at + n]
            if len(shape) == 2:
                v = v.rearrange("p (a b) -> p a b", a=shape[0])
            return v

        hS = hi_lo(act_split, 0, KD, SEQ)
        wS = [hi_lo(w_split, i * 16 * KB, KD, PC) for i in range(2)]
        RP = RS
        mqT = view(RP, MH, SEQ)
        mkT = view(RP + 16 * KB, MH, SEQ)
        vaug = arena[:, RP + 32 * KB:RP + 32 * KB + NT * MH * 129].rearrange(
            "p (t h e) -> p t h e", t=NT, h=MH)
        gate_o = view(RP + 49 * KB, NT, MW)
        sqT = view(RP, MH, SEQ)
        skT = view(RP + 16 * KB, MH, SEQ)
        svn = view(RP + 32 * KB, NT, MW)
        kN = view(RW + 16 * KB, NT, MW)
        xs = view(RP, NT, D)
        x1 = view(RP, NT, D)
        qT = view(RP + 32 * KB, KD, SEQ)
        kTm = view(RP + 64 * KB, KD, MEM)
        mS = hi_lo(region("mem_split", RP + 32 * KB, 16 * KB, F32R), 0, KD, MEM)
        mems = view(RP + 48 * KB, MT, D)
        pT = view(RW + 16 * KB, 2 * XH, BANK)

        consts = {n: sb(n, [P, P]) for n in ("ident", "uincl", "ustrict", "ones")}
        ident, uincl, ustrict, ones = (consts[n] for n in ("ident", "uincl", "ustrict", "ones"))
        sel = sb("sel", [MH, MH, P])
        NV = 4 * KD + CW * 2 * MH + 2 * MH + MH
        vec_rows = sb("vec_rows", [NV, P])
        vecT = sb("vecT", [P, NV])
        GW = 3 * 32 + MH
        gbias = sb("gbias", [GW, 1])
        rbias = sb("rbias", [NR, 1])
        mlg = sb("mlg", [P, MW])
        wpad = view(RW + 16 * KB, KD, GW)
        wpadS = hi_lo(region("wpad_split", RW + 20 * KB, 8 * KB, F32R), 0, KD, GW)
        eps_col = sb("eps_col", [P, 1])
        ss = sb("ss", [P, NT])
        rstd = sb("rstd", [P, NT])
        lnt = sb("lnt", [P, NT])
        work = sb("work", [P, 20 * KB])
        htmp = work[:, 0:2 * D].rearrange("p (b d) -> p b d", b=2)
        pnat = htmp
        tt = [work[:, 2 * D + i * BANK:2 * D + (i + 1) * BANK] for i in range(2)]
        vmem = work[:, 3 * D:5 * D].rearrange("p (m d) -> p m d", m=MT)
        cin = work[:, 2 * D:2 * D + 2 * (SEQ + 4)].rearrange("p (b s) -> p b s", b=2)
        psum = ctx.enter_context(nc.psum_tensor("psum", [P, 8, BANK], F32))

        stack = work[:, 0:SEQ]
        R_G, R_F, R_L, R_K, R_M = range(5)
        grow = [work[0:MH, i * SEQ:(i + 1) * SEQ] for i in range(5)]
        mrow = grow[R_M]
        GC = GW
        cols = work[:, SEQ:SEQ + NT * GC].rearrange("p (c g) -> p c g", c=NT)
        gcol, wicol, flcol, wscol = (cols[:, :, 32 * i:32 * i + MH] for i in range(4))
        woldB = work[:, SEQ + NT * GC:SEQ + NT * GC + NT * MH].rearrange("p (h c) -> p h c", h=MH)
        mprev = sb("mprev", [MH, NT])
        wold = sb("wold", [MH, NT])
        S0 = RW
        NZ, NLT, NL, NX, NRB = 4, 2, 3, 4, 3
        bufs = [view(S0 + i * BANK, BANK) for i in range(16)] + [work[:, i * BANK:(i + 1) * BANK] for i in range(4)]
        zs, bufs = bufs[:NZ], bufs[NZ:]
        lt, bufs = bufs[:NLT], bufs[NLT:]
        Lb, bufs = bufs[:NL], bufs[NL:]
        ex, bufs = bufs[:NX], bufs[NX:]
        Rb, bufs = bufs[:NRB], bufs[NRB:]
        osq, ors, of = bufs[:3]
        E1 = DH + 1
        Dm = [view(S0 + i * BANK, BANK) for i in range(2)]
        Pm = [view(S0 + (2 + i) * BANK, BANK) for i in range(2)]
        vsb = [view(S0 + 4 * BANK + i * MH * E1, MH, E1) for i in range(2)]
        inter = view(S0 + 4 * BANK + 2 * MH * E1, MH, E1)
        wk = SEQ + NT * GC + NT * MH
        CT = [work[:, wk + i * MH * E1:wk + (i + 1) * MH * E1].rearrange("p (h e) -> p h e", h=MH) for i in range(2)]
        wk += 2 * MH * E1
        junk = work[:, wk:wk + DH]
        wk += DH
        assert wk <= 4 * SEQ
        mss = sb("mss", [P, NT * MH])
        mden = sb("mden", [P, NT, MH])
        mfac = sb("mfac", [P, NT, MH])

        G_MIX, G_KV, G_MEM, G_FFN = 0, KD, 2 * KD, 3 * KD
        V_CW = 4 * KD
        V_CB = V_CW + CW * 2 * MH
        V_SBG = V_CB + 2 * MH

        vec_in = sem("vec_in")
        x_in = [sem(f"x_in{i}") for i in range(NT)]
        mem_in = sem("mem_in")
        raw_in = [sem("raw_in0"), sem("raw_in1")]
        w_hi, w_lo, rs_done = sem("w_hi"), sem("w_lo"), sem("rs_done")
        pad_hi, pad_lo = sem("pad_hi"), sem("pad_lo")
        scaled, hi_part, ym_hi, o_made, o_hi, oT_hi = (
            sem(n) for n in ("scaled", "hi_part", "ym_hi", "o_made", "o_hi", "oT_hi"))
        const_made = sem("const_made")
        pool_chain = sem("pool_chain")
        dve_chain = sem("dve_chain")
        act_chain = sem("act_chain")
        vec_tr = sem("vec_tr")
        vecT_ready = sem("vecT_ready")
        h_made = sem("h_made")
        h_trans = sem("h_trans")
        hT_part = sem("hT_part")
        tile_out = sem("tile_out")
        evac = {"act": sem("evac_act"), "dve": sem("evac_dve")}
        conv_done = sem("conv_done")
        silu_done = sem("silu_done")
        gate_pe = sem("gate_pe")
        gate_dve = sem("gate_dve")
        gate_act = sem("gate_act")
        z_ready, zs_done, ab_done, l1_done, L_done = (sem(n) for n in ("z_ready", "zs_done", "ab_done", "l1_done", "L_done"))
        Lmasked, R_done, tail_ready, ex_done, ex_masked = (
            sem(n) for n in ("Lmasked", "R_done", "tail_ready", "ex_done", "ex_masked"))
        a_done, av_done, osq_done, ossq_ready, ors_done, sb_out = (
            sem(n) for n in ("a_done", "av_done", "osq_done", "ossq_ready", "ors_done", "sb_out"))
        kn_ready, kn_done = sem("kn_ready"), sem("kn_done")
        mb_ready, kq_ready, D_done, D_masked, W_done, Pm_done = (
            sem(n) for n in ("mb_ready", "kq_ready", "D_done", "D_masked", "W_done", "Pm_done"))
        vs_done, num_ready, inter_ready, U_ready, inter_done, num_done, CT_done = (
            sem(n) for n in ("vs_done", "num_ready", "inter_ready", "U_ready", "inter_done", "num_done", "CT_done"))
        mss_done, ml_fac, ml_rs, yn_done, yn_trans, ym_done = (
            sem(n) for n in ("mss_done", "ml_fac", "ml_rs", "yn_done", "yn_trans", "ym_done"))
        gate_scaled = sem("gate_scaled")
        wpad_in, lgT_done = sem("wpad_in"), sem("lgT_done")
        VEC_DMAS = 12
        sc_ready, mx_done, p_done, pn_done, pt_ready, pt_done = (
            sem(n) for n in ("sc_ready", "mx_done", "p_done", "pn_done", "pt_ready", "pt_done"))
        hn = view(RP + 64 * KB, NT, D)

        def hS_at(at):
            return hi_lo(act_split, at, KD, F)

        w1s, w3s = hS_at(0), hS_at(32 * KB)
        w2s = hi_lo(region("w2_split", RP + 32 * KB, 32 * KB, F32R), 0, KF, D)
        NQ = 6
        raw_a = region("expert_raw_a", RP + 96 * KB, 16 * KB)
        raw_b = region("expert_raw_b", RP, 32 * KB)
        eraw = [w[:, i * 8 * KB:(i + 1) * 8 * KB] for w, n in ((raw_a, 2), (raw_b, 4)) for i in range(n)]
        eparts = [[w[z][:, KD // 2 * q:KD // 2 * (q + 1), :] for z in range(2)] for w in (w1s, w3s) for q in range(2)]
        eparts += [[w2s[z][:, KF // 2 * q:KF // 2 * (q + 1), :] for z in range(2)] for q in range(2)]
        eraw = [r.rearrange("p (k n) -> p k n", k=e[0].shape[1]) for r, e in zip(eraw, eparts)]
        RB = RP + 64 * KB
        xb = view(RB, D)
        xTs = hi_lo(region("xT_split", RB + 4 * KB, 8 * KB, F32R), 0, KD, P)
        yb = view(RB + 12 * KB, D)
        sg = view(RB + 16 * KB, F)
        hh = view(RB + 18 * KB, F)
        hhTs = hi_lo(region("hhT_split", RB + 20 * KB, 4 * KB, F32R), 0, KF, P)
        gffn = work[:, 4 * D:5 * D]
        zero = view(RP + 61 * KB, D)
        yg_t = [[view(4 * (2 * i + c) * KB, D) for c in range(2)] for i in range(NT)]
        gfin = work[:, 4 * D:5 * D]
        otile = [view(RP + (64 + 4 * i) * KB, D) for i in range(2)]
        sqj = view(RP + 72 * KB, D)
        rpad = work[:, 2 * D:2 * D + KD * 100].rearrange("p (k r) -> p k r", k=KD)
        rpadS = hi_lo(region("rpad_split", RP + 32 * KB, 8 * KB, F32R), 0, KD, 100)
        lgT = work[0:NR, 3 * D:4 * D]
        carve = {"at": 0}

        def small(*shape):
            n = 1
            for q in shape:
                n *= q
            w = work[:, carve["at"]:carve["at"] + n]
            carve["at"] += n
            names = "abc"[:len(shape)]
            if len(shape) == 1:
                return w
            return w.rearrange("p (%s) -> p %s" % (" ".join(names), " ".join(names)),
                               **{k: q for k, q in zip(names, shape)})

        lg = small(NT, NR)
        elt = lg[:, :, NG:NR].rearrange("p t (g e) -> p t g e", g=NG)
        r4 = {n: small(NT, 4) for n in ("oh", "eq", "es", "t1", "t2", "tmp")}
        r1 = {n: small(NT) for n in ("mx", "left", "psel", "m1", "m2", "w1", "w2", "pos")}
        re = {n: small(NT, NG, NE) for n in ("A1", "A2", "M", "tot", "pos")}
        rc = {n: small(E) for n in ("cnt", "nb", "cum", "one", "base")}
        all_stored = sem("all_stored")
        pmx = sb("pmx", [P, NT, XH])
        psm = sb("psm", [P, NT, XH])
        idx = sb("idx", [P, 2, NT], I32)
        nb_i = sb("nb_i", [1, E], I32)
        cum_i = sb("cum_i", [1, E], I32)
        zero_made, zero_filled, routed, scattered, rt_pe, rt_dve, rt_act = (
            sem(n) for n in ("zero_made", "zero_filled", "routed", "scattered", "rt_pe", "rt_dve", "rt_act"))
        moe_in = [sem(f"moe_in{q}") for q in range(NQ)]
        e_hi, e_lo, xT_hi, hhT_hi, spilled, gffn_in, hn_scaled = (
            sem(n) for n in ("e_hi", "e_lo", "xT_hi", "hhT_hi", "spilled", "gffn_in", "hn_scaled"))
        xb_in, xt_ready, xT_done, a_ready, u_ready, sg_done, hh_done = (
            sem(n) for n in ("xb_in", "xt_ready", "xT_done", "a_ready", "u_ready", "sg_done", "hh_done"))
        ht_ready, hhT_done, y_ready, y_evac, y_stored = (
            sem(n) for n in ("ht_ready", "hhT_done", "y_ready", "y_evac", "y_stored"))
        gfin_in, moe_added, fin_rs, out_made = (
            sem(n) for n in ("gfin_in", "moe_added", "fin_rs", "out_made"))
        yg_in = [sem(f"yg_in{i}") for i in range(NT)]
        out_stored = [sem(f"out_stored{i}") for i in range(2)]

        dumped = sem("dumped")
        fin = sem("fin")

        steps = []
        for h in range(MH):
            for hf in range(NH2):
                top = HALF * (hf + 1)
                for j in range(top - 1, -1, -1):
                    lo = max(0, j * P - hf * BANK)
                    steps.append(dict(h=h, hf=hf, j=j, lo=lo, w=BANK - lo, first=(j == top - 1), last=(j == 0),
                                      diag=(j >= HALF * hf), g=h * NH2 + hf))
        NS = len(steps)

        def upto_diag(i):
            return sum(s["diag"] for s in steps[:i + 1])

        def upto_R(i):
            return sum(not s["last"] for s in steps[:i + 1])

        last_step = {s["g"]: i for i, s in enumerate(steps) if s["last"]}
        NGRP = MH * NH2

        def wait_evac(eng, n):
            w, c = evac_no[n]
            eng.wait_ge(evac[w], c)

        def wait_raw(eng, p):
            eng.wait_ge(raw_in[raw_no[p]], 16 * (raw_no[:p + 1].count(raw_no[p])))

        LATE = {PIDX["sq", 0], PIDX["w_out", 0]}

        def buffer_free(eng, p):
            if p >= 2:
                eng.wait_ge(tile_out, piece_end(p - 2))
            if p == 1:
                eng.wait_ge(tile_out, NH2)
            if p in (PIDX["sq", 0], PIDX["sq", 1]):
                eng.wait_ge(num_ready, NT)
                eng.wait_ge(num_done, NT)
            if p in (PIDX["w_out", 0], PIDX["w_out", 1]):
                eng.wait_ge(sb_out, NGRP)
                eng.wait_ge(av_done, NS)
            if p == PIDX["w_mo", 1]:
                eng.wait_ge(tile_out, TIDX["oT", 0, 2 * KD - 1] + 1)

        block = ctx.enter_context(nc.Block())

        @block.sync
        def _(sp):
            def load_raw(p):
                former = [q for q in range(p) if raw_no[q] == raw_no[p]]
                if former:
                    sp.wait_ge(w_lo, former[-1] + 1)
                sp.dma_start(raws[raw_no[p]], pieces[p][2]).then_inc(raw_in[raw_no[p]], 16)

            for i in range(NT):
                sp.dma_start(xs[:, i, :], x_d[i]).then_inc(x_in[i], 16)
                if i == 0:
                    load_raw(0)
            xg_b = xg.rearrange("(b p) d -> b p d", p=P)
            for p in range(1, PIDX["mv", 1]):
                load_raw(p)
                if p == 2:
                    sp.wait_ge(zero_made, 1)
                if p >= 2:
                    for b in range(11 * (p - 2), min(11 * (p - 1), SLOT_BLOCKS)):
                        sp.dma_start(xg_b[b], zero).then_inc(zero_filled, 16)
            for p in range(PIDX["mv", 1], PIDX["w_out", 0] + 1):
                load_raw(p)
            sp.wait_ge(w_lo, PIDX["w_out", 0])
            sp.wait_ge(av_done, NS)
            sp.wait_ge(yn_trans, NT)
            for i in range(NT):
                sp.dma_start(x1[:, i, :], x_d[i]).then_inc(x_in[i], 16)
            for i in range(MT):
                sp.dma_start(mems[:, i, :], mem_d[i]).then_inc(mem_in, 16)
            for p in range(PIDX["w_out", 0] + 1, NP):
                load_raw(p)
            for i in range(NT):
                wait_evac(sp, TIDX["w_mo", 3, i // 2])
                sp.dma_start(x1_d[i], x1[:, i, :]).then_inc(spilled, 16)

            def load_piece(e, q):
                w = t[("w_e1", "w_e3", "w_e2")[q // 2]][0].rearrange("g e d f -> (g e) d f")[bass.ds(e, 1)]
                src = w.rearrange("g (h k p) n -> h p (g k) n", h=2, p=P)[q % 2]
                sp.dma_start(eraw[q], src).then_inc(moe_in[q], 16)

            sp.wait_ge(tile_out, len(tiles))
            sp.wait_ge(w_lo, NP)
            for q in range(NQ):
                if q == 2:
                    sp.wait_ge(h_made, 3 * NT + MT)
                    sp.wait_ge(spilled, 16 * NT)
                load_piece(0, q)
            with sp.Fori(0, E - 1) as e:
                for q in range(NQ):
                    sp.wait_ge(e_lo, e * NQ + q + 1)
                    load_piece(e + 1, q)
            sp.wait_ge(hn_scaled, NT)
            sp.dma_start(gfin, t["ln_final"].rearrange("(a d) -> a d", a=1).broadcast_to([P, D])).then_inc(gfin_in, 16)
            sp.wait_ge(e_lo, E * NQ)
            for i in range(NT):
                sp.dma_start(x1[:, i, :], x1_d[i]).then_inc(x_in[i], 16)
            for i in range(NT):
                sp.wait_ge(out_made, i + 1)
                sp.dma_start(out_d[i], otile[i % 2]).then_inc(out_stored[i % 2], 16)
            for i in range(2):
                sp.wait_ge(out_stored[i], 16 * NT // 2)
            if dbg is not None:
                sp.wait_ge(fin, 1)
                at = 0
                for n, (a0, ln) in enumerate(DUMP):
                    sp.dma_start(dbg[:, at:at + ln], arena[:, a0:a0 + ln]).then_inc(dumped, 16)
                    at += ln
                    sp.wait_ge(dumped, 16 * (n + 1))

        @block.gpsimd
        def _(pool):
            chain = [0]

            def link(ins):
                chain[0] += 1
                ins.then_inc(pool_chain, 1)
                pool.wait_ge(pool_chain, chain[0])

            g = nc.gpsimd
            g.memset(wpad, 0.0).then_inc(pool_chain, 1)
            g.memset(ident[:], 0.0).then_inc(pool_chain, 1)
            g.memset(uincl[:], 1.0).then_inc(pool_chain, 1)
            g.memset(ustrict[:], 1.0).then_inc(pool_chain, 1)
            g.memset(sel[:], 0.0).then_inc(pool_chain, 1)
            chain[0] = 5
            g.memset(ones[:], 1.0).then_inc(const_made, 1)
            g.memset(eps_col[:], EPS).then_inc(const_made, 1)
            pool.wait_ge(pool_chain, 5)
            for c in range(2):
                pool.dma_start(wpad[:, :, 32 * c:32 * c + MH], W_IN[:, OFF["gates"] + c * MH:OFF["gates"] + (c + 1) * MH]
                               .rearrange("(k p) n -> p k n", p=P)).then_inc(wpad_in, 16)
            g.affine_select(out=ident[:], in_=ident[:], compare_op=ALU.not_equal, fill=1.0, base=0,
                            pattern=[[-1, P]], channel_multiplier=1).then_inc(const_made, 1)
            g.affine_select(out=uincl[:], in_=uincl[:], compare_op=ALU.is_ge, fill=0.0, base=0,
                            pattern=[[-1, P]], channel_multiplier=1).then_inc(const_made, 1)
            g.affine_select(out=ustrict[:], in_=ustrict[:], compare_op=ALU.is_gt, fill=0.0, base=0,
                            pattern=[[1, P]], channel_multiplier=-1).then_inc(const_made, 1)
            g.affine_select(out=sel[:], in_=sel[:], compare_op=ALU.not_equal, fill=1.0, base=0,
                            pattern=[[-1, MH], [0, P]], channel_multiplier=1).then_inc(const_made, 1)
            g.memset(zero, 0.0).then_inc(zero_made, 1)

            pool.wait_ge(vec_in, VEC_DMAS * 16)
            for i in range(NT):
                wait_evac(pool, TIDX["mo", 1, i // 2])
                g.tensor_tensor(gate_o[:, i, :], gate_o[:, i, :], mlg[:], ALU.mult).then_inc(gate_scaled, 1)

            for c in range(NT):
                pool.wait_ge(D_done, c + 1)
                v4 = Dm[c % 2].rearrange("p (h s) -> p h s", h=MH)
                g.affine_select(out=v4, in_=v4, compare_op=ALU.is_ge, fill=-NEG, base=0,
                                pattern=[[0, MH], [1, P]], channel_multiplier=-1).then_inc(D_masked, 1)

            for k in range(NS + 3):
                i = k - 1
                if 0 <= i < NS:
                    s = steps[i]
                    lo = s["lo"]
                    L, R, Rn = Lb[i % NL], Rb[i % NRB], Rb[(i + 1) % NRB]
                    pool.wait_ge(L_done, i + 1)
                    if s["diag"]:
                        g.affine_select(out=L[:, lo:lo + P], in_=L[:, lo:lo + P], compare_op=ALU.is_gt,
                                        fill=0.0, base=0, pattern=[[1, P]], channel_multiplier=-1).then_inc(Lmasked, 1)
                        pool.wait_ge(Lmasked, upto_diag(i))
                    if not s["last"]:
                        if i >= 2:
                            pool.wait_ge(tail_ready, i - 1)
                        if i and upto_R(i - 1):
                            pool.wait_ge(R_done, upto_R(i - 1))
                        if lo:
                            link(g.memset(Rn[:, 0:lo], 0.0))
                        if s["first"]:
                            g.tensor_copy(Rn[:, lo:BANK], L[:, lo:BANK]).then_inc(R_done, 1)
                        else:
                            g.tensor_tensor(Rn[:, lo:BANK], R[:, lo:BANK], L[:, lo:BANK], ALU.add).then_inc(R_done, 1)
                i = k - 2
                if 0 <= i < NS and steps[i]["diag"]:
                    lo = steps[i]["lo"]
                    e = ex[i % NX][:, lo:lo + P]
                    pool.wait_ge(ex_done, i + 1)
                    g.affine_select(out=e, in_=e, compare_op=ALU.is_gt, fill=NEG, base=0, pattern=[[1, P]],
                                    channel_multiplier=-1).then_inc(ex_masked, 1)

            pool.wait_ge(tile_out, piece_end(PIDX["w_mq", 3]))
            link(g.memset(rpad, 0.0))
            pool.dma_start(rpad[:, :, 0:NG], t["w_rg"][0].rearrange("(k p) n -> p k n", p=P)).then_inc(wpad_in, 16)
            pool.dma_start(rpad[:, :, NG:NR], t["w_re"][0].rearrange("(k p) n -> p k n", p=P)).then_inc(wpad_in, 16)

            pool.wait_ge(tile_out, TIDX["oT", 0, 2 * KD - 1] + 1)
            pool.dma_start(gffn, t["ln_ffn"].broadcast_to([P, D])).then_inc(gffn_in, 16)
            pool.wait_ge(gffn_in, 16)
            for i in range(NT):
                pool.wait_ge(h_trans, 2 * NT + MT + i + 1)
                g.tensor_tensor(hn[:, i, :], hn[:, i, :], gffn, ALU.mult).then_inc(hn_scaled, 1)

            pool.wait_ge(hn_scaled, NT)
            pool.wait_ge(zero_filled, 16 * SLOT_BLOCKS)
            pool.wait_ge(routed, 1)
            for i in range(NT):
                for c in range(2):
                    g.indirect_dma_start(out=xg, out_offset=bass.IndirectOffsetOnAxis(ap=idx[:, c, i:i + 1], axis=0),
                                         in_=hn[:, i, :], in_offset=None).then_inc(scattered, 16)
            pool.wait_ge(scattered, 16 * 2 * NT)
            xg_b = xg.rearrange("(b p) d -> b p d", p=P)
            for b in range(2):
                if b:
                    pool.wait_ge(xt_ready, 1)
                pool.dma_start(xb, xg_b[b]).then_inc(xb_in, 16)
            blk = pool.alloc_register("pool_block")
            pool.reg_mov(blk, 0)
            tot = pool.value_load(cum_i[0:1, E - 1:E], min_val=1, max_val=MAXB)
            with pool.Fori(0, tot) as b:
                pool.wait_ge(xt_ready, b + 2)
                g.dma_start(xb, xg_b[bass.ds(b + 2, 1)].rearrange("a p d -> p (a d)")).then_inc(xb_in, 16)
            pool.wait_ge(y_stored, (tot + 1) * 16)
            pool.sem_inc(all_stored, 1)
            pool.wait_ge(all_stored, 1)
            for i in range(NT):
                for c in range(2):
                    g.indirect_dma_start(out=yg_t[i][c], out_offset=None, in_=xg,
                                         in_offset=bass.IndirectOffsetOnAxis(ap=idx[:, c, i:i + 1], axis=0)).then_inc(yg_in[i], 16)

        @block.scalar
        def _(act):
            chain = [0]
            a = nc.scalar.activation

            def link(ins):
                chain[0] += 1
                ins.then_inc(act_chain, 1)
                act.wait_ge(act_chain, chain[0])

            def split_hi(p):
                wait_raw(act, p)
                buffer_free(act, p)
                a(wS[p % 2][0], raws[raw_no[p]], ACT.Copy).then_inc(w_hi, 1)

            def begin_piece(p):
                if p + 1 < NP and p + 1 not in LATE:
                    split_hi(p + 1)

            def out_of(n):
                act.wait_ge(tile_out, n + 1)
                return psum[:, n % RING, :]

            at = 0
            for src, n in ((t["ln_mix"][0], KD), (t["ln_memkv"][0], KD), (t["ln_mem"][0], KD), (t["ln_ffn"][0], KD),
                           (t["conv_w"][0].rearrange("w c -> (w c)"), CW * 2 * MH), (t["conv_b"][0], 2 * MH),
                           (t["sb_head_g"][0], MH)):
                act.dma_start(vec_rows[at:at + n, :], src.rearrange("(k p) -> k p", p=P)).then_inc(vec_in, 16)
                at += n
            act.dma_start(gbias[0:MH, :], t["i_bias"].rearrange("a h -> h a")).then_inc(vec_in, 16)
            act.dma_start(gbias[32:32 + MH, :], t["f_bias"].rearrange("a h -> h a")).then_inc(vec_in, 16)
            act.dma_start(rbias[0:NG, :], t["b_rg"].rearrange("a h -> h a")).then_inc(vec_in, 16)
            act.dma_start(rbias[NG:NR, :], t["b_re"].rearrange("a h -> h a")).then_inc(vec_in, 16)
            act.dma_start(mlg[:], t["ml_head_g"].broadcast_to([P, MW])).then_inc(vec_in, 16)

            def norm_rstd(j, i, src, natural=None):
                if natural is not None:
                    o = natural[:, i, :]
                else:
                    o = htmp[:, j % 2, :]
                    if j >= 2:
                        act.wait_ge(h_trans, j - 1)
                link(a(o, src[:, i, :], ACT.Square, accum_out=ss[:, i:i + 1]))
                link(a(lnt[:, i:i + 1], ss[:, i:i + 1], ACT.Ln, bias=eps_col[:], scale=1.0 / D))
                a(rstd[:, i:i + 1], lnt[:, i:i + 1], ACT.Exp, scale=-0.5).then_inc(rs_done, 1)

            def norm_hi(j, i, dst):
                for q in range(2):
                    act.wait_ge(scaled, 2 * j + q + 1)
                    a(dst[0][:, HALF * q:HALF * (q + 1), i * P:(i + 1) * P],
                      tt[q].rearrange("p (k s) -> p k s", k=HALF), ACT.Copy).then_inc(hi_part, 1)

            nc.scalar.preload_act_table_set("natural_log_exp_and_others")
            act.wait_ge(const_made, 2)
            for i in range(NT + 1):
                if i < NT:
                    act.wait_ge(x_in[i], 16)
                    norm_rstd(i, i, xs)
                if i:
                    norm_hi(i - 1, i - 1, hS)
                if i == 3:
                    split_hi(0)
                if i == 5:
                    act.wait_ge(wpad_in, 32)
                    a(wpadS[0], wpad, ACT.Copy).then_inc(pad_hi, 1)

            for ch in range(2 * MH + 1):
                if ch < 2 * MH:
                    nm, c = ("mq", "mk")[ch // MH], ch % MH
                    if c % 2 == 0:
                        begin_piece(PIDX[nm, c // 2])
                    for hf in range(NH2):
                        if hf == 0 and ch >= 2:
                            act.wait_ge(conv_done, ch - 1)
                        n = TIDX[nm, c // 2, (c % 2) * NH2 + hf]
                        a(cin[:, ch % 2, CW - 1 + hf * BANK:CW - 1 + (hf + 1) * BANK], out_of(n),
                          ACT.Copy).then_inc(evac["act"], 1)
                if ch >= 1:
                    c = ch - 1
                    act.wait_ge(conv_done, c + 1)
                    v = (mqT if c < MH else mkT)[:, c % MH, :]
                    a(v, v, ACT.Silu).then_inc(silu_done, 1)

            def N_evacs(nm, c, dst, func=ACT.Copy):
                begin_piece(PIDX[nm, c])
                for i in range(NT // 2):
                    o = out_of(TIDX[nm, c, i]).rearrange("p (t n) -> p t n", t=2)
                    a(dst[:, 2 * i:2 * i + 2, c * PC:(c + 1) * PC], o, func).then_inc(evac["act"], 1)

            def v_evacs(c):
                begin_piece(PIDX["mv", c])
                for i in range(NT // 2):
                    o = out_of(TIDX["mv", c, i]).rearrange("p (t h e) -> p t h e", t=2, h=2)
                    for q in range(2):
                        ins = a(vaug[:, 2 * i + q, 2 * c:2 * c + 2, 0:DH], o[:, q, :, :], ACT.Copy)
                    ins.then_inc(evac["act"], 1)

            nc.scalar.preload_act_table_set("natural_log_exp_and_others")
            v_evacs(0)
            act.wait_ge(gate_dve, 1)
            link(a(grow[R_L], grow[R_L], ACT.Exp))
            a(grow[R_L], grow[R_L], ACT.Ln, bias=1.0).then_inc(gate_act, 1)
            v_evacs(1)
            act.wait_ge(gate_dve, 2)
            a(stack[32:32 + MH, :], grow[R_L], ACT.Exp).then_inc(gate_act, 1)
            a(stack[64:64 + MH, :], grow[R_F], ACT.Exp, scale=-1.0).then_inc(gate_act, 1)
            a(stack[96:96 + MH, :], grow[R_K], ACT.Exp).then_inc(gate_act, 1)
            a(wold[:], wold[:], ACT.Exp).then_inc(gate_act, 1)
            act.wait_ge(zero_filled, 16 * SLOT_BLOCKS)
            for c in range(2):
                N_evacs("mo", c, gate_o, ACT.Sigmoid)

            nc.scalar.preload_act_table_set("natural_log_exp_and_others")
            for c in range(NT):
                act.wait_ge(kn_ready, c + 1)
                if c == 0:
                    act.wait_ge(tile_out, piece_end(PIDX["mo", 1]))
                a(kN[:, c, :], psum[:, 6 + c % 2, :], ACT.Copy).then_inc(kn_done, 1)
            for c in range(NT + 1):
                if c < NT:
                    act.wait_ge(D_masked, c + 1)
                    a(Dm[c % 2], Dm[c % 2], ACT.Exp, scale=-1.0).then_inc(W_done, 1)
                if c:
                    act.wait_ge(num_done, c)
                    for h in range(MH):
                        n = (c - 1) * MH + h
                        if n:
                            act.wait_ge(mss_done, n)
                        a(junk, vaug[:, c - 1, h, 0:DH], ACT.Square, accum_out=mss[:, n:n + 1]).then_inc(mss_done, 1)
            act.wait_ge(ml_fac, 1)
            link(a(mfac[:], mfac[:], ACT.Ln, bias=eps_col[:]))
            a(mfac[:], mfac[:], ACT.Exp, scale=-0.5).then_inc(ml_rs, 1)

            split_hi(PIDX["sq", 0])
            for c in range(2):
                begin_piece(PIDX["sq", c])
                for i in range(4):
                    o = out_of(TIDX["sq", c, i])
                    a(sqT[:, 2 * c + i // NH2, (i % NH2) * BANK:(i % NH2 + 1) * BANK], o, ACT.Copy,
                      scale=QSCALE).then_inc(evac["act"], 1)
            for c in range(2):
                begin_piece(PIDX["sk", c])
            for c in range(2):
                N_evacs("sv", c, svn)
            for c in range(NT):
                act.wait_ge(yn_trans, c + 1)
                a(hS[0][:, 0:MH, c * P:(c + 1) * P], psum[:, 4 + c % 2, :].rearrange("p (h s) -> p h s", h=MH),
                  ACT.Copy).then_inc(ym_hi, 1)

            for k in range(NS + 12):
                if k < NS:
                    lo = steps[k]["lo"]
                    z, l = zs[k % NZ], lt[k % NLT]
                    act.wait_ge(z_ready, k + 1)
                    if k >= NZ:
                        act.wait_ge(ex_done, k - NZ + 1)
                    a(z[:, lo:BANK], psum[:, k % 2, lo:BANK], ACT.Copy).then_inc(zs_done, 1)
                    act.wait_ge(ab_done, k + 1)
                    link(a(l[:, lo:BANK], l[:, lo:BANK], ACT.Exp))
                    a(l[:, lo:BANK], l[:, lo:BANK], ACT.Ln, bias=1.0).then_inc(l1_done, 1)
                i = k - 3
                if 0 <= i < NS:
                    lo = steps[i]["lo"]
                    if steps[i]["diag"]:
                        act.wait_ge(ex_masked, upto_diag(i))
                    act.wait_ge(ex_done, i + 1)
                    a(ex[i % NX][:, lo:BANK], ex[i % NX][:, lo:BANK], ACT.Exp).then_inc(a_done, 1)
                i = k - 5
                if 0 <= i < NS and steps[i]["last"]:
                    gi = steps[i]["g"]
                    act.wait_ge(av_done, i + 1)
                    if gi:
                        act.wait_ge(ossq_ready, gi)
                    a(osq, psum[:, 4 + gi % 2, :], ACT.Square).then_inc(osq_done, 1)
                i = k - 7
                if 0 <= i < NS and steps[i]["last"]:
                    gi = steps[i]["g"]
                    act.wait_ge(ossq_ready, gi + 1)
                    if gi:
                        act.wait_ge(o_made, gi)
                    link(a(ors, psum[:, 6 + gi % 2, :], ACT.Ln, bias=eps_col[:], scale=1.0 / DH))
                    a(ors, ors, ACT.Exp, scale=-0.5).then_inc(ors_done, 1)
                i = k - 8
                if 0 <= i < NS and steps[i]["last"]:
                    s = steps[i]
                    act.wait_ge(o_made, s["g"] + 1)
                    a(hS[0][:, MH + s["h"], s["hf"] * BANK:(s["hf"] + 1) * BANK], of, ACT.Copy).then_inc(o_hi, 1)

            split_hi(PIDX["w_out", 0])
            begin_piece(PIDX["w_out", 0])
            act.wait_ge(mem_in, 16 * MT)
            for i in range(MT + 1):
                if i < MT:
                    norm_rstd(NT + i, i, mems)
                if i:
                    norm_hi(NT + i - 1, i - 1, mS)
            for c in range(1, 4):
                begin_piece(PIDX["w_out", c])
            for i in range(NT + 1):
                if i < NT:
                    nm, c = ("w_mk", "w_mv")[i // 4], i % 4
                    begin_piece(PIDX[nm, c])
                    wait_evac(act, TIDX["w_out", 3, i // 2])
                    norm_rstd(NT + MT + i, i, x1)
                    o = out_of(TIDX[nm, c, 0])
                    if nm == "w_mk":
                        a(kTm[:, 2 * c:2 * c + 2, :], o.rearrange("p (c m) -> p c m", c=2), ACT.Copy).then_inc(evac["act"], 1)
                    else:
                        a(vmem[:, :, c * PC:(c + 1) * PC], o.rearrange("p (t n) -> p t n", t=2),
                          ACT.Copy).then_inc(evac["act"], 1)
                if i:
                    norm_hi(NT + MT + i - 1, i - 1, hS)
            for c in range(4):
                begin_piece(PIDX["w_mq", c])
                for i in range(4):
                    o = out_of(TIDX["w_mq", c, i])
                    a(qT[:, 2 * c + i // NH2, (i % NH2) * BANK:(i % NH2 + 1) * BANK], o,
                      ACT.Copy).then_inc(evac["act"], 1)

            for k in range(NT + 1):
                if k < NT:
                    act.wait_ge(mx_done, k + 1)
                    if k >= 2:
                        act.wait_ge(pt_ready, k - 1)
                    for h in range(XH):
                        a(pnat[:, k % 2, h * MEM:(h + 1) * MEM],
                          psum[:, 4 + 2 * (k % 2) + h // 2, (h % 2) * MEM:(h % 2 + 1) * MEM], ACT.Exp,
                          bias=pmx[:, k, h:h + 1], scale=XSCALE, accum_out=psm[:, k, h:h + 1]).then_inc(p_done, 1)
                if k >= 1:
                    i = k - 1
                    act.wait_ge(pt_ready, i + 1)
                    if i == 0:
                        act.wait_ge(tile_out, piece_end(PIDX["w_mq", 3]))
                    if i == HALF:
                        act.wait_ge(tile_out, TIDX["oT", 0, KD - 1] + 1)
                    for q in range(2):
                        a(pT[:, 4 * q:4 * q + 4, (i % HALF) * P:(i % HALF + 1) * P],
                          psum[:, 4 + 2 * (i % 2) + q, :].rearrange("p (j s) -> p j s", j=4),
                          ACT.Copy).then_inc(pt_done, 1)
                    if i % HALF == HALF - 1:
                        hf = i // HALF
                        for c in range(KD):
                            n = TIDX["oT", 0, hf * KD + c]
                            a(hS[0][:, c, hf * BANK:(hf + 1) * BANK], out_of(n), ACT.Copy).then_inc(oT_hi, 1)
            for c in range(4):
                begin_piece(PIDX["w_mo", c])

            act.wait_ge(wpad_in, 64)
            act.wait_ge(tile_out, TIDX["oT", 0, 2 * KD - 1] + 1)
            a(rpadS[0], rpad, ACT.Copy).then_inc(pad_hi, 1)
            act.wait_ge(tile_out, len(tiles))
            for i in range(NT + 1):
                if i < NT:
                    wait_evac(act, TIDX["w_mo", 3, i // 2])
                    norm_rstd(2 * NT + MT + i, i, x1, hn)
                if i:
                    norm_hi(2 * NT + MT + i - 1, i - 1, hS)
            act.wait_ge(rt_dve, 1)
            a(r4["tmp"], r4["tmp"], ACT.Exp).then_inc(rt_act, 1)
            act.wait_ge(rt_dve, 2)
            a(r1["w2"], r1["w2"], ACT.Exp).then_inc(rt_act, 1)

            def expert_hi(e, q):
                act.wait_ge(moe_in[q], (e + 1) * 16)
                a(eparts[q][0], eraw[q], ACT.Copy).then_inc(e_hi, 1)

            act.sem_inc(sg_done, 1)
            act.sem_inc(y_evac, 1)
            act.sem_inc(y_stored, 16)
            for q in range(NQ):
                expert_hi(0, q)
            act.wait_ge(routed, 1)

            def x_hi(n):
                act.wait_ge(xt_ready, n)
                a(xTs[0], psum[:, 4:6, :].rearrange("p b (k s) -> p (b k) s", k=HALF), ACT.Copy).then_inc(xT_hi, 1)

            act.wait_ge(scattered, 16 * 2 * NT)
            x_hi(1)
            yg_b = xg.rearrange("(b p) d -> b p d", p=P)
            blk = act.alloc_register("act_block")
            act.reg_mov(blk, 0)

            def block_act(nxt):
                b = act.snap(blk, min_val=0, max_val=MAXB)
                act.wait_ge(a_ready, b + 1)
                act.wait_ge(hh_done, b + 1)
                a(sg, psum[:, 0, :], ACT.Silu).then_inc(sg_done, 1)
                if nxt is not None:
                    for q in range(2):
                        expert_hi(nxt, q)
                x_hi(b + 2)
                act.wait_ge(ht_ready, b + 1)
                a(hhTs[0], psum[:, 6, :].rearrange("p (k s) -> p k s", k=KF), ACT.Copy).then_inc(hhT_hi, 1)
                if nxt is not None:
                    for q in range(2, 4):
                        expert_hi(nxt, q)
                act.wait_ge(y_ready, b + 2)
                act.wait_ge(y_stored, (b + 1) * 16)
                a(yb.rearrange("p (b n) -> p b n", b=2), psum[:, 2:4, :], ACT.Copy).then_inc(y_evac, 1)
                act.wait_ge(y_evac, b + 2)
                act.dma_start(yg_b[bass.ds(b, 1)].rearrange("a p d -> p (a d)"), yb).then_inc(y_stored, 16)
                if nxt is not None:
                    for q in range(4, NQ):
                        expert_hi(nxt, q)
                act.reg_add(blk, blk, 1)

            def expert_act(e, nxt):
                n_more = act.value_load(nb_i[0:1, bass.ds(e, 1)], min_val=0, max_val=NT - 1)
                with act.If(n_more > 0):
                    with act.Fori(0, n_more) as _j:
                        block_act(None)
                block_act(nxt)

            nc.scalar.preload_act_table(ACT.Silu)
            with act.Fori(0, E - 1) as e:
                expert_act(e, e + 1)
            expert_act(E - 1, None)
            nc.scalar.preload_act_table_set("natural_log_exp_and_others")
            for i in range(NT):
                act.wait_ge(moe_added, i + 1)
                link(a(sqj, x1[:, i, :], ACT.Square, accum_out=ss[:, i:i + 1]))
                link(a(lnt[:, i:i + 1], ss[:, i:i + 1], ACT.Ln, bias=eps_col[:], scale=1.0 / D))
                a(rstd[:, i:i + 1], lnt[:, i:i + 1], ACT.Exp, scale=-0.5).then_inc(fin_rs, 1)

        @block.vector
        def _(dve):
            chain = [0]
            v = nc.vector

            def link(ins):
                chain[0] += 1
                ins.then_inc(dve_chain, 1)
                dve.wait_ge(dve_chain, chain[0])

            def out_of(n):
                dve.wait_ge(tile_out, n + 1)
                return psum[:, n % RING, :]

            def split_lo(p):
                dve.wait_ge(w_hi, p + 1)
                buffer_free(dve, p)
                wait_raw(dve, p)
                v.tensor_tensor(wS[p % 2][1], raws[raw_no[p]], wS[p % 2][0].bitcast(F32), ALU.subtract).then_inc(w_lo, 1)

            def begin_piece(p):
                if p + 1 < NP and p + 1 not in LATE:
                    split_lo(p + 1)

            def norm_scale(j, i, src, natural=None):
                o = htmp[:, j % 2, :] if natural is None else natural[:, i, :]
                dve.wait_ge(rs_done, j + 1)
                v.tensor_scalar(o, src[:, i, :], rstd[:, i:i + 1], None, ALU.mult).then_inc(h_made, 1)

            def norm_parts(j, i, dst, goff):
                dve.wait_ge(h_trans, j + 1)
                if j:
                    dve.wait_ge(hT_part, 2 * j)
                for q in range(2):
                    v.tensor_tensor(tt[q].rearrange("p (k s) -> p k s", k=HALF),
                                    psum[:, 4 + 2 * (j % 2) + q, :].rearrange("p (k s) -> p k s", k=HALF),
                                    vecT[:, goff + HALF * q:goff + HALF * (q + 1)].unsqueeze(2).broadcast_to(
                                        [P, HALF, P]), ALU.mult).then_inc(scaled, 1)
                for q in range(2):
                    sl = (slice(None), slice(HALF * q, HALF * (q + 1)), slice(i * P, (i + 1) * P))
                    dve.wait_ge(hi_part, 2 * j + q + 1)
                    v.tensor_tensor(dst[1][sl], tt[q].rearrange("p (k s) -> p k s", k=HALF),
                                    dst[0][sl].bitcast(F32), ALU.subtract).then_inc(hT_part, 1)

            for i in range(NT + 1):
                if i < NT:
                    dve.wait_ge(x_in[i], 16)
                    norm_scale(i, i, xs)
                if i == 1:
                    dve.wait_ge(vec_tr, 1)
                    v.tensor_copy(vecT[:], psum[:, 0, 0:NV]).then_inc(vecT_ready, 1)
                    dve.wait_ge(vecT_ready, 1)
                if i:
                    norm_parts(i - 1, i - 1, hS, G_MIX)
                if i == 3:
                    split_lo(0)
                if i == 5:
                    dve.wait_ge(pad_hi, 1)
                    v.tensor_tensor(wpadS[1], wpad, wpadS[0].bitcast(F32), ALU.subtract).then_inc(pad_lo, 1)

            dve.wait_ge(h_trans, NT)
            link(v.memset(stack, 0.0))
            for b in range(2):
                link(v.memset(cin[:, b, 0:CW - 1], 0.0))
            for hf in range(NH2):
                o = out_of(TIDX["gates", 0, hf])
                cs = slice(hf * BANK, (hf + 1) * BANK)
                link(v.tensor_scalar(grow[R_G][:, cs], o[0:MH, :], gbias[0:MH, :], None, ALU.add))
                v.tensor_scalar(grow[R_F][:, cs], o[32:32 + MH, :], gbias[32:32 + MH, :], None,
                                ALU.add).then_inc(evac["dve"], 1)
            for ch in range(2 * MH):
                nm, c = ("mq", "mk")[ch // MH], ch % MH
                if c % 2 == 0:
                    begin_piece(PIDX[nm, c // 2])
                wait_evac(dve, TIDX[nm, c // 2, (c % 2) * NH2 + 1])
                o = (mqT if ch < MH else mkT)[:, c, :]
                for tap in range(CW - 1, -1, -1):
                    w = vecT[:, V_CW + tap * 2 * MH + ch:V_CW + tap * 2 * MH + ch + 1]
                    src = cin[:, ch % 2, tap:tap + SEQ]
                    if tap == CW - 1:
                        link(v.tensor_scalar(o, src, w, vecT[:, V_CB + ch:V_CB + ch + 1], ALU.mult, ALU.add))
                    elif tap:
                        link(v.scalar_tensor_tensor(o, src, w, o, ALU.mult, ALU.add))
                    else:
                        v.scalar_tensor_tensor(o, src, w, o, ALU.mult, ALU.add).then_inc(conv_done, 1)
            link(v.memset(vaug[:, :, :, DH:DH + 1], 1.0))

            begin_piece(PIDX["mv", 0])
            chunk = [r.rearrange("p (c s) -> p c s", c=NT) for r in grow]
            mch = chunk[R_M]
            dve.wait_ge(conv_done, 2 * MH)
            wait_evac(dve, TIDX["gates", 0, 1])
            v.scalar_tensor_tensor(grow[R_L], grow[R_F], -1.0, grow[R_F], ALU.mult, ALU.min).then_inc(gate_dve, 1)
            link(v.memset(grow[R_K], 1.0))
            link(v.memset(chunk[R_K][:, :, 0:1], 0.0))
            dve.wait_ge(gate_act, 1)
            link(v.scalar_tensor_tensor(grow[R_L], grow[R_F], 0.0, grow[R_L], ALU.min, ALU.subtract))
            link(v.tensor_tensor_scan(grow[R_F], grow[R_K], grow[R_L], 0.0, ALU.mult, ALU.add))
            link(v.tensor_tensor(grow[R_G], grow[R_G], grow[R_F], ALU.subtract))
            link(v.memset(grow[R_K], 0.0))
            link(v.tensor_copy(chunk[R_K][:, 1:NT, 0:1], chunk[R_F][:, 0:NT - 1, P - 1:P]))
            link(v.tensor_tensor_scan(grow[R_M], grow[R_K], grow[R_G], 0.0, ALU.add, ALU.max))
            link(v.memset(mprev[:], 0.0))
            link(v.tensor_tensor(mprev[:, 1:NT].unsqueeze(2), chunk[R_F][:, 0:NT - 1, P - 1:P],
                                 mch[:, 0:NT - 1, P - 1:P], ALU.add))
            begin_piece(PIDX["mv", 1])
            link(v.tensor_tensor(chunk[R_L], mprev[:].unsqueeze(2).broadcast_to([MH, NT, P]), mch, ALU.subtract))
            link(v.tensor_tensor(grow[R_F], grow[R_F], grow[R_M], ALU.add))
            link(v.tensor_tensor(chunk[R_K], chunk[R_G], mch[:, :, P - 1:P].broadcast_to([MH, NT, P]), ALU.subtract))
            v.tensor_tensor(wold[:].unsqueeze(2), mprev[:].unsqueeze(2), mch[:, :, P - 1:P],
                            ALU.subtract).then_inc(gate_dve, 1)
            dve.wait_ge(gate_dve, 2)
            dve.wait_ge(gate_act, 5)
            v.tensor_scalar(stack[96:96 + MH, :], stack[96:96 + MH, :], QSCALE, None, ALU.mult).then_inc(gate_dve, 1)
            begin_piece(PIDX["mo", 0])
            dve.wait_ge(gate_pe, 1)
            for q in range(2):
                link(v.tensor_copy(cols[:, q * HALF:(q + 1) * HALF, :],
                                   psum[:, 4 + q, 0:HALF * GC].rearrange("p (c g) -> p c g", c=HALF)))
            v.tensor_copy(woldB, psum[:, 6, 0:MH * NT].rearrange("p (h c) -> p h c", h=MH)).then_inc(gate_dve, 1)
            dve.wait_ge(gate_dve, 4)

            def two_banks(b):
                return psum[:, b:b + 2, 0:2 * E1].rearrange("p b (h e) -> p b h e", h=2)

            def pairs(ap):
                return ap.rearrange("p (b h) e -> p b h e", b=2)

            def per_head(col, n):
                return col.rearrange("p (b h) -> p b h", b=2).unsqueeze(3).broadcast_to([P, 2, 2, n])

            def distance(c):
                dve.wait_ge(mb_ready, c + 1)
                if c >= 2:
                    dve.wait_ge(Pm_done, c - 1)
                v.tensor_tensor(Dm[c % 2].rearrange("p (h s) -> p h s", h=MH),
                                psum[:, 0, :].rearrange("p (h s) -> p h s", h=MH),
                                gcol[:, c, :].unsqueeze(2).broadcast_to([P, MH, P]), ALU.subtract).then_inc(D_done, 1)

            def weighted_values(c):
                if c >= 2:
                    dve.wait_ge(U_ready, c - 1)
                v.tensor_tensor(vsb[c % 2], vaug[:, c, :, :], wscol[:, c, :].unsqueeze(2).broadcast_to([P, MH, E1]),
                                ALU.mult).then_inc(vs_done, 1)

            dve.wait_ge(tile_out, piece_end(PIDX["mo", 1]))
            distance(0)
            weighted_values(0)
            for c in range(NT):
                dve.wait_ge(kq_ready, c + 1)
                dve.wait_ge(W_done, c + 1)
                if c >= 2:
                    dve.wait_ge(num_ready, c - 1)
                v.scalar_tensor_tensor(Pm[c % 2], psum[:, 1, :], QSCALE, Dm[c % 2], ALU.mult, ALU.mult).then_inc(Pm_done, 1)
                if c < NT - 1:
                    distance(c + 1)
                    weighted_values(c + 1)
                if c:
                    dve.wait_ge(inter_ready, c)
                    if c > 1:
                        dve.wait_ge(num_done, c)
                    v.tensor_tensor(pairs(inter), two_banks(4), per_head(wicol[:, c, :], E1), ALU.mult).then_inc(inter_done, 1)
                    dve.wait_ge(inter_done, c)
                dve.wait_ge(num_ready, c + 1)
                dve.wait_ge(vs_done, c + 1)
                if c:
                    v.tensor_tensor(pairs(vaug[:, c, :, :]), two_banks(2), pairs(inter), ALU.add).then_inc(num_done, 1)
                else:
                    v.tensor_copy(pairs(vaug[:, c, :, :]), two_banks(2)).then_inc(num_done, 1)
                if c < NT - 1:
                    dve.wait_ge(U_ready, c + 1)
                    if c:
                        dve.wait_ge(CT_done, c)
                        link(v.tensor_tensor(CT[(c + 1) % 2], CT[c % 2],
                                             woldB[:, :, c:c + 1].broadcast_to([P, MH, E1]), ALU.mult))
                        v.tensor_tensor(pairs(CT[(c + 1) % 2]), two_banks(6), pairs(CT[(c + 1) % 2]),
                                        ALU.add).then_inc(CT_done, 1)
                    else:
                        v.tensor_copy(pairs(CT[1]), two_banks(6)).then_inc(CT_done, 1)

            dve.wait_ge(mss_done, NT * MH)
            dve.wait_ge(num_done, NT)
            link(v.tensor_copy(mden[:].unsqueeze(3), vaug[:, :, :, DH:E1]))
            link(v.scalar_tensor_tensor(mfac[:], mden[:], -1.0, mden[:], ALU.mult, ALU.max))
            link(v.tensor_tensor(mden[:], mfac[:], flcol, ALU.max))
            link(v.reciprocal(mden[:], mden[:]))
            ms3 = mss[:].rearrange("p (c h) -> p c h", c=NT)
            link(v.tensor_tensor(mfac[:], mden[:], mden[:], ALU.mult))
            v.scalar_tensor_tensor(mfac[:], mfac[:], 1.0 / DH, ms3, ALU.mult, ALU.mult).then_inc(ml_fac, 1)
            split_lo(PIDX["sq", 0])
            dve.wait_ge(ml_rs, 1)
            link(v.tensor_tensor(mfac[:], mfac[:], mden[:], ALU.mult))
            dve.wait_ge(gate_scaled, NT)
            for c in range(NT):
                link(v.tensor_tensor(vaug[:, c, :, 0:DH], vaug[:, c, :, 0:DH],
                                     mfac[:, c, :].unsqueeze(2).broadcast_to([P, MH, DH]), ALU.mult))
                v.tensor_tensor(gate_o[:, c, :].rearrange("p (h e) -> p h e", h=MH), vaug[:, c, :, 0:DH],
                                gate_o[:, c, :].rearrange("p (h e) -> p h e", h=MH), ALU.mult).then_inc(yn_done, 1)

            for c in range(2):
                begin_piece(PIDX["sq", c])
            for c in range(2):
                begin_piece(PIDX["sk", c])
                for i in range(4):
                    o = out_of(TIDX["sk", c, i])
                    v.tensor_copy(skT[:, 2 * c + i // NH2, (i % NH2) * BANK:(i % NH2 + 1) * BANK],
                                  o).then_inc(evac["dve"], 1)
            for c in range(2):
                begin_piece(PIDX["sv", c])
            for c in range(NT):
                dve.wait_ge(ym_hi, c + 1)
                sl = (slice(None), slice(0, MH), slice(c * P, (c + 1) * P))
                v.tensor_tensor(hS[1][sl], psum[:, 4 + c % 2, :].rearrange("p (h s) -> p h s", h=MH),
                                hS[0][sl].bitcast(F32), ALU.subtract).then_inc(ym_done, 1)

            for k in range(NS + 12):
                if k < NS:
                    lo = steps[k]["lo"]
                    z = zs[k % NZ][:, lo:BANK]
                    dve.wait_ge(zs_done, k + 1)
                    if k >= NLT:
                        dve.wait_ge(L_done, k - NLT + 1)
                    v.scalar_tensor_tensor(lt[k % NLT][:, lo:BANK], z, -1.0, z, ALU.mult, ALU.min).then_inc(ab_done, 1)
                i = k - 1
                if 0 <= i < NS:
                    lo = steps[i]["lo"]
                    dve.wait_ge(l1_done, i + 1)
                    if i >= NL:
                        dve.wait_ge(tail_ready, i - NL + 1)
                        if upto_R(i - NL):
                            dve.wait_ge(R_done, upto_R(i - NL))
                    v.scalar_tensor_tensor(Lb[i % NL][:, lo:BANK], zs[i % NZ][:, lo:BANK], 0.0,
                                           lt[i % NLT][:, lo:BANK], ALU.max, ALU.add).then_inc(L_done, 1)
                i = k - 2
                if 0 <= i < NS:
                    lo = steps[i]["lo"]
                    dve.wait_ge(tail_ready, i + 1)
                    if i >= NX:
                        dve.wait_ge(av_done, i - NX + 1)
                    v.tensor_tensor(ex[i % NX][:, lo:BANK], zs[i % NZ][:, lo:BANK], psum[:, 2 + i % 2, lo:BANK],
                                    ALU.subtract).then_inc(ex_done, 1)
                i = k - 7
                if 0 <= i < NS and steps[i]["last"]:
                    s = steps[i]
                    dve.wait_ge(ors_done, s["g"] + 1)
                    if s["g"]:
                        dve.wait_ge(sb_out, s["g"])
                    v.scalar_tensor_tensor(of, psum[:, 4 + s["g"] % 2, :], vecT[:, V_SBG + s["h"]:V_SBG + s["h"] + 1],
                                           ors, ALU.mult, ALU.mult).then_inc(o_made, 1)
                i = k - 8
                if 0 <= i < NS and steps[i]["last"]:
                    s = steps[i]
                    dve.wait_ge(o_hi, s["g"] + 1)
                    sl = (slice(None), MH + s["h"], slice(s["hf"] * BANK, (s["hf"] + 1) * BANK))
                    v.tensor_tensor(hS[1][sl], of, hS[0][sl].bitcast(F32), ALU.subtract).then_inc(sb_out, 1)

            def add_residual(nm, c):
                begin_piece(PIDX[nm, c])
                for i in range(NT // 2):
                    o = out_of(TIDX[nm, c, i]).rearrange("p (t n) -> p t n", t=2)
                    xt = x1[:, 2 * i:2 * i + 2, c * PC:(c + 1) * PC]
                    v.tensor_tensor(xt, xt, o, ALU.add).then_inc(evac["dve"], 1)

            split_lo(PIDX["w_out", 0])
            for i in range(NT):
                dve.wait_ge(x_in[i], 32)
            add_residual("w_out", 0)
            for i in range(MT + 1):
                if i < MT:
                    norm_scale(NT + i, i, mems)
                if i:
                    norm_parts(NT + i - 1, i - 1, mS, G_KV)
            for c in range(1, 4):
                add_residual("w_out", c)
            dve.wait_ge(tile_out, piece_end(PIDX["w_out", 3]))
            for i in range(NT + 1):
                if i < NT:
                    begin_piece(PIDX[("w_mk", "w_mv")[i // 4], i % 4])
                    norm_scale(NT + MT + i, i, x1)
                if i:
                    norm_parts(NT + MT + i - 1, i - 1, hS, G_MEM)
            for c in range(4):
                begin_piece(PIDX["w_mq", c])
            for k in range(NT + 1):
                if k < NT:
                    dve.wait_ge(sc_ready, k + 1)
                    link(v.tensor_reduce(pmx[:, k, :], psum[:, 4 + 2 * (k % 2):6 + 2 * (k % 2), :].rearrange(
                        "p b (h m) -> p (b h) m", h=2), AX.X, ALU.max))
                    v.tensor_scalar(pmx[:, k, :], pmx[:, k, :], -XSCALE, None, ALU.mult).then_inc(mx_done, 1)
                    dve.wait_ge(p_done, XH * (k + 1))
                    link(v.reciprocal(psm[:, k, :], psm[:, k, :]))
                    pk = pnat[:, k % 2, :].rearrange("p (h m) -> p h m", h=XH)
                    v.tensor_tensor(pk, pk, psm[:, k, :].unsqueeze(2).broadcast_to([P, XH, MEM]),
                                    ALU.mult).then_inc(pn_done, 1)
                if k >= 1 and (k - 1) % HALF == HALF - 1:
                    hf = (k - 1) // HALF
                    for c in range(KD):
                        n = TIDX["oT", 0, hf * KD + c]
                        sl = (slice(None), c, slice(hf * BANK, (hf + 1) * BANK))
                        dve.wait_ge(oT_hi, hf * KD + c + 1)
                        v.tensor_tensor(hS[1][sl], out_of(n), hS[0][sl].bitcast(F32),
                                        ALU.subtract).then_inc(evac["dve"], 1)
            for c in range(4):
                add_residual("w_mo", c)
            dve.wait_ge(pad_hi, 2)
            v.tensor_tensor(rpadS[1], rpad, rpadS[0].bitcast(F32), ALU.subtract).then_inc(pad_lo, 1)
            dve.wait_ge(pad_lo, 2)
            for i in range(NT + 1):
                if i < NT:
                    norm_scale(2 * NT + MT + i, i, x1, hn)
                if i:
                    norm_parts(2 * NT + MT + i - 1, i - 1, hS, G_FFN)
            for hf in range(NH2):
                dve.wait_ge(rt_pe, hf + 1)
                v.tensor_scalar(lgT[:, hf * BANK:(hf + 1) * BANK], psum[0:NR, hf, :], rbias[:], None,
                                ALU.add).then_inc(lgT_done, 1)
            dve.wait_ge(rt_pe, NH2 + 1)
            link(v.tensor_copy(lg, psum[:, 2, 0:NT * NR].rearrange("p (t r) -> p t r", t=NT)))

            def over4(col):
                return col.unsqueeze(2).broadcast_to([P, NT, 4])

            def first_max(dst, src, mx):
                link(v.tensor_reduce(mx, src, AX.X, ALU.max))
                link(v.tensor_tensor(r4["eq"], src, over4(mx), ALU.is_equal))
                link(v.memset(r1["left"], 1.0))
                for j in range(4):
                    link(v.tensor_tensor(dst[:, :, j], r4["eq"][:, :, j], r1["left"], ALU.mult))
                    if j < 3:
                        link(v.tensor_tensor(r1["left"], r1["left"], dst[:, :, j], ALU.subtract))

            oh, t1, t2, es = (r4[n] for n in ("oh", "t1", "t2", "es"))
            first_max(oh, lg[:, :, 0:NG], r1["mx"])
            v.tensor_tensor(r4["tmp"], lg[:, :, 0:NG], over4(r1["mx"]), ALU.subtract).then_inc(rt_dve, 1)
            M = re["M"]
            link(v.tensor_tensor(M, elt, oh.unsqueeze(3).broadcast_to([P, NT, NG, NE]), ALU.mult))
            link(v.tensor_reduce(es, M.rearrange("p t g e -> p t e g"), AX.X, ALU.add))
            first_max(t1, es, r1["m1"])
            link(v.scalar_tensor_tensor(es, t1, NEG, es, ALU.mult, ALU.add))
            first_max(t2, es, r1["m2"])
            v.tensor_tensor(r1["w2"], r1["m2"], r1["m1"], ALU.subtract).then_inc(rt_dve, 1)
            g4 = [P, NT, NG, NE]
            link(v.tensor_tensor(re["A1"], oh.unsqueeze(3).broadcast_to(g4), t1.unsqueeze(2).broadcast_to(g4), ALU.mult))
            link(v.tensor_tensor(re["A2"], oh.unsqueeze(3).broadcast_to(g4), t2.unsqueeze(2).broadcast_to(g4), ALU.mult))
            v.tensor_tensor(M, re["A1"], re["A2"], ALU.add).then_inc(rt_dve, 1)
            dve.wait_ge(rt_act, 2)
            link(v.tensor_reduce(r1["psel"], r4["tmp"], AX.X, ALU.add))
            link(v.tensor_scalar(r1["w1"], r1["w2"], 1.0, None, ALU.add))
            link(v.tensor_tensor(r1["w1"], r1["w1"], r1["psel"], ALU.mult))
            link(v.reciprocal(r1["w1"], r1["w1"]))
            link(v.tensor_tensor(r1["w2"], r1["w2"], r1["w1"], ALU.mult))
            dve.wait_ge(rt_pe, NH2 + 2)
            flat = [n.rearrange("p t g e -> p t (g e)") for n in (re["tot"], re["pos"])]
            link(v.tensor_copy(flat[0], psum[:, 1, NT * E:2 * NT * E].rearrange("p (t e) -> p t e", t=NT)))
            link(v.tensor_copy(flat[1], psum[:, 1, 0:NT * E].rearrange("p (t e) -> p t e", t=NT)))
            cnt, nb, cum, one, base = (rc[n] for n in ("cnt", "nb", "cum", "one", "base"))
            link(v.tensor_copy(cnt, flat[0][:, 0, :]))
            for i in range(1, NT):
                link(v.tensor_tensor(flat[1][:, i, :], flat[1][:, i, :], cnt, ALU.add))
                link(v.tensor_tensor(cnt, cnt, flat[0][:, i, :], ALU.add))
            link(v.memset(nb, 1.0))
            link(v.memset(one, 1.0))
            for b in range(1, NT):
                link(v.scalar_tensor_tensor(nb, cnt, float(b * P), nb, ALU.is_gt, ALU.add))
            link(v.tensor_tensor_scan(cum, one, nb, 0.0, ALU.mult, ALU.add))
            link(v.tensor_tensor(base, cum, nb, ALU.subtract))
            link(v.tensor_scalar(base, base, float(P), None, ALU.mult))
            link(v.tensor_tensor(flat[1], flat[1], base.unsqueeze(1).broadcast_to([P, NT, E]), ALU.add))
            for c, A in enumerate((re["A1"], re["A2"])):
                link(v.tensor_tensor(M, A, re["pos"], ALU.mult))
                link(v.tensor_reduce(r1["pos"], M, AX.XY, ALU.add))
                link(v.tensor_copy(idx[:, c, :], r1["pos"]))
            link(v.tensor_scalar(nb_i[:], nb[0:1, :], -1.0, None, ALU.add))
            v.tensor_copy(cum_i[:], cum[0:1, :]).then_inc(routed, 1)

            def expert_lo(e, q, b=None):
                dve.wait_ge(e_hi, e * NQ + q + 1)
                dve.wait_ge(moe_in[q], (e + 1) * 16)
                if b is not None:
                    dve.wait_ge((a_ready, u_ready, y_ready)[q // 2], b + (1 if q < 4 else 2))
                v.tensor_tensor(eparts[q][1], eraw[q], eparts[q][0].bitcast(F32), ALU.subtract).then_inc(e_lo, 1)

            for q in range(NQ):
                expert_lo(0, q)
            dve.wait_ge(routed, 1)
            dve.sem_inc(hh_done, 1)

            def x_lo(n):
                dve.wait_ge(xt_ready, n)
                dve.wait_ge(xT_hi, n)
                v.tensor_tensor(xTs[1], psum[:, 4:6, :].rearrange("p b (k s) -> p (b k) s", k=HALF),
                                xTs[0].bitcast(F32), ALU.subtract).then_inc(xT_done, 1)

            x_lo(1)
            blk = dve.alloc_register("dve_block")
            dve.reg_mov(blk, 0)

            def block_dve(nxt):
                b = dve.snap(blk, min_val=0, max_val=MAXB)
                if nxt is not None:
                    expert_lo(nxt, 0, b)
                dve.wait_ge(u_ready, b + 1)
                dve.wait_ge(sg_done, b + 2)
                v.tensor_tensor(hh, sg, psum[:, 1, :], ALU.mult).then_inc(hh_done, 1)
                if nxt is not None:
                    expert_lo(nxt, 1, b)
                x_lo(b + 2)
                dve.wait_ge(ht_ready, b + 1)
                dve.wait_ge(hhT_hi, b + 1)
                v.tensor_tensor(hhTs[1], psum[:, 6, :].rearrange("p (k s) -> p k s", k=KF), hhTs[0].bitcast(F32),
                                ALU.subtract).then_inc(hhT_done, 1)
                if nxt is not None:
                    for q in range(2, NQ):
                        expert_lo(nxt, q, b)
                dve.reg_add(blk, blk, 1)

            def expert_dve(e, nxt):
                n_more = dve.value_load(nb_i[0:1, bass.ds(e, 1)], min_val=0, max_val=NT - 1)
                with dve.If(n_more > 0):
                    with dve.Fori(0, n_more) as _j:
                        block_dve(None)
                block_dve(nxt)

            with dve.Fori(0, E - 1) as e:
                expert_dve(e, e + 1)
            expert_dve(E - 1, None)
            for i in range(NT + 1):
                if i < NT:
                    dve.wait_ge(yg_in[i], 32)
                    dve.wait_ge(x_in[i], 48)
                    link(v.scalar_tensor_tensor(x1[:, i, :], yg_t[i][0], r1["w1"][:, i:i + 1], x1[:, i, :],
                                                ALU.mult, ALU.add))
                    v.scalar_tensor_tensor(x1[:, i, :], yg_t[i][1], r1["w2"][:, i:i + 1], x1[:, i, :], ALU.mult,
                                           ALU.add).then_inc(moe_added, 1)
                if i:
                    k = i - 1
                    dve.wait_ge(fin_rs, i)
                    if k == 0:
                        dve.wait_ge(gfin_in, 16)
                    if k >= 2:
                        dve.wait_ge(out_stored[k % 2], 16 * (k // 2))
                    v.scalar_tensor_tensor(otile[k % 2], x1[:, k, :], rstd[:, k:k + 1], gfin, ALU.mult,
                                           ALU.mult).then_inc(out_made, 1)

        @block.tensor
        def _(pe):
            te = nc.tensor
            pe.wait_ge(vec_in, VEC_DMAS * 16)
            pe.wait_ge(const_made, 6)
            te.transpose(psum[:, 0, 0:NV], vec_rows[:], ident[0:NV, 0:NV]).then_inc(vec_tr, 1)

            def norm_transposes(j, src):
                pe.wait_ge(h_made, j + 1)
                if j >= 2:
                    pe.wait_ge(scaled, 2 * (j - 1))
                for k in range(KD):
                    last = te.transpose(psum[:, 4 + 2 * (j % 2) + k // HALF, (k % HALF) * P:(k % HALF + 1) * P],
                                        src[:, k * P:(k + 1) * P], ident[:])
                last.then_inc(h_trans, 1)

            def open_tile(n):
                if n >= RING:
                    wait_evac(pe, n - RING)
                return psum[:, n % RING, :]

            def product(o, lhs, rhs, n):
                for k in range(n):
                    te.matmul(o, lhs(0, k), rhs(0, k), start=(k == 0), stop=False)
                    te.matmul(o, lhs(0, k), rhs(1, k), start=False, stop=False)
                    last = te.matmul(o, lhs(1, k), rhs(0, k), start=False, stop=(k == n - 1))
                return last

            def T_piece(nm, c, xS, cols=BANK):
                p = PIDX[nm, c]
                w = wS[p % 2]
                pe.wait_ge(w_lo, p + 1)
                per = xS[0].shape[2] // cols
                in_bank = BANK // cols
                for i in range(2 * per // in_bank):
                    n = TIDX[nm, c, i]
                    o = open_tile(n)
                    for q in range(in_bank):
                        ch, part = (i * in_bank + q) // per, (i * in_bank + q) % per
                        last = product(o[:, q * cols:(q + 1) * cols],
                                       lambda z, k: w[z][:, k, ch * P:(ch + 1) * P],
                                       lambda z, k: xS[z][:, k, part * cols:(part + 1) * cols], KD)
                    last.then_inc(tile_out, 1)

            def N_piece(nm, c, xS):
                p = PIDX[nm, c]
                w = wS[p % 2]
                pe.wait_ge(w_lo, p + 1)
                for i in range(xS[0].shape[2] // (2 * P)):
                    n = TIDX[nm, c, i]
                    o = open_tile(n)
                    for q in range(2):
                        tk = 2 * i + q
                        last = product(o[:, q * PC:(q + 1) * PC], lambda z, k: xS[z][:, k, tk * P:(tk + 1) * P],
                                       lambda z, k: w[z][:, k, :], KD)
                    last.then_inc(tile_out, 1)

            for i in range(NT):
                norm_transposes(i, htmp[:, i % 2, :])
            pe.wait_ge(vecT_ready, 1)
            pe.wait_ge(pad_lo, 1)
            for hf in range(NH2):
                pe.wait_ge(hT_part, 2 * HALF * (hf + 1))
                o = open_tile(TIDX["gates", 0, hf])
                product(o[0:GW, :], lambda z, k: wpadS[z][:, k, :],
                        lambda z, k: hS[z][:, k, hf * BANK:(hf + 1) * BANK], KD).then_inc(tile_out, 1)
            for nm in ("mq", "mk"):
                for c in range(2):
                    T_piece(nm, c, hS)
            for c in range(2):
                N_piece("mv", c, hS)
            N_piece("mo", 0, hS)
            pe.wait_ge(gate_dve, 3)
            pe.wait_ge(gate_act, 5)
            for c in range(NT):
                te.transpose(psum[:, 4 + c // HALF, (c % HALF) * GC:(c % HALF + 1) * GC],
                             stack[0:GC, c * P:(c + 1) * P], ident[0:GC, 0:GC])
            for h in range(MH):
                last = te.matmul(psum[:, 6, h * NT:(h + 1) * NT], sel[:, h, :], wold[:], start=True, stop=True)
            last.then_inc(gate_pe, 1)
            N_piece("mo", 1, hS)

            wait_evac(pe, TIDX["mo", 1, NT // 2 - 1])
            pe.wait_ge(gate_dve, 4)
            pe.wait_ge(silu_done, 2 * MH)
            for c in range(NT):
                if c >= 2:
                    pe.wait_ge(kn_done, c - 1)
                for h in range(MH):
                    last = te.transpose(psum[:, 6 + c % 2, h * P:(h + 1) * P], mkT[:, h, c * P:(c + 1) * P], ident[:])
                last.then_inc(kn_ready, 1)

            def at_head(b, h):
                return psum[:, b + h // 2, (h % 2) * E1:(h % 2 + 1) * E1]

            def max_rows(c):
                if c:
                    pe.wait_ge(D_done, c)
                for h in range(MH):
                    last = te.matmul(psum[:, 0, h * P:(h + 1) * P], sel[:, h, :], mrow[:, c * P:(c + 1) * P],
                                     start=True, stop=True)
                last.then_inc(mb_ready, 1)

            def scores(c):
                if c:
                    pe.wait_ge(Pm_done, c)
                for h in range(MH):
                    last = te.matmul(psum[:, 1, h * P:(h + 1) * P], mkT[:, h, c * P:(c + 1) * P],
                                     mqT[:, h, c * P:(c + 1) * P], start=True, stop=True)
                last.then_inc(kq_ready, 1)

            max_rows(0)
            scores(0)
            pe.wait_ge(kn_done, NT)
            for c in range(NT):
                cs = slice(c * P, (c + 1) * P)
                if c < NT - 1:
                    pe.wait_ge(vs_done, c + 1)
                    if c:
                        pe.wait_ge(CT_done, c)
                    for h in range(MH):
                        last = te.matmul(at_head(6, h), kN[:, c, h * P:(h + 1) * P], vsb[c % 2][:, h, :],
                                         start=True, stop=True)
                    last.then_inc(U_ready, 1)
                    max_rows(c + 1)
                if c:
                    pe.wait_ge(CT_done, c)
                    pe.wait_ge(num_done, c)
                    for h in range(MH):
                        last = te.matmul(at_head(4, h), mqT[:, h, cs], CT[c % 2][:, h, :], start=True, stop=True)
                    last.then_inc(inter_ready, 1)
                pe.wait_ge(Pm_done, c + 1)
                if c:
                    pe.wait_ge(num_done, c)
                for h in range(MH):
                    last = te.matmul(at_head(2, h), Pm[c % 2][:, h * P:(h + 1) * P], vaug[:, c, h, :],
                                     start=True, stop=True)
                last.then_inc(num_ready, 1)
                if c < NT - 1:
                    scores(c + 1)

            for c in range(2):
                T_piece("sq", c, hS)
            for c in range(2):
                T_piece("sk", c, hS)
            for c in range(2):
                N_piece("sv", c, hS)
            for c in range(NT):
                pe.wait_ge(yn_done, c + 1)
                if c >= 2:
                    pe.wait_ge(ym_done, c - 1)
                for h in range(MH):
                    last = te.transpose(psum[:, 4 + c % 2, h * P:(h + 1) * P], gate_o[:, c, h * P:(h + 1) * P], ident[:])
                last.then_inc(yn_trans, 1)

            for i in range(4):
                wait_evac(pe, TIDX["sv", 1, i])
            wait_evac(pe, TIDX["sk", 1, 3])
            pe.wait_ge(ym_done, NT)
            for k in range(NS + 12):
                if k < NS:
                    s = steps[k]
                    lo = s["lo"]
                    if k >= 2:
                        pe.wait_ge(zs_done, k - 1)
                    te.matmul(psum[:, k % 2, lo:BANK], skT[:, s["h"], s["j"] * P:(s["j"] + 1) * P],
                              sqT[:, s["h"], s["hf"] * BANK + lo:(s["hf"] + 1) * BANK],
                              start=True, stop=True).then_inc(z_ready, 1)
                i = k - 2
                if 0 <= i < NS:
                    s = steps[i]
                    lo = s["lo"]
                    if s["diag"]:
                        pe.wait_ge(Lmasked, upto_diag(i))
                    pe.wait_ge(L_done, i + 1)
                    if i >= 2:
                        pe.wait_ge(ex_done, i - 1)
                    if not s["first"]:
                        pe.wait_ge(R_done, upto_R(i - 1))
                        te.matmul(psum[:, 2 + i % 2, lo:BANK], ones[:], Rb[i % NRB][:, lo:BANK], start=True, stop=False)
                    te.matmul(psum[:, 2 + i % 2, lo:BANK], uincl[:], Lb[i % NL][:, lo:BANK],
                              start=s["first"], stop=True).then_inc(tail_ready, 1)
                i = k - 4
                if 0 <= i < NS:
                    s = steps[i]
                    lo = s["lo"]
                    if s["first"] and s["g"] >= 2:
                        pe.wait_ge(o_made, s["g"] - 1)
                    pe.wait_ge(a_done, i + 1)
                    te.matmul(psum[:, 4 + s["g"] % 2, lo:BANK], svn[:, s["j"], s["h"] * DH:(s["h"] + 1) * DH],
                              ex[i % NX][:, lo:BANK], start=s["first"], stop=s["last"],
                              skip_group_check=True).then_inc(av_done, 1)
                i = k - 6
                if 0 <= i < NS and steps[i]["last"]:
                    gi = steps[i]["g"]
                    pe.wait_ge(osq_done, gi + 1)
                    if gi >= 2:
                        pe.wait_ge(ors_done, gi - 1)
                    te.matmul(psum[:, 6 + gi % 2, :], ones[:], osq, start=True, stop=True).then_inc(ossq_ready, 1)

            pe.wait_ge(sb_out, NGRP)
            N_piece("w_out", 0, hS)
            for i in range(MT):
                norm_transposes(NT + i, htmp[:, (NT + i) % 2, :])
            for c in range(1, 4):
                N_piece("w_out", c, hS)
            pe.wait_ge(hT_part, 2 * (NT + MT))
            for i in range(NT):
                if i < 4:
                    T_piece("w_mk", i, mS, MEM)
                else:
                    N_piece("w_mv", i - 4, mS)
                norm_transposes(NT + MT + i, htmp[:, (NT + MT + i) % 2, :])
            pe.wait_ge(hT_part, 2 * (2 * NT + MT))
            for c in range(4):
                T_piece("w_mq", c, hS)

            wait_evac(pe, TIDX["w_mq", 3, 3])
            JH = XD // P
            for k in range(NT + 1):
                if k < NT:
                    if k >= 2:
                        pe.wait_ge(pt_done, 2 * (k - 1))
                    for h in range(XH):
                        for j in range(JH):
                            last = te.matmul(psum[:, 4 + 2 * (k % 2) + h // 2, (h % 2) * MEM:(h % 2 + 1) * MEM],
                                             qT[:, JH * h + j, k * P:(k + 1) * P], kTm[:, JH * h + j, :],
                                             start=(j == 0), stop=(j == JH - 1))
                    last.then_inc(sc_ready, 1)
                if k >= 1:
                    i = k - 1
                    pe.wait_ge(pn_done, i + 1)
                    for q in range(2 * XH):
                        last = te.transpose(psum[:, 4 + 2 * (i % 2) + q // 4, (q % 4) * P:(q % 4 + 1) * P],
                                            pnat[:, i % 2, q * P:(q + 1) * P], ident[:])
                    last.then_inc(pt_ready, 1)
                    if i % HALF == HALF - 1:
                        hf = i // HALF
                        pe.wait_ge(pt_done, 2 * (i + 1))
                        for c in range(KD):
                            n = TIDX["oT", 0, hf * KD + c]
                            o = open_tile(n)
                            for m in range(MT):
                                last = te.matmul(o, vmem[:, m, c * P:(c + 1) * P], pT[:, MT * (c // JH) + m, :],
                                                 start=(m == 0), stop=(m == MT - 1))
                            last.then_inc(tile_out, 1)
            wait_evac(pe, TIDX["oT", 0, 2 * KD - 1])
            for c in range(4):
                N_piece("w_mo", c, hS)

            pe.wait_ge(pad_lo, 2)
            for i in range(NT):
                norm_transposes(2 * NT + MT + i, hn[:, i, :])
            wait_evac(pe, len(tiles) - 1)
            pe.wait_ge(hT_part, 2 * (3 * NT + MT))
            for hf in range(NH2):
                product(psum[0:100, hf, :], lambda z, k: rpadS[z][:, k, :],
                        lambda z, k: hS[z][:, k, hf * BANK:(hf + 1) * BANK], KD).then_inc(rt_pe, 1)
            for i in range(NT):
                pe.wait_ge(lgT_done, i // HALF + 1)
                last = te.transpose(psum[:, 2, i * NR:(i + 1) * NR], lgT[:, i * P:(i + 1) * P], ident[0:NR, 0:NR])
            last.then_inc(rt_pe, 1)
            pe.wait_ge(rt_dve, 3)
            Mf = re["M"].rearrange("p t g e -> p (t g e)")
            te.matmul(psum[:, 1, 0:NT * E], ustrict[:], Mf, start=True, stop=True)
            te.matmul(psum[:, 1, NT * E:2 * NT * E], ones[:], Mf, start=True, stop=True).then_inc(rt_pe, 1)
            pe.wait_ge(routed, 1)

            def x_transposes():
                for k in range(KD):
                    last = te.transpose(psum[:, 4 + k // HALF, (k % HALF) * P:(k % HALF + 1) * P],
                                        xb[:, k * P:(k + 1) * P], ident[:])
                last.then_inc(xt_ready, 1)

            pe.sem_inc(y_ready, 1)
            pe.wait_ge(xb_in, 16)
            x_transposes()
            blk = pe.alloc_register("pe_block")
            pe.reg_mov(blk, 0)

            def in_product(o, w, e, q0):
                for h in range(2):
                    pe.wait_ge(e_lo, e * NQ + (q0 + h + 1))
                    for k in range(h * (KD // 2), (h + 1) * (KD // 2)):
                        te.matmul(o, xTs[0][:, k, :], w[0][:, k, :], start=(k == 0), stop=False)
                        te.matmul(o, xTs[0][:, k, :], w[1][:, k, :], start=False, stop=False)
                        last = te.matmul(o, xTs[1][:, k, :], w[0][:, k, :], start=False, stop=(k == KD - 1))
                return last

            def out_part(c, z, zw, start=False, stop=False):
                for k in range(KF):
                    last = te.matmul(psum[:, 2 + c, :], hhTs[z][:, k, :], w2s[zw][:, k, c * BANK:(c + 1) * BANK],
                                     start=start and k == 0, stop=stop and k == KF - 1)
                return last

            def block_pe(e):
                b = pe.snap(blk, min_val=0, max_val=MAXB)
                pe.wait_ge(xT_done, b + 1)
                pe.wait_ge(sg_done, b + 1)
                in_product(psum[:, 0, :], w1s, e, 0).then_inc(a_ready, 1)
                pe.wait_ge(hh_done, b + 1)
                in_product(psum[:, 1, :], w3s, e, 2).then_inc(u_ready, 1)
                pe.wait_ge(xb_in, (b + 2) * 16)
                x_transposes()
                pe.wait_ge(hh_done, b + 2)
                for k in range(KF):
                    last = te.transpose(psum[:, 6, k * P:(k + 1) * P], hh[:, k * P:(k + 1) * P], ident[:])
                last.then_inc(ht_ready, 1)
                pe.wait_ge(e_lo, e * NQ + NQ)
                pe.wait_ge(hhT_hi, b + 1)
                pe.wait_ge(y_evac, b + 1)
                for c in range(2):
                    out_part(c, 0, 0, start=True)
                    out_part(c, 0, 1)
                pe.wait_ge(hhT_done, b + 1)
                for c in range(2):
                    last = out_part(c, 1, 0, stop=True)
                last.then_inc(y_ready, 1)
                pe.reg_add(blk, blk, 1)

            with pe.Fori(0, E) as e:
                n_more = pe.value_load(nb_i[0:1, bass.ds(e, 1)], min_val=0, max_val=NT - 1)
                with pe.Fori(0, n_more + 1) as _j:
                    block_pe(e)


def kernel(**inputs):
    import numpy as np
    import concourse.bacc as bacc
    from concourse.bass_utils import run_bass_kernel_spmd as run

    nc = bacc.Bacc("TRN2", target_bir_lowering=False, num_devices=1)
    arrays, t = {}, {}
    for name in sorted(inputs):
        arrays["in_" + name] = np.ascontiguousarray(inputs[name])
        t[name] = nc.dram_tensor("in_" + name, arrays["in_" + name].shape, F32, kind="ExternalInput").ap()
    shape = tuple(inputs["x"].shape)
    out = nc.dram_tensor("out", shape, F32, kind="ExternalOutput").ap()
    experts = inputs["w_e1"].shape[1] * inputs["w_e1"].shape[2]
    rows = ((2 * shape[1] + experts * (P - 1)) // P + 2) * P
    xg = nc.dram_tensor("token_blocks", (rows, shape[2]), F32).ap()
    hybrid_layer(nc, t, out, xg)
    return run(nc, [arrays], core_ids=[0]).results[0]["out"]
```

```python
from contextlib import ExitStack

import concourse.bass as bass
from concourse import mybir

ALU = mybir.AluOpType
ACT = mybir.ActivationFunctionType
AX = mybir.AxisListType
F32 = mybir.dt.float32
F32R = mybir.dt.float32r
I32 = mybir.dt.int32

P = 128
BANK = 512
EPS = 1e-6
NEG = -1.0e30


def hybrid_layer(nc, t, out):
    SEQ, D = t["x"].shape[1:]
    MEM = t["mem"].shape[1]
    NT = SEQ // P
    KD = D // P
    MT = MEM // P
    MH = t["i_bias"].shape[1]
    DH = P
    MW = MH * DH
    CW = t["conv_w"].shape[1]
    XH = 4
    XD = D // XH
    NG = t["w_e1"].shape[1]
    NE = t["w_e1"].shape[2]
    E = NG * NE
    F = t["w_e1"].shape[4]
    KF = F // P
    HALF = BANK // P
    NH2 = SEQ // BANK
    QSCALE = float(DH) ** -0.5
    XSCALE = float(XD) ** -0.5
    NR = NG + E
    MAXB = (2 * SEQ + E * (P - 1)) // P
    SLOT_BLOCKS = MAXB + 2
    assert MW == BANK and F == BANK and D == 2 * BANK and MH == 4

    x_d = t["x"][0].rearrange("(t p) d -> t p d", p=P)
    mem_d = t["mem"][0].rearrange("(t p) d -> t p d", p=P)
    SLOTS = SLOT_BLOCKS * P
    h_d = nc.dram_tensor("normed_rows", (SEQ, D), F32).ap()
    slot_d = nc.dram_tensor("slot_table", (SLOTS, 2), I32).ap()
    y_d = nc.dram_tensor("expert_rows", (2 * SEQ + SLOTS, D), F32).ap()
    x1_d = nc.dram_tensor("x1_rows", (SEQ, D), F32).ap().rearrange("(t p) d -> t p d", p=P)
    out_d = out[0].rearrange("(t p) d -> t p d", p=P)

    PC = BANK // 2
    W_IN = t["w_in"][0]
    OFF = dict(mq=0, mk=MW, mv=2 * MW, mo=3 * MW, gates=4 * MW, sq=4 * MW + 2 * MH,
               sk=5 * MW + 2 * MH, sv=6 * MW + 2 * MH)

    def piece_d(name, c0):
        return t[name][0][:, c0:c0 + PC].rearrange("(k p) n -> p k n", p=P)

    pieces = []
    for nm, who in (("mq", "act"), ("mk", "act"), ("mv", "act"), ("mo", "act"), ("sq", "act"),
                    ("sk", "dve"), ("sv", "act")):
        for c in range(2):
            pieces.append((nm, c, piece_d("w_in", OFF[nm] + c * PC), 4, who))
    for nm, n, who in (("w_out", 4, "dve"), ("w_mk", 1, "act"), ("w_mv", 1, "act"), ("w_mq", 4, "act"),
                       ("w_mo", 4, "dve")):
        for c in range(4):
            pieces.append((nm, c, piece_d(nm, c * PC), n, who))
    PIDX = {(x[0], x[1]): i for i, x in enumerate(pieces)}
    NP = len(pieces)

    tiles = [("gates", 0, i, "dve") for i in range(NH2)]
    for nm, c, _, n, who in pieces:
        if (nm, c) == ("w_mo", 0):
            tiles += [("oT", 0, i, "dve") for i in range(2 * KD)]
        if (nm, c) == ("w_mo", 2):
            tiles += [(nm, c + q, i, who) for i in range(n) for q in range(2)]
        elif (nm, c) != ("w_mo", 3):
            tiles += [(nm, c, i, who) for i in range(n)]
    tiles[1], tiles[2] = tiles[2], tiles[1]
    TIDX = {(n, c, i): k for k, (n, c, i, _) in enumerate(tiles)}
    evac_no = []
    seen = {"act": 0, "dve": 0}
    for *_, w in tiles:
        seen[w] += 1
        evac_no.append((w, seen[w]))
    RING = 4

    def piece_end(p):
        nm, c, _, n, _ = pieces[p]
        return TIDX[nm, c, n - 1] + 1

    with ExitStack() as ctx:
        def sb(name, shape, dt=F32):
            return ctx.enter_context(nc.sbuf_tensor(name, shape, dt))

        def sem(name):
            return ctx.enter_context(nc.semaphore(name))

        KB = 256
        fence_base = nc.sbuf_base
        sb("fence", [P, 178 * KB + 128])
        base = -(-fence_base // 32) * 32

        def region(name, at, words, dt=F32):
            return nc.alloc_sbuf_tensor_at(name, [P, words], dt, offset=base + 4 * at)

        RS = 64 * KB
        arena = region("arena", 0, 178 * KB + 128)
        act_split = region("act_split", 0, 64 * KB, F32R)
        RW = RS + 74 * KB + 128
        w_split = region("w_split", RW, 32 * KB, F32R)
        raws = [arena[:, at:at + 8 * KB].rearrange("p (k n) -> p k n", k=KD) for at in (RW + 32 * KB, RS + 56 * KB)]
        raw_no = [int(p % 2 == 1 and PIDX["w_mk", 0] <= p <= PIDX["w_mq", 1]) for p in range(NP)]

        def hi_lo(tensor, at, a, b):
            return [tensor[:, at + i * a * b:at + (i + 1) * a * b].rearrange("p (a b) -> p a b", a=a) for i in range(2)]

        def view(at, *shape):
            n = 1
            for q in shape:
                n *= q
            v = arena[:, at:at + n]
            if len(shape) == 2:
                v = v.rearrange("p (a b) -> p a b", a=shape[0])
            return v

        hS = hi_lo(act_split, 0, KD, SEQ)
        wS = [hi_lo(w_split, i * 16 * KB, KD, PC) for i in range(2)]
        RP = RS
        mqT = view(RP, MH, SEQ)
        mkT = view(RP + 16 * KB, MH, SEQ)
        vaug = arena[:, RP + 32 * KB:RP + 32 * KB + NT * MH * 129].rearrange(
            "p (t h e) -> p t h e", t=NT, h=MH)
        gate_o = view(RP + 49 * KB, NT, MW)
        sqT = view(RP, MH, SEQ)
        skT = view(RP + 16 * KB, MH, SEQ)
        svn = view(RP + 32 * KB, NT, MW)
        kN = view(RW + 16 * KB, NT, MW)
        xs = view(RP, NT, D)
        x1 = view(RP, NT, D)
        qT = view(RP + 32 * KB, KD, SEQ)
        kTm = view(RP + 64 * KB, KD, MEM)
        mS = hi_lo(region("mem_split", RP + 32 * KB, 16 * KB, F32R), 0, KD, MEM)
        mems = view(RP + 48 * KB, MT, D)
        pT = view(RW + 16 * KB, 2 * XH, BANK)

        consts = {n: sb(n, [P, P]) for n in ("ident", "uincl", "ustrict", "ones")}
        ident, uincl, ustrict, ones = (consts[n] for n in ("ident", "uincl", "ustrict", "ones"))
        sel = sb("sel", [MH, MH, P])
        NV = 4 * KD + CW * 2 * MH + 2 * MH + MH
        vec_rows = sb("vec_rows", [NV, P])
        vecT = sb("vecT", [P, NV])
        GW = 3 * 32 + MH
        gbias = sb("gbias", [GW, 1])
        rbias = sb("rbias", [NR, 1])
        mlg = sb("mlg", [P, MW])
        sq_mix, sq_kv, sq_mem = view(RP + 32 * KB, D), view(RP + 64 * KB, D), view(RP + 48 * KB, D)
        wpad = view(RW + 16 * KB, KD, GW)
        wpadS = hi_lo(region("wpad_split", RW + 20 * KB, 8 * KB, F32R), 0, KD, GW)
        eps_col = sb("eps_col", [P, 1])
        ss = sb("ss", [P, NT])
        rstd = sb("rstd", [P, NT])
        lnt = sb("lnt", [P, NT])
        work = sb("work", [P, 20 * KB])
        htmp = work[:, 0:2 * D].rearrange("p (b d) -> p b d", b=2)
        pnat = htmp
        tt = [work[:, 2 * D + i * BANK:2 * D + (i + 1) * BANK] for i in range(2)]
        vmem = work[:, 3 * D:5 * D].rearrange("p (m d) -> p m d", m=MT)
        cin = work[:, 2 * D:2 * D + 2 * (SEQ + 4)].rearrange("p (b s) -> p b s", b=2)
        psum = ctx.enter_context(nc.psum_tensor("psum", [P, 8, BANK], F32))

        stack = work[:, 0:SEQ]
        R_G, R_F, R_L, R_K, R_M = range(5)
        grow = [work[0:MH, i * SEQ:(i + 1) * SEQ] for i in range(5)]
        mrow = grow[R_M]
        GC = GW
        cols = work[:, SEQ:SEQ + NT * GC].rearrange("p (c g) -> p c g", c=NT)
        gcol, wicol, flcol, wscol = (cols[:, :, 32 * i:32 * i + MH] for i in range(4))
        woldB = work[:, SEQ + NT * GC:SEQ + NT * GC + NT * MH].rearrange("p (h c) -> p h c", h=MH)
        mprev = sb("mprev", [MH, NT])
        wold = sb("wold", [MH, NT])
        S0 = RW
        NZ, NLT, NL, NX, NRB = 4, 2, 3, 4, 3
        bufs = [view(S0 + i * BANK, BANK) for i in range(16)] + [work[:, i * BANK:(i + 1) * BANK] for i in range(4)]
        zs, bufs = bufs[:NZ], bufs[NZ:]
        lt, bufs = bufs[:NLT], bufs[NLT:]
        Lb, bufs = bufs[:NL], bufs[NL:]
        ex, bufs = bufs[:NX], bufs[NX:]
        Rb, bufs = bufs[:NRB], bufs[NRB:]
        osq, ors, of = bufs[:3]
        E1 = DH + 1
        Dm = [view(S0 + i * BANK, BANK) for i in range(2)]
        Pm = [view(S0 + (2 + i) * BANK, BANK) for i in range(2)]
        vsb = [view(S0 + 4 * BANK + i * MH * E1, MH, E1) for i in range(2)]
        inter = view(S0 + 4 * BANK + 2 * MH * E1, MH, E1)
        wk = SEQ + NT * GC + NT * MH
        CT = [work[:, wk + i * MH * E1:wk + (i + 1) * MH * E1].rearrange("p (h e) -> p h e", h=MH) for i in range(2)]
        wk += 2 * MH * E1
        junk = work[:, wk:wk + DH]
        wk += DH
        assert wk <= 4 * SEQ
        mss = sb("mss", [P, NT * MH])
        mden = sb("mden", [P, NT, MH])
        mfac = sb("mfac", [P, NT, MH])

        G_MIX, G_KV, G_MEM, G_FFN = 0, KD, 2 * KD, 3 * KD
        V_CW = 4 * KD
        V_CB = V_CW + CW * 2 * MH
        V_SBG = V_CB + 2 * MH

        vec_in, bias_in = sem("vec_in"), sem("bias_in")
        VECS = [src.rearrange("(k p) -> k p", p=P) for src in
                (t["ln_mix"][0], t["ln_memkv"][0], t["ln_mem"][0], t["ln_ffn"][0],
                 t["conv_w"][0].rearrange("w c -> (w c)"), t["conv_b"][0], t["sb_head_g"][0])]
        N_BIAS = 5
        x_in = [sem(f"x_in{i}") for i in range(NT)]
        mem_in = sem("mem_in")
        raw_in = [sem("raw_in0"), sem("raw_in1")]
        w_hi, w_lo, rs_done = sem("w_hi"), sem("w_lo"), sem("rs_done")
        pad_hi, pad_lo = sem("pad_hi"), sem("pad_lo")
        scaled, hi_part, ym_hi, o_made, o_hi, oT_hi = (
            sem(n) for n in ("scaled", "hi_part", "ym_hi", "o_made", "o_hi", "oT_hi"))
        const_made = sem("const_made")
        pool_chain = sem("pool_chain")
        dve_chain = sem("dve_chain")
        act_chain = sem("act_chain")
        vec_tr = sem("vec_tr")
        vecT_ready = sem("vecT_ready")
        h_made = sem("h_made")
        h_trans = sem("h_trans")
        hT_part = sem("hT_part")
        tile_out = sem("tile_out")
        evac = {"act": sem("evac_act"), "dve": sem("evac_dve")}
        conv_done = sem("conv_done")
        silu_done = sem("silu_done")
        gate_pe = sem("gate_pe")
        gate_dve = sem("gate_dve")
        gate_act = sem("gate_act")
        z_ready, zs_done, ab_done, l1_done, L_done = (sem(n) for n in ("z_ready", "zs_done", "ab_done", "l1_done", "L_done"))
        Lmasked, R_done, tail_ready, ex_done, ex_masked = (
            sem(n) for n in ("Lmasked", "R_done", "tail_ready", "ex_done", "ex_masked"))
        a_done, av_done, osq_done, ossq_ready, ors_done, sb_out = (
            sem(n) for n in ("a_done", "av_done", "osq_done", "ossq_ready", "ors_done", "sb_out"))
        kn_ready, kn_done = sem("kn_ready"), sem("kn_done")
        mb_ready, kq_ready, D_done, D_masked, W_done, Pm_done = (
            sem(n) for n in ("mb_ready", "kq_ready", "D_done", "D_masked", "W_done", "Pm_done"))
        vs_done, num_ready, inter_ready, U_ready, inter_done, num_done, CT_done = (
            sem(n) for n in ("vs_done", "num_ready", "inter_ready", "U_ready", "inter_done", "num_done", "CT_done"))
        mss_done, ml_fac, ml_rs, yn_done, yn_trans, ym_done = (
            sem(n) for n in ("mss_done", "ml_fac", "ml_rs", "yn_done", "yn_trans", "ym_done"))
        gate_scaled = sem("gate_scaled")
        wpad_in, lgT_done = sem("wpad_in"), sem("lgT_done")
        sc_ready, mx_done, p_done, pn_done, pt_ready, pt_done = (
            sem(n) for n in ("sc_ready", "mx_done", "p_done", "pn_done", "pt_ready", "pt_done"))
        hn = view(RP + 32 * KB, NT, D)
        JF = 2 * NT + MT

        def hS_at(at):
            return hi_lo(act_split, at, KD, F)

        w1s, w3s = hS_at(0), hS_at(32 * KB)
        w2s = hi_lo(region("w2_split", RP + 32 * KB, 32 * KB, F32R), 0, KF, D)
        NQ = 6
        raw_a = region("expert_raw_a", RP + 96 * KB, 16 * KB)
        raw_b = region("expert_raw_b", RP, 32 * KB)
        eraw = [w[:, i * 8 * KB:(i + 1) * 8 * KB] for w, n in ((raw_a, 2), (raw_b, 4)) for i in range(n)]
        eparts = [[w[z][:, KD // 2 * q:KD // 2 * (q + 1), :] for z in range(2)] for w in (w1s, w3s) for q in range(2)]
        eparts += [[w2s[z][:, KF // 2 * q:KF // 2 * (q + 1), :] for z in range(2)] for q in range(2)]
        eraw = [r.rearrange("p (k n) -> p k n", k=e[0].shape[1]) for r, e in zip(eraw, eparts)]
        RB = RP + 64 * KB
        xb = view(RB, D)
        xTs = hi_lo(region("xT_split", RB + 4 * KB, 8 * KB, F32R), 0, KD, P)
        yb = view(RB + 12 * KB, D)
        sg = view(RB + 16 * KB, F)
        hh = view(RB + 18 * KB, F)
        hhTs = hi_lo(region("hhT_split", RB + 20 * KB, 4 * KB, F32R), 0, KF, P)
        gffn = work[:, 4 * D:5 * D]
        yg_t = [[view(4 * (2 * i + c) * KB, D) for c in range(2)] for i in range(NT)]
        gfin = work[:, 4 * D:5 * D]
        otile = [view(RP + (64 + 4 * i) * KB, D) for i in range(NT)]
        sq_out = view(RP + 96 * KB, D)
        rpad = work[:, 2 * D:2 * D + KD * 100].rearrange("p (k r) -> p k r", k=KD)
        rpadS = hi_lo(region("rpad_split", RP + 64 * KB, 8 * KB, F32R), 0, KD, 100)
        lgT = work[0:NR, 3 * D:4 * D]
        carve = {"at": 0}

        def small(*shape):
            n = 1
            for q in shape:
                n *= q
            w = work[:, carve["at"]:carve["at"] + n]
            carve["at"] += n
            names = "abc"[:len(shape)]
            if len(shape) == 1:
                return w
            return w.rearrange("p (%s) -> p %s" % (" ".join(names), " ".join(names)),
                               **{k: q for k, q in zip(names, shape)})

        lg = small(NT, NR)
        elt = lg[:, :, NG:NR].rearrange("p t (g e) -> p t g e", g=NG)
        r4 = {n: small(NT, 4) for n in ("oh", "eq", "es", "t1", "t2", "tmp")}
        r1 = {n: small(NT) for n in ("mx", "left", "psel", "m1", "m2", "w1", "w2", "pos")}
        re = {n: small(NT, NG, NE) for n in ("A1", "A2", "M", "pos")}
        rc = {n: small(E) for n in ("nb", "cum", "one", "base")}
        tile_cnt, run_cnt, cont, over, full = (small(E, NT) for _ in range(5))
        assert carve["at"] <= 2 * D
        slot_init = sb("slot_init", [P, SLOT_BLOCKS, 2], I32)
        slot_of = sb("slot_of", [P, SLOT_BLOCKS, 2], I32)
        token_ids = sb("token_ids", [P, NT, 2, 2], I32)
        rows = sb("rows", [P, 2], I32)
        pmx = sb("pmx", [P, NT, XH])
        psm = sb("psm", [P, NT, XH])
        idx = sb("idx", [P, 2, NT], I32)
        nb_i = sb("nb_i", [1, E], I32)
        cum_i = sb("cum_i", [1, E], I32)
        routed, rt_pe, rt_dve, rt_act = (sem(n) for n in ("routed", "rt_pe", "rt_dve", "rt_act"))
        ids_made, table_init, table_set, table_in, h_stored, rows_ready, step = (
            sem(n) for n in ("ids_made", "table_init", "table_set", "table_in", "h_stored", "rows_ready", "step"))
        moe_in = [sem(f"moe_in{q}") for q in range(NQ)]
        e_hi, e_lo, xT_hi, hhT_hi, spilled, gffn_in, hn_scaled = (
            sem(n) for n in ("e_hi", "e_lo", "xT_hi", "hhT_hi", "spilled", "gffn_in", "hn_scaled"))
        xb_in, xt_ready, xT_done, a_ready, u_ready, sg_done, hh_done = (
            sem(n) for n in ("xb_in", "xt_ready", "xT_done", "a_ready", "u_ready", "sg_done", "hh_done"))
        ht_ready, hhT_done, y_ready, y_evac, y_stored = (
            sem(n) for n in ("ht_ready", "hhT_done", "y_ready", "y_evac", "y_stored"))
        gfin_in, moe_added, fin_rs, out_made = (
            sem(n) for n in ("gfin_in", "moe_added", "fin_rs", "out_made"))
        yg_in = [sem(f"yg_in{i}") for i in range(NT)]
        out_stored = sem("out_stored")


        steps = []
        for h in range(MH):
            for hf in range(NH2):
                top = HALF * (hf + 1)
                for j in range(top - 1, -1, -1):
                    lo = max(0, j * P - hf * BANK)
                    steps.append(dict(h=h, hf=hf, j=j, lo=lo, w=BANK - lo, first=(j == top - 1), last=(j == 0),
                                      diag=(j >= HALF * hf), g=h * NH2 + hf))
        NS = len(steps)

        def upto_diag(i):
            return sum(s["diag"] for s in steps[:i + 1])

        def upto_R(i):
            return sum(not s["last"] for s in steps[:i + 1])

        NGRP = MH * NH2

        def wait_evac(eng, n):
            w, c = evac_no[n]
            eng.wait_ge(evac[w], c)

        def wait_raw(eng, p):
            eng.wait_ge(raw_in[raw_no[p]], 16 * (raw_no[:p + 1].count(raw_no[p])))

        LATE = {PIDX["sq", 0], PIDX["w_out", 0]}

        def buffer_free(eng, p):
            if p >= 2:
                eng.wait_ge(tile_out, piece_end(p - 2))
            if p == 1:
                eng.wait_ge(tile_out, TIDX["gates", 0, NH2 - 1] + 1)
            if p in (PIDX["sq", 0], PIDX["sq", 1]):
                eng.wait_ge(num_ready, NT)
                eng.wait_ge(num_done, NT)
            if p in (PIDX["w_out", 0], PIDX["w_out", 1]):
                eng.wait_ge(av_done, NS)
            if p == PIDX["w_mo", 1]:
                eng.wait_ge(tile_out, TIDX["oT", 0, 2 * KD - 1] + 1)

        block = ctx.enter_context(nc.Block())

        @block.sync
        def _(sp):
            def load_raw(p):
                former = [q for q in range(p) if raw_no[q] == raw_no[p]]
                if former:
                    sp.wait_ge(w_lo, former[-1] + 1)
                sp.dma_start(raws[raw_no[p]], pieces[p][2]).then_inc(raw_in[raw_no[p]], 16)

            for i in range(NT):
                sp.dma_start(xs[:, i, :], x_d[i]).then_inc(x_in[i], 16)
                if i == 1:
                    at = 0
                    for src in VECS:
                        n = src.shape[0]
                        sp.dma_start(vec_rows[at:at + n, :], src).then_inc(vec_in, 16)
                        at += n
                if i == 4:
                    load_raw(0)
            load_raw(1)
            sp.wait_ge(ids_made, 4)
            sp.dma_start(slot_d.rearrange("(p b) c -> p (b c)", p=P),
                         slot_init[:].rearrange("p b c -> p (b c)")).then_inc(table_init, 16)
            for p in range(2, PIDX["w_out", 0] + 1):
                load_raw(p)
            sp.wait_ge(w_lo, PIDX["w_out", 0])
            sp.wait_ge(z_ready, NS)
            sp.wait_ge(yn_trans, NT)
            for i in range(NT):
                sp.dma_start(x1[:, i, :], x_d[i]).then_inc(x_in[i], 16)
            for i in range(MT):
                sp.dma_start(mems[:, i, :], mem_d[i]).then_inc(mem_in, 16)
            for p in range(PIDX["w_out", 0] + 1, NP):
                load_raw(p)
            for i in range(NT):
                wait_evac(sp, TIDX["w_mo", 3, i // 2])
                sp.dma_start(x1_d[i], x1[:, i, :]).then_inc(spilled, 16)

            def load_piece(e, q):
                w = t[("w_e1", "w_e3", "w_e2")[q // 2]][0].rearrange("g e d f -> (g e) d f")[bass.ds(e, 1)]
                src = w.rearrange("g (h k p) n -> h p (g k) n", h=2, p=P)[q % 2]
                sp.dma_start(eraw[q], src).then_inc(moe_in[q], 16)

            sp.wait_ge(tile_out, len(tiles))
            sp.wait_ge(w_lo, NP)
            for q in range(NQ):
                if q == 2:
                    sp.wait_ge(h_made, 3 * NT + MT)
                    sp.wait_ge(spilled, 16 * NT)
                    h_rows = h_d.rearrange("(t p) d -> t p d", p=P)
                    for i in range(NT):
                        sp.wait_ge(hn_scaled, i + 1)
                        sp.dma_start(h_rows[i], hn[:, i, :]).then_inc(h_stored, 16)
                load_piece(0, q)
            with sp.Fori(0, E - 1) as e:
                for q in range(NQ):
                    sp.wait_ge(e_lo, e * NQ + q + 1)
                    load_piece(e + 1, q)
            sp.wait_ge(hn_scaled, NT)
            sp.dma_start(gfin, t["ln_final"].rearrange("(a d) -> a d", a=1).broadcast_to([P, D])).then_inc(gfin_in, 16)
            sp.wait_ge(e_lo, E * NQ)
            for i in range(NT):
                sp.dma_start(x1[:, i, :], x1_d[i]).then_inc(x_in[i], 16)
            sp.wait_ge(table_set, 16 * 2 * NT)
            tot = sp.value_load(cum_i[0:1, E - 1:E], min_val=1, max_val=MAXB)
            sp.wait_ge(y_stored, (tot + 1) * 16)
            for i in range(NT):
                for c in range(2):
                    at = c * SEQ + i * P
                    sp.dma_start(yg_t[i][c], y_d[at:at + P, :]).then_inc(yg_in[i], 16)
            for i in range(NT):
                sp.wait_ge(out_made, i + 1)
                sp.dma_start(out_d[i], otile[i]).then_inc(out_stored, 16)
            sp.wait_ge(out_stored, 16 * NT)

        @block.gpsimd
        def _(pool):
            chain = [0]

            def link(ins):
                chain[0] += 1
                ins.then_inc(pool_chain, 1)
                pool.wait_ge(pool_chain, chain[0])

            g = nc.gpsimd
            g.memset(wpad, 0.0).then_inc(pool_chain, 1)
            g.memset(ident[:], 0.0).then_inc(pool_chain, 1)
            g.memset(uincl[:], 1.0).then_inc(pool_chain, 1)
            g.memset(ustrict[:], 1.0).then_inc(pool_chain, 1)
            g.memset(sel[:], 0.0).then_inc(pool_chain, 1)
            chain[0] = 5
            g.memset(ones[:], 1.0).then_inc(const_made, 1)
            g.memset(eps_col[:], EPS).then_inc(const_made, 1)
            pool.wait_ge(pool_chain, 5)
            for c in range(2):
                pool.dma_start(wpad[:, :, 32 * c:32 * c + MH], W_IN[:, OFF["gates"] + c * MH:OFF["gates"] + (c + 1) * MH]
                               .rearrange("(k p) n -> p k n", p=P)).then_inc(wpad_in, 16)
            g.affine_select(out=ident[:], in_=ident[:], compare_op=ALU.not_equal, fill=1.0, base=0,
                            pattern=[[-1, P]], channel_multiplier=1).then_inc(const_made, 1)
            g.affine_select(out=uincl[:], in_=uincl[:], compare_op=ALU.is_ge, fill=0.0, base=0,
                            pattern=[[-1, P]], channel_multiplier=1).then_inc(const_made, 1)
            g.affine_select(out=ustrict[:], in_=ustrict[:], compare_op=ALU.is_gt, fill=0.0, base=0,
                            pattern=[[1, P]], channel_multiplier=-1).then_inc(const_made, 1)
            g.affine_select(out=sel[:], in_=sel[:], compare_op=ALU.not_equal, fill=1.0, base=0,
                            pattern=[[-1, MH], [0, P]], channel_multiplier=1).then_inc(const_made, 1)
            g.memset(slot_init[:, :, 0], 0).then_inc(ids_made, 1)
            g.iota(slot_init[:, :, 1], pattern=[[1, SLOT_BLOCKS]], base=2 * SEQ,
                   channel_multiplier=SLOT_BLOCKS).then_inc(ids_made, 1)
            g.iota(token_ids[:, :, :, 0], pattern=[[P, NT], [0, 2]], base=0, channel_multiplier=1).then_inc(ids_made, 1)
            g.iota(token_ids[:, :, :, 1], pattern=[[P, NT], [SEQ, 2]], base=0, channel_multiplier=1).then_inc(ids_made, 1)
            for dst, src in ((gbias[0:MH, :], t["i_bias"].rearrange("a h -> h a")),
                             (gbias[32:32 + MH, :], t["f_bias"].rearrange("a h -> h a")),
                             (rbias[0:NG, :], t["b_rg"].rearrange("a h -> h a")),
                             (rbias[NG:NR, :], t["b_re"].rearrange("a h -> h a")),
                             (mlg[:], t["ml_head_g"].broadcast_to([P, MW]))):
                pool.dma_start(dst, src).then_inc(bias_in, 16)

            pool.wait_ge(bias_in, 16 * N_BIAS)
            for i in range(NT):
                wait_evac(pool, TIDX["mo", 1, i // 2])
                g.tensor_tensor(gate_o[:, i, :], gate_o[:, i, :], mlg[:], ALU.mult).then_inc(gate_scaled, 1)

            for c in range(NT):
                pool.wait_ge(D_done, c + 1)
                v4 = Dm[c % 2].rearrange("p (h s) -> p h s", h=MH)
                g.affine_select(out=v4, in_=v4, compare_op=ALU.is_ge, fill=-NEG, base=0,
                                pattern=[[0, MH], [1, P]], channel_multiplier=-1).then_inc(D_masked, 1)

            for k in range(NS + 3):
                i = k - 1
                if 0 <= i < NS:
                    s = steps[i]
                    lo = s["lo"]
                    L, R, Rn = Lb[i % NL], Rb[i % NRB], Rb[(i + 1) % NRB]
                    pool.wait_ge(L_done, i + 1)
                    if s["diag"]:
                        g.affine_select(out=L[:, lo:lo + P], in_=L[:, lo:lo + P], compare_op=ALU.is_gt,
                                        fill=0.0, base=0, pattern=[[1, P]], channel_multiplier=-1).then_inc(Lmasked, 1)
                        pool.wait_ge(Lmasked, upto_diag(i))
                    if not s["last"]:
                        if i >= 2:
                            pool.wait_ge(tail_ready, i - 1)
                        if i and upto_R(i - 1):
                            pool.wait_ge(R_done, upto_R(i - 1))
                        if lo:
                            link(g.memset(Rn[:, 0:lo], 0.0))
                        if s["first"]:
                            g.tensor_copy(Rn[:, lo:BANK], L[:, lo:BANK]).then_inc(R_done, 1)
                        else:
                            g.tensor_tensor(Rn[:, lo:BANK], R[:, lo:BANK], L[:, lo:BANK], ALU.add).then_inc(R_done, 1)
                i = k - 2
                if 0 <= i < NS and steps[i]["diag"]:
                    lo = steps[i]["lo"]
                    e = ex[i % NX][:, lo:lo + P]
                    pool.wait_ge(ex_done, i + 1)
                    g.affine_select(out=e, in_=e, compare_op=ALU.is_gt, fill=NEG, base=0, pattern=[[1, P]],
                                    channel_multiplier=-1).then_inc(ex_masked, 1)

            pool.wait_ge(tile_out, piece_end(PIDX["w_mq", 3]))
            link(g.memset(rpad, 0.0))
            pool.dma_start(rpad[:, :, 0:NG], t["w_rg"][0].rearrange("(k p) n -> p k n", p=P)).then_inc(wpad_in, 16)
            pool.dma_start(rpad[:, :, NG:NR], t["w_re"][0].rearrange("(k p) n -> p k n", p=P)).then_inc(wpad_in, 16)

            pool.wait_ge(tile_out, TIDX["oT", 0, 2 * KD - 1] + 1)
            pool.dma_start(gffn, t["ln_ffn"].broadcast_to([P, D])).then_inc(gffn_in, 16)
            pool.wait_ge(gffn_in, 16)
            for i in range(NT):
                pool.wait_ge(h_trans, 2 * NT + MT + i + 1)
                g.tensor_tensor(hn[:, i, :], hn[:, i, :], gffn, ALU.mult).then_inc(hn_scaled, 1)

            pool.wait_ge(ids_made, 4)
            pool.wait_ge(table_init, 16)
            pool.wait_ge(routed, 1)
            for i in range(NT):
                for c in range(2):
                    g.indirect_dma_start(out=slot_d, out_offset=bass.IndirectOffsetOnAxis(ap=idx[:, c, i:i + 1], axis=0),
                                         in_=token_ids[:, i, c, :], in_offset=None).then_inc(table_set, 16)
            pool.wait_ge(table_set, 16 * 2 * NT)
            table = slot_d.rearrange("(b p) c -> p b c", p=P)
            pool.dma_start(slot_of[:, 0:1, :], table[:, 0:1, :]).then_inc(table_in, 16)
            pool.wait_ge(table_in, 16)
            pool.wait_ge(h_stored, 16 * NT)

            def rows_of(c, b, n):
                g.tensor_copy(rows[:, c:c + 1], slot_of[:, bass.ds(b, 1), c]).then_inc(rows_ready, 1)
                pool.wait_ge(rows_ready, n)
                pool.sem_inc(step, 1)
                pool.wait_ge(step, 1)

            def load_tokens():
                g.indirect_dma_start(out=xb, out_offset=None, in_=h_d,
                                     in_offset=bass.IndirectOffsetOnAxis(ap=rows[:, 0:1], axis=0)).then_inc(xb_in, 16)

            for b in range(2):
                if b:
                    pool.wait_ge(xt_ready, 1)
                rows_of(0, b, b + 1)
                load_tokens()
                if b == 0:
                    pool.dma_start(slot_of[:, 1:, :], table[:, 1:, :]).then_inc(y_stored, 16)
                    pool.wait_ge(y_stored, 16)
            tot = pool.value_load(cum_i[0:1, E - 1:E], min_val=1, max_val=MAXB)
            with pool.Fori(0, tot) as b:
                pool.wait_ge(xt_ready, b + 2)
                rows_of(0, b + 2, b * 2 + 3)
                load_tokens()
                pool.wait_ge(y_evac, b + 2)
                rows_of(1, b, b * 2 + 4)
                g.indirect_dma_start(out=y_d, out_offset=bass.IndirectOffsetOnAxis(ap=rows[:, 1:2], axis=0),
                                     in_=yb, in_offset=None).then_inc(y_stored, 16)

        @block.scalar
        def _(act):
            chain = [0]
            a = nc.scalar.activation

            def link(ins):
                chain[0] += 1
                ins.then_inc(act_chain, 1)
                act.wait_ge(act_chain, chain[0])

            def split_hi(p):
                wait_raw(act, p)
                buffer_free(act, p)
                a(wS[p % 2][0], raws[raw_no[p]], ACT.Copy).then_inc(w_hi, 1)

            def begin_piece(p):
                if p + 1 < NP and p + 1 not in LATE:
                    split_hi(p + 1)

            def out_of(n):
                act.wait_ge(tile_out, n + 1)
                return psum[:, n % RING, :]

            def norm_rstd(i, src, squares):
                link(a(squares, src[:, i, :], ACT.Square, accum_out=ss[:, i:i + 1]))
                link(a(lnt[:, i:i + 1], ss[:, i:i + 1], ACT.Ln, bias=eps_col[:], scale=1.0 / D))
                a(rstd[:, i:i + 1], lnt[:, i:i + 1], ACT.Exp, scale=-0.5).then_inc(rs_done, 1)

            def norm_hi(j, i, dst):
                for q in range(2):
                    act.wait_ge(scaled, 2 * j + q + 1)
                    a(dst[0][:, HALF * q:HALF * (q + 1), i * P:(i + 1) * P],
                      tt[q].rearrange("p (k s) -> p k s", k=HALF), ACT.Copy).then_inc(hi_part, 1)

            nc.scalar.preload_act_table_set("natural_log_exp_and_others")
            act.wait_ge(const_made, 2)
            for i in range(NT + 2):
                if i < NT:
                    act.wait_ge(x_in[i], 16)
                    norm_rstd(i, xs, sq_mix)
                if i >= 2:
                    norm_hi(i - 2, i - 2, hS)
                if i == 7:
                    split_hi(0)
                if i == 5:
                    act.wait_ge(wpad_in, 32)
                    a(wpadS[0], wpad, ACT.Copy).then_inc(pad_hi, 1)

            act.wait_ge(hT_part, 2 * NT)
            for ch in range(2 * MH + 1):
                if ch < 2 * MH:
                    nm, c = ("mq", "mk")[ch // MH], ch % MH
                    if c % 2 == 0:
                        begin_piece(PIDX[nm, c // 2])
                    for hf in range(NH2):
                        if hf == 0 and ch >= 2:
                            act.wait_ge(conv_done, ch - 1)
                        n = TIDX[nm, c // 2, (c % 2) * NH2 + hf]
                        a(cin[:, ch % 2, CW - 1 + hf * BANK:CW - 1 + (hf + 1) * BANK], out_of(n),
                          ACT.Copy).then_inc(evac["act"], 1)
                if ch >= 1:
                    c = ch - 1
                    act.wait_ge(conv_done, c + 1)
                    v = (mqT if c < MH else mkT)[:, c % MH, :]
                    a(v, v, ACT.Silu).then_inc(silu_done, 1)

            def N_evacs(nm, c, dst, func=ACT.Copy):
                begin_piece(PIDX[nm, c])
                for i in range(NT // 2):
                    o = out_of(TIDX[nm, c, i]).rearrange("p (t n) -> p t n", t=2)
                    a(dst[:, 2 * i:2 * i + 2, c * PC:(c + 1) * PC], o, func).then_inc(evac["act"], 1)

            def v_evacs(c):
                begin_piece(PIDX["mv", c])
                for i in range(NT // 2):
                    o = out_of(TIDX["mv", c, i]).rearrange("p (t h e) -> p t h e", t=2, h=2)
                    for q in range(2):
                        ins = a(vaug[:, 2 * i + q, 2 * c:2 * c + 2, 0:DH], o[:, q, :, :], ACT.Copy)
                    ins.then_inc(evac["act"], 1)

            nc.scalar.preload_act_table_set("natural_log_exp_and_others")
            v_evacs(0)
            act.wait_ge(gate_dve, 1)
            link(a(grow[R_L], grow[R_L], ACT.Exp))
            a(grow[R_L], grow[R_L], ACT.Ln, bias=1.0).then_inc(gate_act, 1)
            v_evacs(1)
            act.wait_ge(gate_dve, 2)
            a(stack[32:32 + MH, :], grow[R_L], ACT.Exp).then_inc(gate_act, 1)
            a(stack[64:64 + MH, :], grow[R_F], ACT.Exp, scale=-1.0).then_inc(gate_act, 1)
            a(stack[96:96 + MH, :], grow[R_K], ACT.Exp).then_inc(gate_act, 1)
            a(wold[:], wold[:], ACT.Exp).then_inc(gate_act, 1)
            for c in range(2):
                N_evacs("mo", c, gate_o, ACT.Sigmoid)

            nc.scalar.preload_act_table_set("natural_log_exp_and_others")
            for c in range(NT):
                act.wait_ge(kn_ready, c + 1)
                if c == 0:
                    act.wait_ge(tile_out, piece_end(PIDX["mo", 1]))
                a(kN[:, c, :], psum[:, 6 + c % 2, :], ACT.Copy).then_inc(kn_done, 1)
            for c in range(NT + 1):
                if c < NT:
                    act.wait_ge(D_masked, c + 1)
                    a(Dm[c % 2], Dm[c % 2], ACT.Exp, scale=-1.0).then_inc(W_done, 1)
                if c == NT:
                    split_hi(PIDX["sq", 0])
                if c:
                    act.wait_ge(num_done, c)
                    for h in range(MH):
                        n = (c - 1) * MH + h
                        if n:
                            act.wait_ge(mss_done, n)
                        a(junk, vaug[:, c - 1, h, 0:DH], ACT.Square, accum_out=mss[:, n:n + 1]).then_inc(mss_done, 1)
            act.wait_ge(ml_fac, 1)
            link(a(mfac[:], mfac[:], ACT.Ln, bias=eps_col[:]))
            a(mfac[:], mfac[:], ACT.Exp, scale=-0.5).then_inc(ml_rs, 1)

            for c in range(2):
                begin_piece(PIDX["sq", c])
                for i in range(4):
                    o = out_of(TIDX["sq", c, i])
                    a(sqT[:, 2 * c + i // NH2, (i % NH2) * BANK:(i % NH2 + 1) * BANK], o, ACT.Copy,
                      scale=QSCALE).then_inc(evac["act"], 1)
            for c in range(2):
                begin_piece(PIDX["sk", c])
            N_evacs("sv", 0, svn)
            begin_piece(PIDX["sv", 1])
            for i in range(NT // 2 + 1):
                if i < NT // 2:
                    o = out_of(TIDX["sv", 1, i]).rearrange("p (t n) -> p t n", t=2)
                    a(svn[:, 2 * i:2 * i + 2, PC:2 * PC], o, ACT.Copy).then_inc(evac["act"], 1)
                if i:
                    for c in (2 * i - 2, 2 * i - 1):
                        act.wait_ge(yn_trans, c + 1)
                        a(hS[0][:, 0:MH, c * P:(c + 1) * P], psum[:, 4 + c % 2, :].rearrange("p (h s) -> p h s", h=MH),
                          ACT.Copy).then_inc(ym_hi, 1)

            for k in range(NS + 12):
                if k < NS:
                    lo = steps[k]["lo"]
                    z, l = zs[k % NZ], lt[k % NLT]
                    act.wait_ge(z_ready, k + 1)
                    if k >= NZ:
                        act.wait_ge(ex_done, k - NZ + 1)
                    a(z[:, lo:BANK], psum[:, k % 2, lo:BANK], ACT.Copy).then_inc(zs_done, 1)
                    act.wait_ge(ab_done, k + 1)
                    link(a(l[:, lo:BANK], l[:, lo:BANK], ACT.Exp))
                    a(l[:, lo:BANK], l[:, lo:BANK], ACT.Ln, bias=1.0).then_inc(l1_done, 1)
                i = k - 3
                if 0 <= i < NS:
                    lo = steps[i]["lo"]
                    if steps[i]["diag"]:
                        act.wait_ge(ex_masked, upto_diag(i))
                    act.wait_ge(ex_done, i + 1)
                    a(ex[i % NX][:, lo:BANK], ex[i % NX][:, lo:BANK], ACT.Exp).then_inc(a_done, 1)
                i = k - 5
                if 0 <= i < NS and steps[i]["last"]:
                    gi = steps[i]["g"]
                    act.wait_ge(av_done, i + 1)
                    if gi:
                        act.wait_ge(ossq_ready, gi)
                    a(osq, psum[:, 4 + gi % 2, :], ACT.Square).then_inc(osq_done, 1)
                if k == NS + 4:
                    split_hi(PIDX["w_out", 0])
                i = k - 7
                if 0 <= i < NS and steps[i]["last"]:
                    gi = steps[i]["g"]
                    act.wait_ge(ossq_ready, gi + 1)
                    if gi:
                        act.wait_ge(o_made, gi)
                    link(a(ors, psum[:, 6 + gi % 2, :], ACT.Ln, bias=eps_col[:], scale=1.0 / DH))
                    a(ors, ors, ACT.Exp, scale=-0.5).then_inc(ors_done, 1)
                i = k - 8
                if 0 <= i < NS and steps[i]["last"]:
                    s = steps[i]
                    act.wait_ge(o_made, s["g"] + 1)
                    a(hS[0][:, MH + s["h"], s["hf"] * BANK:(s["hf"] + 1) * BANK], of, ACT.Copy).then_inc(o_hi, 1)

            begin_piece(PIDX["w_out", 0])
            act.wait_ge(mem_in, 16 * MT)
            for i in range(MT + 1):
                if i < MT:
                    norm_rstd(i, mems, sq_kv)
                if i:
                    norm_hi(NT + i - 1, i - 1, mS)
            for c in range(1, 4):
                begin_piece(PIDX["w_out", c])
            for i in range(NT + 1):
                if i < NT:
                    nm, c = ("w_mk", "w_mv")[i // 4], i % 4
                    begin_piece(PIDX[nm, c])
                    wait_evac(act, TIDX["w_out", 3, i // 2])
                    norm_rstd(i, x1, sq_mem)
                    o = out_of(TIDX[nm, c, 0])
                    if nm == "w_mk":
                        a(kTm[:, 2 * c:2 * c + 2, :], o.rearrange("p (c m) -> p c m", c=2), ACT.Copy).then_inc(evac["act"], 1)
                    else:
                        a(vmem[:, :, c * PC:(c + 1) * PC], o.rearrange("p (t n) -> p t n", t=2),
                          ACT.Copy).then_inc(evac["act"], 1)
                if i:
                    norm_hi(NT + MT + i - 1, i - 1, hS)
            for c in range(4):
                begin_piece(PIDX["w_mq", c])
                for i in range(4):
                    o = out_of(TIDX["w_mq", c, i])
                    a(qT[:, 2 * c + i // NH2, (i % NH2) * BANK:(i % NH2 + 1) * BANK], o,
                      ACT.Copy).then_inc(evac["act"], 1)

            for k in range(NT + 1):
                if k < NT:
                    act.wait_ge(mx_done, k + 1)
                    if k >= 2:
                        act.wait_ge(pt_ready, k - 1)
                    for h in range(XH):
                        a(pnat[:, k % 2, h * MEM:(h + 1) * MEM],
                          psum[:, 4 + 2 * (k % 2) + h // 2, (h % 2) * MEM:(h % 2 + 1) * MEM], ACT.Exp,
                          bias=pmx[:, k, h:h + 1], scale=XSCALE, accum_out=psm[:, k, h:h + 1]).then_inc(p_done, 1)
                if k >= 1:
                    i = k - 1
                    act.wait_ge(pt_ready, i + 1)
                    if i == 0:
                        act.wait_ge(tile_out, piece_end(PIDX["w_mq", 3]))
                    if i == HALF:
                        act.wait_ge(tile_out, TIDX["oT", 0, KD - 1] + 1)
                    for q in range(2):
                        a(pT[:, 4 * q:4 * q + 4, (i % HALF) * P:(i % HALF + 1) * P],
                          psum[:, 2 * (i % 2) + q, :].rearrange("p (j s) -> p j s", j=4),
                          ACT.Copy).then_inc(pt_done, 1)
                    if i % HALF == HALF - 1:
                        hf = i // HALF
                        for c in range(KD):
                            n = TIDX["oT", 0, hf * KD + c]
                            a(hS[0][:, c, hf * BANK:(hf + 1) * BANK], out_of(n), ACT.Copy).then_inc(oT_hi, 1)
            for c in range(4):
                begin_piece(PIDX["w_mo", c])

            act.wait_ge(wpad_in, 64)
            act.wait_ge(tile_out, TIDX["oT", 0, 2 * KD - 1] + 1)
            a(rpadS[0], rpad, ACT.Copy).then_inc(pad_hi, 1)
            for i in range(0, NT + 2, 2):
                if i < NT:
                    wait_evac(act, TIDX["w_mo", 3, i // 2])
                    for q in range(2):
                        norm_rstd(i + q, x1, hn[:, i + q, :])
                if i:
                    for q in range(i - 2, i):
                        norm_hi(JF + q, q, hS)
            act.wait_ge(rt_dve, 1)
            a(r4["tmp"], r4["tmp"], ACT.Exp).then_inc(rt_act, 1)
            act.wait_ge(rt_dve, 2)
            a(r1["w2"], r1["w2"], ACT.Exp).then_inc(rt_act, 1)

            def expert_hi(e, q):
                act.wait_ge(moe_in[q], (e + 1) * 16)
                a(eparts[q][0], eraw[q], ACT.Copy).then_inc(e_hi, 1)

            act.sem_inc(sg_done, 1)
            act.sem_inc(y_evac, 1)
            act.wait_ge(rt_pe, NH2)
            for q in range(4):
                expert_hi(0, q)
            act.wait_ge(routed, 1)

            def x_hi(n):
                act.wait_ge(xt_ready, n)
                a(xTs[0], psum[:, 4:6, :].rearrange("p b (k s) -> p (b k) s", k=HALF), ACT.Copy).then_inc(xT_hi, 1)

            x_hi(1)
            act.wait_ge(h_stored, 16 * NT)
            for q in range(4, NQ):
                expert_hi(0, q)
            blk = act.alloc_register("act_block")
            act.reg_mov(blk, 0)

            def block_act(nxt):
                b = act.snap(blk, min_val=0, max_val=MAXB)
                act.wait_ge(a_ready, b + 1)
                act.wait_ge(hh_done, b * 2 + 2)
                a(sg, psum[:, 0, :], ACT.Silu).then_inc(sg_done, 1)
                if nxt is not None:
                    for q in range(2):
                        expert_hi(nxt, q)
                for q in range(2):
                    act.wait_ge(ht_ready, b * 2 + (q + 1))
                    a(hhTs[0][:, KF // 2 * q:KF // 2 * (q + 1), :],
                      psum[:, 6 + q, F // 2:F].rearrange("p (k s) -> p k s", k=KF // 2),
                      ACT.Copy).then_inc(hhT_hi, 1)
                x_hi(b + 2)
                if nxt is not None:
                    for q in range(2, 4):
                        expert_hi(nxt, q)
                act.wait_ge(y_ready, b + 2)
                act.wait_ge(y_stored, (b + 1) * 16)
                a(yb.rearrange("p (b n) -> p b n", b=2), psum[:, 2:4, :], ACT.Copy).then_inc(y_evac, 1)
                if nxt is not None:
                    for q in range(4, NQ):
                        expert_hi(nxt, q)
                act.reg_add(blk, blk, 1)

            def expert_act(e, nxt):
                n_more = act.value_load(nb_i[0:1, bass.ds(e, 1)], min_val=0, max_val=NT - 1)
                with act.If(n_more > 0):
                    with act.Fori(0, n_more) as _j:
                        block_act(None)
                block_act(nxt)

            nc.scalar.preload_act_table(ACT.Silu)
            with act.Fori(0, E - 1) as e:
                expert_act(e, e + 1)
            expert_act(E - 1, None)
            nc.scalar.preload_act_table_set("natural_log_exp_and_others")
            for i in range(NT):
                act.wait_ge(moe_added, i + 1)
                link(a(sq_out, x1[:, i, :], ACT.Square, accum_out=ss[:, i:i + 1]))
                link(a(lnt[:, i:i + 1], ss[:, i:i + 1], ACT.Ln, bias=eps_col[:], scale=1.0 / D))
                a(rstd[:, i:i + 1], lnt[:, i:i + 1], ACT.Exp, scale=-0.5).then_inc(fin_rs, 1)

        @block.vector
        def _(dve):
            chain = [0]
            v = nc.vector

            def link(ins):
                chain[0] += 1
                ins.then_inc(dve_chain, 1)
                dve.wait_ge(dve_chain, chain[0])

            def out_of(n):
                dve.wait_ge(tile_out, n + 1)
                return psum[:, n % RING, :]

            def split_lo(p):
                dve.wait_ge(w_hi, p + 1)
                buffer_free(dve, p)
                wait_raw(dve, p)
                v.tensor_tensor(wS[p % 2][1], raws[raw_no[p]], wS[p % 2][0].bitcast(F32), ALU.subtract).then_inc(w_lo, 1)

            def begin_piece(p):
                if p + 1 < NP and p + 1 not in LATE:
                    split_lo(p + 1)

            def norm_scale(j, i, src, natural=None):
                if natural is None:
                    o = htmp[:, j % 2, :]
                    if j >= 2:
                        dve.wait_ge(h_trans, j - 1)
                else:
                    o = natural[:, i, :]
                dve.wait_ge(rs_done, j + 1)
                v.tensor_scalar(o, src[:, i, :], rstd[:, i:i + 1], None, ALU.mult).then_inc(h_made, 1)

            def norm_parts(j, i, dst, goff):
                dve.wait_ge(h_trans, j + 1)
                if j:
                    dve.wait_ge(hT_part, 2 * j)
                for q in range(2):
                    v.tensor_tensor(tt[q].rearrange("p (k s) -> p k s", k=HALF),
                                    psum[:, 4 + 2 * (j % 2) + q, :].rearrange("p (k s) -> p k s", k=HALF),
                                    vecT[:, goff + HALF * q:goff + HALF * (q + 1)].unsqueeze(2).broadcast_to(
                                        [P, HALF, P]), ALU.mult).then_inc(scaled, 1)
                for q in range(2):
                    sl = (slice(None), slice(HALF * q, HALF * (q + 1)), slice(i * P, (i + 1) * P))
                    dve.wait_ge(hi_part, 2 * j + q + 1)
                    v.tensor_tensor(dst[1][sl], tt[q].rearrange("p (k s) -> p k s", k=HALF),
                                    dst[0][sl].bitcast(F32), ALU.subtract).then_inc(hT_part, 1)

            for i in range(NT + 1):
                if i < NT:
                    dve.wait_ge(x_in[i], 16)
                    norm_scale(i, i, xs)
                if i == 1:
                    dve.wait_ge(vec_tr, 1)
                    v.tensor_copy(vecT[:], psum[:, 0, 0:NV]).then_inc(vecT_ready, 1)
                    dve.wait_ge(vecT_ready, 1)
                if i:
                    norm_parts(i - 1, i - 1, hS, G_MIX)
                if i == 7:
                    split_lo(0)
                if i == 5:
                    dve.wait_ge(pad_hi, 1)
                    v.tensor_tensor(wpadS[1], wpad, wpadS[0].bitcast(F32), ALU.subtract).then_inc(pad_lo, 1)

            dve.wait_ge(h_trans, NT)
            dve.wait_ge(bias_in, 16 * N_BIAS)
            link(v.memset(stack, 0.0))
            for b in range(2):
                link(v.memset(cin[:, b, 0:CW - 1], 0.0))
            for hf in range(NH2):
                o = out_of(TIDX["gates", 0, hf])
                cs = slice(hf * BANK, (hf + 1) * BANK)
                link(v.tensor_scalar(grow[R_G][:, cs], o[0:MH, :], gbias[0:MH, :], None, ALU.add))
                v.tensor_scalar(grow[R_F][:, cs], o[32:32 + MH, :], gbias[32:32 + MH, :], None,
                                ALU.add).then_inc(evac["dve"], 1)
            for ch in range(2 * MH):
                nm, c = ("mq", "mk")[ch // MH], ch % MH
                if c % 2 == 0:
                    begin_piece(PIDX[nm, c // 2])
                wait_evac(dve, TIDX[nm, c // 2, (c % 2) * NH2 + 1])
                o = (mqT if ch < MH else mkT)[:, c, :]
                for tap in range(CW - 1, -1, -1):
                    w = vecT[:, V_CW + tap * 2 * MH + ch:V_CW + tap * 2 * MH + ch + 1]
                    src = cin[:, ch % 2, tap:tap + SEQ]
                    if tap == CW - 1:
                        link(v.tensor_scalar(o, src, w, vecT[:, V_CB + ch:V_CB + ch + 1], ALU.mult, ALU.add))
                    elif tap:
                        link(v.scalar_tensor_tensor(o, src, w, o, ALU.mult, ALU.add))
                    else:
                        v.scalar_tensor_tensor(o, src, w, o, ALU.mult, ALU.add).then_inc(conv_done, 1)
            link(v.memset(vaug[:, :, :, DH:DH + 1], 1.0))

            begin_piece(PIDX["mv", 0])
            chunk = [r.rearrange("p (c s) -> p c s", c=NT) for r in grow]
            mch = chunk[R_M]
            dve.wait_ge(conv_done, 2 * MH)
            wait_evac(dve, TIDX["gates", 0, 1])
            v.scalar_tensor_tensor(grow[R_L], grow[R_F], -1.0, grow[R_F], ALU.mult, ALU.min).then_inc(gate_dve, 1)
            link(v.memset(grow[R_K], 1.0))
            link(v.memset(chunk[R_K][:, :, 0:1], 0.0))
            dve.wait_ge(gate_act, 1)
            link(v.scalar_tensor_tensor(grow[R_L], grow[R_F], 0.0, grow[R_L], ALU.min, ALU.subtract))
            link(v.tensor_tensor_scan(grow[R_F], grow[R_K], grow[R_L], 0.0, ALU.mult, ALU.add))
            link(v.tensor_tensor(grow[R_G], grow[R_G], grow[R_F], ALU.subtract))
            link(v.memset(grow[R_K], 0.0))
            link(v.tensor_copy(chunk[R_K][:, 1:NT, 0:1], chunk[R_F][:, 0:NT - 1, P - 1:P]))
            link(v.tensor_tensor_scan(grow[R_M], grow[R_K], grow[R_G], 0.0, ALU.add, ALU.max))
            link(v.memset(mprev[:], 0.0))
            link(v.tensor_tensor(mprev[:, 1:NT].unsqueeze(2), chunk[R_F][:, 0:NT - 1, P - 1:P],
                                 mch[:, 0:NT - 1, P - 1:P], ALU.add))
            begin_piece(PIDX["mv", 1])
            link(v.tensor_tensor(chunk[R_L], mprev[:].unsqueeze(2).broadcast_to([MH, NT, P]), mch, ALU.subtract))
            link(v.tensor_tensor(grow[R_F], grow[R_F], grow[R_M], ALU.add))
            link(v.tensor_tensor(chunk[R_K], chunk[R_G], mch[:, :, P - 1:P].broadcast_to([MH, NT, P]), ALU.subtract))
            v.tensor_tensor(wold[:].unsqueeze(2), mprev[:].unsqueeze(2), mch[:, :, P - 1:P],
                            ALU.subtract).then_inc(gate_dve, 1)
            dve.wait_ge(gate_dve, 2)
            dve.wait_ge(gate_act, 5)
            v.tensor_scalar(stack[96:96 + MH, :], stack[96:96 + MH, :], QSCALE, None, ALU.mult).then_inc(gate_dve, 1)
            begin_piece(PIDX["mo", 0])
            dve.wait_ge(gate_pe, 1)
            for q in range(2):
                link(v.tensor_copy(cols[:, q * HALF:(q + 1) * HALF, :],
                                   psum[:, 4 + q, 0:HALF * GC].rearrange("p (c g) -> p c g", c=HALF)))
            v.tensor_copy(woldB, psum[:, 6, 0:MH * NT].rearrange("p (h c) -> p h c", h=MH)).then_inc(gate_dve, 1)
            dve.wait_ge(gate_dve, 4)

            def two_banks(b):
                return psum[:, b:b + 2, 0:2 * E1].rearrange("p b (h e) -> p b h e", h=2)

            def pairs(ap):
                return ap.rearrange("p (b h) e -> p b h e", b=2)

            def per_head(col, n):
                return col.rearrange("p (b h) -> p b h", b=2).unsqueeze(3).broadcast_to([P, 2, 2, n])

            def distance(c):
                dve.wait_ge(mb_ready, c + 1)
                if c >= 2:
                    dve.wait_ge(Pm_done, c - 1)
                v.tensor_tensor(Dm[c % 2].rearrange("p (h s) -> p h s", h=MH),
                                psum[:, 0, :].rearrange("p (h s) -> p h s", h=MH),
                                gcol[:, c, :].unsqueeze(2).broadcast_to([P, MH, P]), ALU.subtract).then_inc(D_done, 1)

            def weighted_values(c):
                if c >= 2:
                    dve.wait_ge(U_ready, c - 1)
                v.tensor_tensor(vsb[c % 2], vaug[:, c, :, :], wscol[:, c, :].unsqueeze(2).broadcast_to([P, MH, E1]),
                                ALU.mult).then_inc(vs_done, 1)

            dve.wait_ge(tile_out, piece_end(PIDX["mo", 1]))
            distance(0)
            weighted_values(0)
            for c in range(NT):
                dve.wait_ge(kq_ready, c + 1)
                dve.wait_ge(W_done, c + 1)
                if c >= 2:
                    dve.wait_ge(num_ready, c - 1)
                v.scalar_tensor_tensor(Pm[c % 2], psum[:, 1, :], QSCALE, Dm[c % 2], ALU.mult, ALU.mult).then_inc(Pm_done, 1)
                if c < NT - 1:
                    distance(c + 1)
                    weighted_values(c + 1)
                if c:
                    dve.wait_ge(inter_ready, c)
                    if c > 1:
                        dve.wait_ge(num_done, c)
                    v.tensor_tensor(pairs(inter), two_banks(4), per_head(wicol[:, c, :], E1), ALU.mult).then_inc(inter_done, 1)
                    dve.wait_ge(inter_done, c)
                dve.wait_ge(num_ready, c + 1)
                dve.wait_ge(vs_done, c + 1)
                if c:
                    v.tensor_tensor(pairs(vaug[:, c, :, :]), two_banks(2), pairs(inter), ALU.add).then_inc(num_done, 1)
                else:
                    v.tensor_copy(pairs(vaug[:, c, :, :]), two_banks(2)).then_inc(num_done, 1)
                if c < NT - 1:
                    dve.wait_ge(U_ready, c + 1)
                    if c:
                        dve.wait_ge(CT_done, c)
                        link(v.tensor_tensor(CT[(c + 1) % 2], CT[c % 2],
                                             woldB[:, :, c:c + 1].broadcast_to([P, MH, E1]), ALU.mult))
                        v.tensor_tensor(pairs(CT[(c + 1) % 2]), two_banks(6), pairs(CT[(c + 1) % 2]),
                                        ALU.add).then_inc(CT_done, 1)
                    else:
                        v.tensor_copy(pairs(CT[1]), two_banks(6)).then_inc(CT_done, 1)

            split_lo(PIDX["sq", 0])
            dve.wait_ge(mss_done, NT * MH)
            dve.wait_ge(num_done, NT)
            link(v.tensor_copy(mden[:].unsqueeze(3), vaug[:, :, :, DH:E1]))
            link(v.scalar_tensor_tensor(mfac[:], mden[:], -1.0, mden[:], ALU.mult, ALU.max))
            link(v.tensor_tensor(mden[:], mfac[:], flcol, ALU.max))
            link(v.reciprocal(mden[:], mden[:]))
            ms3 = mss[:].rearrange("p (c h) -> p c h", c=NT)
            link(v.tensor_tensor(mfac[:], mden[:], mden[:], ALU.mult))
            v.scalar_tensor_tensor(mfac[:], mfac[:], 1.0 / DH, ms3, ALU.mult, ALU.mult).then_inc(ml_fac, 1)
            dve.wait_ge(ml_rs, 1)
            link(v.tensor_tensor(mfac[:], mfac[:], mden[:], ALU.mult))
            dve.wait_ge(gate_scaled, NT)
            for c in range(NT):
                link(v.tensor_tensor(vaug[:, c, :, 0:DH], vaug[:, c, :, 0:DH],
                                     mfac[:, c, :].unsqueeze(2).broadcast_to([P, MH, DH]), ALU.mult))
                v.tensor_tensor(gate_o[:, c, :].rearrange("p (h e) -> p h e", h=MH), vaug[:, c, :, 0:DH],
                                gate_o[:, c, :].rearrange("p (h e) -> p h e", h=MH), ALU.mult).then_inc(yn_done, 1)

            for c in range(2):
                begin_piece(PIDX["sq", c])
            for c in range(2):
                begin_piece(PIDX["sk", c])
                for i in range(4):
                    o = out_of(TIDX["sk", c, i])
                    v.tensor_copy(skT[:, 2 * c + i // NH2, (i % NH2) * BANK:(i % NH2 + 1) * BANK],
                                  o).then_inc(evac["dve"], 1)
            for c in range(2):
                begin_piece(PIDX["sv", c])
            for c in range(NT):
                dve.wait_ge(ym_hi, c + 1)
                sl = (slice(None), slice(0, MH), slice(c * P, (c + 1) * P))
                v.tensor_tensor(hS[1][sl], psum[:, 4 + c % 2, :].rearrange("p (h s) -> p h s", h=MH),
                                hS[0][sl].bitcast(F32), ALU.subtract).then_inc(ym_done, 1)

            for k in range(NS + 12):
                if k < NS:
                    lo = steps[k]["lo"]
                    z = zs[k % NZ][:, lo:BANK]
                    dve.wait_ge(zs_done, k + 1)
                    if k >= NLT:
                        dve.wait_ge(L_done, k - NLT + 1)
                    v.scalar_tensor_tensor(lt[k % NLT][:, lo:BANK], z, -1.0, z, ALU.mult, ALU.min).then_inc(ab_done, 1)
                i = k - 1
                if 0 <= i < NS:
                    lo = steps[i]["lo"]
                    dve.wait_ge(l1_done, i + 1)
                    if i >= NL:
                        dve.wait_ge(tail_ready, i - NL + 1)
                        if upto_R(i - NL):
                            dve.wait_ge(R_done, upto_R(i - NL))
                    v.scalar_tensor_tensor(Lb[i % NL][:, lo:BANK], zs[i % NZ][:, lo:BANK], 0.0,
                                           lt[i % NLT][:, lo:BANK], ALU.max, ALU.add).then_inc(L_done, 1)
                i = k - 2
                if 0 <= i < NS:
                    lo = steps[i]["lo"]
                    dve.wait_ge(tail_ready, i + 1)
                    if i >= NX:
                        dve.wait_ge(av_done, i - NX + 1)
                    v.tensor_tensor(ex[i % NX][:, lo:BANK], zs[i % NZ][:, lo:BANK], psum[:, 2 + i % 2, lo:BANK],
                                    ALU.subtract).then_inc(ex_done, 1)
                i = k - 7
                if k == NS + 6:
                    split_lo(PIDX["w_out", 0])
                if 0 <= i < NS and steps[i]["last"]:
                    s = steps[i]
                    dve.wait_ge(ors_done, s["g"] + 1)
                    if s["g"]:
                        dve.wait_ge(sb_out, s["g"])
                    v.scalar_tensor_tensor(of, psum[:, 4 + s["g"] % 2, :], vecT[:, V_SBG + s["h"]:V_SBG + s["h"] + 1],
                                           ors, ALU.mult, ALU.mult).then_inc(o_made, 1)
                i = k - 8
                if 0 <= i < NS and steps[i]["last"]:
                    s = steps[i]
                    dve.wait_ge(o_hi, s["g"] + 1)
                    sl = (slice(None), MH + s["h"], slice(s["hf"] * BANK, (s["hf"] + 1) * BANK))
                    v.tensor_tensor(hS[1][sl], of, hS[0][sl].bitcast(F32), ALU.subtract).then_inc(sb_out, 1)

            def residual_pair(nm, c, i):
                if (nm, c) == ("w_out", 0):
                    for q in range(2):
                        dve.wait_ge(x_in[2 * i + q], 32)
                o = out_of(TIDX[nm, c, i]).rearrange("p (t n) -> p t n", t=2)
                xt = x1[:, 2 * i:2 * i + 2, c * PC:(c + 1) * PC]
                v.tensor_tensor(xt, xt, o, ALU.add).then_inc(evac["dve"], 1)

            def add_residual(nm, c):
                begin_piece(PIDX[nm, c])
                for i in range(NT // 2):
                    residual_pair(nm, c, i)

            add_residual("w_out", 0)
            for i in range(MT + 1):
                if i < MT:
                    norm_scale(NT + i, i, mems)
                if i:
                    norm_parts(NT + i - 1, i - 1, mS, G_KV)
            for c in range(1, 4):
                add_residual("w_out", c)
            dve.wait_ge(tile_out, piece_end(PIDX["w_out", 3]))
            for i in range(NT + 1):
                if i < NT:
                    begin_piece(PIDX[("w_mk", "w_mv")[i // 4], i % 4])
                    norm_scale(NT + MT + i, i, x1)
                if i:
                    norm_parts(NT + MT + i - 1, i - 1, hS, G_MEM)
            for c in range(4):
                begin_piece(PIDX["w_mq", c])
            for k in range(NT + 1):
                if k < NT:
                    dve.wait_ge(sc_ready, k + 1)
                    link(v.tensor_reduce(pmx[:, k, :], psum[:, 4 + 2 * (k % 2):6 + 2 * (k % 2), :].rearrange(
                        "p b (h m) -> p (b h) m", h=2), AX.X, ALU.max))
                    v.tensor_scalar(pmx[:, k, :], pmx[:, k, :], -XSCALE, None, ALU.mult).then_inc(mx_done, 1)
                    dve.wait_ge(p_done, XH * (k + 1))
                    link(v.reciprocal(psm[:, k, :], psm[:, k, :]))
                    pk = pnat[:, k % 2, :].rearrange("p (h m) -> p h m", h=XH)
                    v.tensor_tensor(pk, pk, psm[:, k, :].unsqueeze(2).broadcast_to([P, XH, MEM]),
                                    ALU.mult).then_inc(pn_done, 1)
                if k >= 1 and (k - 1) % HALF == HALF - 1:
                    hf = (k - 1) // HALF
                    for c in range(KD):
                        n = TIDX["oT", 0, hf * KD + c]
                        sl = (slice(None), c, slice(hf * BANK, (hf + 1) * BANK))
                        dve.wait_ge(oT_hi, hf * KD + c + 1)
                        v.tensor_tensor(hS[1][sl], out_of(n), hS[0][sl].bitcast(F32),
                                        ALU.subtract).then_inc(evac["dve"], 1)
            for c in range(2):
                add_residual("w_mo", c)
            begin_piece(PIDX["w_mo", 2])
            dve.wait_ge(pad_hi, 2)
            v.tensor_tensor(rpadS[1], rpad, rpadS[0].bitcast(F32), ALU.subtract).then_inc(pad_lo, 1)
            dve.wait_ge(pad_lo, 2)
            for i in range(0, NT + 2, 2):
                if i < NT:
                    for c in (2, 3):
                        residual_pair("w_mo", c, i // 2)
                    for q in range(2):
                        norm_scale(JF + i + q, i + q, x1, hn)
                if i:
                    for q in range(i - 2, i):
                        norm_parts(JF + q, q, hS, G_FFN)
            for hf in range(NH2):
                dve.wait_ge(rt_pe, hf + 1)
                v.tensor_scalar(lgT[:, hf * BANK:(hf + 1) * BANK], psum[0:NR, hf, :], rbias[:], None,
                                ALU.add).then_inc(lgT_done, 1)
            dve.wait_ge(rt_pe, NH2 + 1)
            link(v.tensor_copy(lg, psum[:, 2, 0:NT * NR].rearrange("p (t r) -> p t r", t=NT)))

            def over4(col):
                return col.unsqueeze(2).broadcast_to([P, NT, 4])

            def first_max(dst, src, mx):
                link(v.tensor_reduce(mx, src, AX.X, ALU.max))
                link(v.tensor_tensor(r4["eq"], src, over4(mx), ALU.is_equal))
                link(v.memset(r1["left"], 1.0))
                for j in range(4):
                    link(v.tensor_tensor(dst[:, :, j], r4["eq"][:, :, j], r1["left"], ALU.mult))
                    if j < 3:
                        link(v.tensor_tensor(r1["left"], r1["left"], dst[:, :, j], ALU.subtract))

            oh, t1, t2, es = (r4[n] for n in ("oh", "t1", "t2", "es"))
            first_max(oh, lg[:, :, 0:NG], r1["mx"])
            v.tensor_tensor(r4["tmp"], lg[:, :, 0:NG], over4(r1["mx"]), ALU.subtract).then_inc(rt_dve, 1)
            M = re["M"]
            link(v.tensor_tensor(M, elt, oh.unsqueeze(3).broadcast_to([P, NT, NG, NE]), ALU.mult))
            link(v.tensor_reduce(es, M.rearrange("p t g e -> p t e g"), AX.X, ALU.add))
            first_max(t1, es, r1["m1"])
            link(v.scalar_tensor_tensor(es, t1, NEG, es, ALU.mult, ALU.add))
            first_max(t2, es, r1["m2"])
            v.tensor_tensor(r1["w2"], r1["m2"], r1["m1"], ALU.subtract).then_inc(rt_dve, 1)
            g4 = [P, NT, NG, NE]
            link(v.tensor_tensor(re["A1"], oh.unsqueeze(3).broadcast_to(g4), t1.unsqueeze(2).broadcast_to(g4), ALU.mult))
            link(v.tensor_tensor(re["A2"], oh.unsqueeze(3).broadcast_to(g4), t2.unsqueeze(2).broadcast_to(g4), ALU.mult))
            v.tensor_tensor(M, re["A1"], re["A2"], ALU.add).then_inc(rt_dve, 1)
            link(v.memset(rc["one"], 1.0))
            link(v.memset(cont, 1.0))
            link(v.memset(cont[:, :, 0:1], 0.0))
            for b in range(NT):
                link(v.memset(full[:, :, b:b + 1], float(b * P) if b else -1.0))
            dve.wait_ge(rt_pe, NH2 + 2)
            flat = re["pos"].rearrange("p t g e -> p t (g e)")
            nb, cum, one, base = (rc[n] for n in ("nb", "cum", "one", "base"))
            link(v.tensor_copy(tile_cnt, psum[:, 1, NT * E:2 * NT * E].rearrange("p (t e) -> p e t", t=NT)))
            link(v.tensor_tensor_scan(run_cnt.rearrange("p e t -> p (e t)"), cont.rearrange("p e t -> p (e t)"),
                                      tile_cnt.rearrange("p e t -> p (e t)"), 0.0, ALU.mult, ALU.add))
            link(v.tensor_tensor(tile_cnt, run_cnt, tile_cnt, ALU.subtract))
            link(v.tensor_tensor(flat, tile_cnt.rearrange("p e t -> p t e"),
                                 psum[:, 1, 0:NT * E].rearrange("p (t e) -> p t e", t=NT), ALU.add))
            link(v.tensor_tensor(over, run_cnt[:, :, NT - 1:NT].broadcast_to([P, E, NT]), full, ALU.is_gt))
            link(v.tensor_reduce(nb, over, AX.X, ALU.add))
            link(v.tensor_tensor_scan(cum, one, nb, 0.0, ALU.mult, ALU.add))
            link(v.tensor_tensor(base, cum, nb, ALU.subtract))
            link(v.tensor_scalar(base, base, float(P), None, ALU.mult))
            link(v.tensor_tensor(flat, flat, base.unsqueeze(1).broadcast_to([P, NT, E]), ALU.add))
            for c, A in enumerate((re["A1"], re["A2"])):
                link(v.tensor_tensor(M, A, re["pos"], ALU.mult))
                link(v.tensor_reduce(r1["pos"], M, AX.XY, ALU.add))
                link(v.tensor_copy(idx[:, c, :], r1["pos"]))
            link(v.tensor_scalar(nb_i[:], nb[0:1, :], -1.0, None, ALU.add))
            v.tensor_copy(cum_i[:], cum[0:1, :]).then_inc(routed, 1)
            dve.wait_ge(rt_act, 2)
            link(v.tensor_reduce(r1["psel"], r4["tmp"], AX.X, ALU.add))
            link(v.tensor_scalar(r1["w1"], r1["w2"], 1.0, None, ALU.add))
            link(v.tensor_tensor(r1["w1"], r1["w1"], r1["psel"], ALU.mult))
            link(v.reciprocal(r1["w1"], r1["w1"]))
            link(v.tensor_tensor(r1["w2"], r1["w2"], r1["w1"], ALU.mult))

            def expert_lo(e, q, b=None):
                dve.wait_ge(e_hi, e * NQ + q + 1)
                dve.wait_ge(moe_in[q], (e + 1) * 16)
                if b is not None:
                    if q < 2:
                        dve.wait_ge(a_ready, b + 1)
                    elif q < 4:
                        dve.wait_ge(u_ready, b * 2 + 2)
                    else:
                        dve.wait_ge(y_ready, b + 2)
                v.tensor_tensor(eparts[q][1], eraw[q], eparts[q][0].bitcast(F32), ALU.subtract).then_inc(e_lo, 1)

            for q in range(4):
                expert_lo(0, q)
            dve.wait_ge(routed, 1)
            dve.sem_inc(hh_done, 2)

            def x_lo(n):
                dve.wait_ge(xt_ready, n)
                dve.wait_ge(xT_hi, n)
                v.tensor_tensor(xTs[1], psum[:, 4:6, :].rearrange("p b (k s) -> p (b k) s", k=HALF),
                                xTs[0].bitcast(F32), ALU.subtract).then_inc(xT_done, 1)

            x_lo(1)
            for q in range(4, NQ):
                expert_lo(0, q)
            blk = dve.alloc_register("dve_block")
            dve.reg_mov(blk, 0)

            def block_dve(nxt):
                b = dve.snap(blk, min_val=0, max_val=MAXB)
                if nxt is not None:
                    expert_lo(nxt, 0, b)
                dve.wait_ge(sg_done, b + 2)
                for q in range(2):
                    cols = slice(F // 2 * q, F // 2 * (q + 1))
                    dve.wait_ge(u_ready, b * 2 + (q + 1))
                    v.tensor_tensor(hh[:, cols], sg[:, cols], psum[:, (1, 7)[q], 0:F // 2], ALU.mult).then_inc(hh_done, 1)
                if nxt is not None:
                    expert_lo(nxt, 1, b)
                dve.wait_ge(ht_ready, b * 2 + 2)
                dve.wait_ge(hhT_hi, b * 2 + 2)
                v.tensor_tensor(hhTs[1].rearrange("p k s -> p (k s)").rearrange("p (q n) -> p q n", q=2),
                                psum[:, 6:8, F // 2:F],
                                hhTs[0].rearrange("p k s -> p (k s)").rearrange("p (q n) -> p q n", q=2).bitcast(F32),
                                ALU.subtract).then_inc(hhT_done, 1)
                x_lo(b + 2)
                if nxt is not None:
                    for q in range(2, NQ):
                        expert_lo(nxt, q, b)
                dve.reg_add(blk, blk, 1)

            def expert_dve(e, nxt):
                n_more = dve.value_load(nb_i[0:1, bass.ds(e, 1)], min_val=0, max_val=NT - 1)
                with dve.If(n_more > 0):
                    with dve.Fori(0, n_more) as _j:
                        block_dve(None)
                block_dve(nxt)

            with dve.Fori(0, E - 1) as e:
                expert_dve(e, e + 1)
            expert_dve(E - 1, None)
            for i in range(NT + 1):
                if i < NT:
                    dve.wait_ge(yg_in[i], 32)
                    dve.wait_ge(x_in[i], 48)
                    link(v.scalar_tensor_tensor(x1[:, i, :], yg_t[i][0], r1["w1"][:, i:i + 1], x1[:, i, :],
                                                ALU.mult, ALU.add))
                    v.scalar_tensor_tensor(x1[:, i, :], yg_t[i][1], r1["w2"][:, i:i + 1], x1[:, i, :], ALU.mult,
                                           ALU.add).then_inc(moe_added, 1)
                if i:
                    k = i - 1
                    dve.wait_ge(fin_rs, i)
                    if k == 0:
                        dve.wait_ge(gfin_in, 16)
                    v.scalar_tensor_tensor(otile[k], x1[:, k, :], rstd[:, k:k + 1], gfin, ALU.mult,
                                           ALU.mult).then_inc(out_made, 1)

        @block.tensor
        def _(pe):
            te = nc.tensor
            pe.wait_ge(vec_in, 16 * len(VECS))
            pe.wait_ge(const_made, 6)
            te.transpose(psum[:, 0, 0:NV], vec_rows[:], ident[0:NV, 0:NV]).then_inc(vec_tr, 1)

            def norm_transposes(j, src):
                pe.wait_ge(h_made, j + 1)
                if j >= 2:
                    pe.wait_ge(scaled, 2 * (j - 1))
                for k in range(KD):
                    last = te.transpose(psum[:, 4 + 2 * (j % 2) + k // HALF, (k % HALF) * P:(k % HALF + 1) * P],
                                        src[:, k * P:(k + 1) * P], ident[:])
                last.then_inc(h_trans, 1)

            def open_tile(n):
                if n >= RING:
                    wait_evac(pe, n - RING)
                return psum[:, n % RING, :]

            def product(o, lhs, rhs, n):
                for k in range(n):
                    te.matmul(o, lhs(0, k), rhs(0, k), start=(k == 0), stop=False)
                    te.matmul(o, lhs(0, k), rhs(1, k), start=False, stop=False)
                    last = te.matmul(o, lhs(1, k), rhs(0, k), start=False, stop=(k == n - 1))
                return last

            def T_tile(nm, c, i, xS, cols=BANK, normed=None):
                w = wS[PIDX[nm, c] % 2]
                per = xS[0].shape[2] // cols
                in_bank = BANK // cols
                o = open_tile(TIDX[nm, c, i])
                for q in range(in_bank):
                    ch, part = (i * in_bank + q) // per, (i * in_bank + q) % per
                    if normed is not None:
                        pe.wait_ge(hT_part, 2 * (normed + HALF * (part + 1)))
                    last = product(o[:, q * cols:(q + 1) * cols],
                                   lambda z, k: w[z][:, k, ch * P:(ch + 1) * P],
                                   lambda z, k: xS[z][:, k, part * cols:(part + 1) * cols], KD)
                last.then_inc(tile_out, 1)

            def T_piece(nm, c, xS, cols=BANK, normed=None, first=0):
                pe.wait_ge(w_lo, PIDX[nm, c] + 1)
                for i in range(first, 2 * xS[0].shape[2] // BANK):
                    T_tile(nm, c, i, xS, cols, normed)

            def N_piece(nm, c, xS):
                pe.wait_ge(w_lo, PIDX[nm, c] + 1)
                for i in range(xS[0].shape[2] // (2 * P)):
                    N_tile(nm, c, i, xS)

            def N_tile(nm, c, i, xS):
                w = wS[PIDX[nm, c] % 2]
                n = TIDX[nm, c, i]
                o = open_tile(n)
                for q in range(2):
                    tk = 2 * i + q
                    last = product(o[:, q * PC:(q + 1) * PC], lambda z, k: xS[z][:, k, tk * P:(tk + 1) * P],
                                   lambda z, k: w[z][:, k, :], KD)
                last.then_inc(tile_out, 1)

            def gates(hf):
                pe.wait_ge(hT_part, 2 * HALF * (hf + 1))
                o = open_tile(TIDX["gates", 0, hf])
                product(o[0:GW, :], lambda z, k: wpadS[z][:, k, :],
                        lambda z, k: hS[z][:, k, hf * BANK:(hf + 1) * BANK], KD).then_inc(tile_out, 1)

            for i in range(NT):
                norm_transposes(i, htmp[:, i % 2, :])
                if i == 5:
                    pe.wait_ge(vecT_ready, 1)
                    pe.wait_ge(pad_lo, 1)
                    gates(0)
            pe.wait_ge(w_lo, 1)
            T_tile("mq", 0, 0, hS, normed=0)
            gates(1)
            T_piece("mq", 0, hS, first=1)
            for nm, c in (("mq", 1), ("mk", 0), ("mk", 1)):
                T_piece(nm, c, hS)
            for c in range(2):
                N_piece("mv", c, hS)
            N_piece("mo", 0, hS)
            pe.wait_ge(gate_dve, 3)
            pe.wait_ge(gate_act, 5)
            for c in range(NT):
                te.transpose(psum[:, 4 + c // HALF, (c % HALF) * GC:(c % HALF + 1) * GC],
                             stack[0:GC, c * P:(c + 1) * P], ident[0:GC, 0:GC])
            for h in range(MH):
                last = te.matmul(psum[:, 6, h * NT:(h + 1) * NT], sel[:, h, :], wold[:], start=True, stop=True)
            last.then_inc(gate_pe, 1)
            N_piece("mo", 1, hS)

            wait_evac(pe, TIDX["mo", 1, NT // 2 - 1])
            pe.wait_ge(gate_dve, 4)
            pe.wait_ge(silu_done, 2 * MH)
            for c in range(NT):
                if c >= 2:
                    pe.wait_ge(kn_done, c - 1)
                for h in range(MH):
                    last = te.transpose(psum[:, 6 + c % 2, h * P:(h + 1) * P], mkT[:, h, c * P:(c + 1) * P], ident[:])
                last.then_inc(kn_ready, 1)

            def at_head(b, h):
                return psum[:, b + h // 2, (h % 2) * E1:(h % 2 + 1) * E1]

            def max_rows(c):
                if c:
                    pe.wait_ge(D_done, c)
                for h in range(MH):
                    last = te.matmul(psum[:, 0, h * P:(h + 1) * P], sel[:, h, :], mrow[:, c * P:(c + 1) * P],
                                     start=True, stop=True)
                last.then_inc(mb_ready, 1)

            def scores(c):
                if c:
                    pe.wait_ge(Pm_done, c)
                for h in range(MH):
                    last = te.matmul(psum[:, 1, h * P:(h + 1) * P], mkT[:, h, c * P:(c + 1) * P],
                                     mqT[:, h, c * P:(c + 1) * P], start=True, stop=True)
                last.then_inc(kq_ready, 1)

            max_rows(0)
            scores(0)
            pe.wait_ge(kn_done, NT)
            for c in range(NT):
                cs = slice(c * P, (c + 1) * P)
                if c < NT - 1:
                    max_rows(c + 1)
                    pe.wait_ge(vs_done, c + 1)
                    if c:
                        pe.wait_ge(CT_done, c)
                    for h in range(MH):
                        last = te.matmul(at_head(6, h), kN[:, c, h * P:(h + 1) * P], vsb[c % 2][:, h, :],
                                         start=True, stop=True)
                    last.then_inc(U_ready, 1)
                if c:
                    pe.wait_ge(CT_done, c)
                    pe.wait_ge(num_done, c)
                    for h in range(MH):
                        last = te.matmul(at_head(4, h), mqT[:, h, cs], CT[c % 2][:, h, :], start=True, stop=True)
                    last.then_inc(inter_ready, 1)
                pe.wait_ge(Pm_done, c + 1)
                if c:
                    pe.wait_ge(num_done, c)
                for h in range(MH):
                    last = te.matmul(at_head(2, h), Pm[c % 2][:, h * P:(h + 1) * P], vaug[:, c, h, :],
                                     start=True, stop=True)
                last.then_inc(num_ready, 1)
                if c < NT - 1:
                    scores(c + 1)

            for c in range(2):
                T_piece("sq", c, hS)
            for c in range(2):
                T_piece("sk", c, hS)
            N_piece("sv", 0, hS)
            pe.wait_ge(w_lo, PIDX["sv", 1] + 1)
            for i in range(NT // 2 + 1):
                if i < NT // 2:
                    N_tile("sv", 1, i, hS)
                if i:
                    for c in (2 * i - 2, 2 * i - 1):
                        pe.wait_ge(yn_done, c + 1)
                        if c >= 2:
                            pe.wait_ge(ym_done, c - 1)
                        for h in range(MH):
                            last = te.transpose(psum[:, 4 + c % 2, h * P:(h + 1) * P],
                                                gate_o[:, c, h * P:(h + 1) * P], ident[:])
                        last.then_inc(yn_trans, 1)

            for i in range(4):
                wait_evac(pe, TIDX["sv", 1, i])
            wait_evac(pe, TIDX["sk", 1, 3])
            pe.wait_ge(ym_done, NT)
            for k in range(NS + 12):
                if k < NS:
                    s = steps[k]
                    lo = s["lo"]
                    if k >= 2:
                        pe.wait_ge(zs_done, k - 1)
                    te.matmul(psum[:, k % 2, lo:BANK], skT[:, s["h"], s["j"] * P:(s["j"] + 1) * P],
                              sqT[:, s["h"], s["hf"] * BANK + lo:(s["hf"] + 1) * BANK],
                              start=True, stop=True).then_inc(z_ready, 1)
                i = k - 2
                if 0 <= i < NS:
                    s = steps[i]
                    lo = s["lo"]
                    if s["diag"]:
                        pe.wait_ge(Lmasked, upto_diag(i))
                    pe.wait_ge(L_done, i + 1)
                    if i >= 2:
                        pe.wait_ge(ex_done, i - 1)
                    if not s["first"]:
                        pe.wait_ge(R_done, upto_R(i - 1))
                        te.matmul(psum[:, 2 + i % 2, lo:BANK], ones[:], Rb[i % NRB][:, lo:BANK], start=True, stop=False)
                    te.matmul(psum[:, 2 + i % 2, lo:BANK], uincl[:], Lb[i % NL][:, lo:BANK],
                              start=s["first"], stop=True).then_inc(tail_ready, 1)
                i = k - 4
                if 0 <= i < NS:
                    s = steps[i]
                    lo = s["lo"]
                    if s["first"] and s["g"] >= 2:
                        pe.wait_ge(o_made, s["g"] - 1)
                    pe.wait_ge(a_done, i + 1)
                    te.matmul(psum[:, 4 + s["g"] % 2, lo:BANK], svn[:, s["j"], s["h"] * DH:(s["h"] + 1) * DH],
                              ex[i % NX][:, lo:BANK], start=s["first"], stop=s["last"],
                              skip_group_check=True).then_inc(av_done, 1)
                i = k - 6
                if 0 <= i < NS and steps[i]["last"]:
                    gi = steps[i]["g"]
                    pe.wait_ge(osq_done, gi + 1)
                    if gi >= 2:
                        pe.wait_ge(ors_done, gi - 1)
                    te.matmul(psum[:, 6 + gi % 2, :], ones[:], osq, start=True, stop=True).then_inc(ossq_ready, 1)

            pe.wait_ge(sb_out, NGRP)
            N_piece("w_out", 0, hS)
            for i in range(MT):
                norm_transposes(NT + i, htmp[:, (NT + i) % 2, :])
            for c in range(1, 4):
                N_piece("w_out", c, hS)
            pe.wait_ge(hT_part, 2 * (NT + MT))
            for i in range(NT):
                if i < 4:
                    T_piece("w_mk", i, mS, MEM)
                else:
                    N_piece("w_mv", i - 4, mS)
                norm_transposes(NT + MT + i, htmp[:, (NT + MT + i) % 2, :])
            for c in range(4):
                T_piece("w_mq", c, hS, normed=NT + MT)

            wait_evac(pe, TIDX["w_mq", 3, 3])
            JH = XD // P
            for k in range(NT + 1):
                if k < NT:
                    if k >= 2:
                        pe.wait_ge(p_done, XH * (k - 1))
                    for h in range(XH):
                        for j in range(JH):
                            last = te.matmul(psum[:, 4 + 2 * (k % 2) + h // 2, (h % 2) * MEM:(h % 2 + 1) * MEM],
                                             qT[:, JH * h + j, k * P:(k + 1) * P], kTm[:, JH * h + j, :],
                                             start=(j == 0), stop=(j == JH - 1))
                    last.then_inc(sc_ready, 1)
                if k >= 1:
                    i = k - 1
                    pe.wait_ge(pn_done, i + 1)
                    if i >= 2:
                        pe.wait_ge(pt_done, 2 * (i - 1))
                    if i == HALF:
                        wait_evac(pe, TIDX["oT", 0, KD - 1])
                    for q in range(2 * XH):
                        last = te.transpose(psum[:, 2 * (i % 2) + q // 4, (q % 4) * P:(q % 4 + 1) * P],
                                            pnat[:, i % 2, q * P:(q + 1) * P], ident[:])
                    last.then_inc(pt_ready, 1)
                    if i % HALF == HALF - 1:
                        hf = i // HALF
                        pe.wait_ge(pt_done, 2 * (i + 1))
                        for c in range(KD):
                            n = TIDX["oT", 0, hf * KD + c]
                            o = open_tile(n)
                            for m in range(MT):
                                last = te.matmul(o, vmem[:, m, c * P:(c + 1) * P], pT[:, MT * (c // JH) + m, :],
                                                 start=(m == 0), stop=(m == MT - 1))
                            last.then_inc(tile_out, 1)
            wait_evac(pe, TIDX["oT", 0, 2 * KD - 1])
            for c in range(2):
                N_piece("w_mo", c, hS)

            def router(hf):
                pe.wait_ge(hT_part, 2 * (JF + HALF * (hf + 1)))
                product(psum[0:100, hf, :], lambda z, k: rpadS[z][:, k, :],
                        lambda z, k: hS[z][:, k, hf * BANK:(hf + 1) * BANK], KD).then_inc(rt_pe, 1)

            pe.wait_ge(w_lo, NP)
            for i in range(NT // 2):
                for c in (2, 3):
                    N_tile("w_mo", c, i, hS)
                if i:
                    for q in range(2 * i - 2, 2 * i):
                        norm_transposes(JF + q, hn[:, q, :])
            wait_evac(pe, len(tiles) - 1)
            pe.wait_ge(pad_lo, 2)
            router(0)
            for q in range(NT - 2, NT):
                norm_transposes(JF + q, hn[:, q, :])
            router(1)
            for i in range(NT):
                pe.wait_ge(lgT_done, i // HALF + 1)
                last = te.transpose(psum[:, 2, i * NR:(i + 1) * NR], lgT[:, i * P:(i + 1) * P], ident[0:NR, 0:NR])
            last.then_inc(rt_pe, 1)
            pe.wait_ge(rt_dve, 3)
            Mf = re["M"].rearrange("p t g e -> p (t g e)")
            te.matmul(psum[:, 1, 0:NT * E], ustrict[:], Mf, start=True, stop=True)
            te.matmul(psum[:, 1, NT * E:2 * NT * E], ones[:], Mf, start=True, stop=True).then_inc(rt_pe, 1)
            pe.wait_ge(routed, 1)

            def x_transposes(q):
                for k in range(HALF * q, HALF * (q + 1)):
                    last = te.transpose(psum[:, 4 + k // HALF, (k % HALF) * P:(k % HALF + 1) * P],
                                        xb[:, k * P:(k + 1) * P], ident[:])
                if q == 1:
                    last.then_inc(xt_ready, 1)

            pe.sem_inc(y_ready, 1)
            pe.wait_ge(xb_in, 16)
            for q in range(2):
                x_transposes(q)
            blk = pe.alloc_register("pe_block")
            pe.reg_mov(blk, 0)

            def in_product(o, w, e, q0, cols):
                for h in range(2):
                    pe.wait_ge(e_lo, e * NQ + (q0 + h + 1))
                    for k in range(h * (KD // 2), (h + 1) * (KD // 2)):
                        te.matmul(o, xTs[0][:, k, :], w[0][:, k, cols], start=(k == 0), stop=False)
                        te.matmul(o, xTs[0][:, k, :], w[1][:, k, cols], start=False, stop=False)
                        last = te.matmul(o, xTs[1][:, k, :], w[0][:, k, cols], start=False, stop=(k == KD - 1))
                return last

            def out_part(ks, z, zw, stop=False):
                for c in range(2):
                    for k in ks:
                        last = te.matmul(psum[:, 2 + c, :], hhTs[z][:, k, :], w2s[zw][:, k, c * BANK:(c + 1) * BANK],
                                         start=(k == 0 and z == 0 and zw == 0), stop=stop and k == KF - 1)
                return last

            def block_pe(e):
                b = pe.snap(blk, min_val=0, max_val=MAXB)
                pe.wait_ge(xT_done, b + 1)
                pe.wait_ge(sg_done, b + 1)
                in_product(psum[:, 0, :], w1s, e, 0, slice(0, F)).then_inc(a_ready, 1)
                pe.wait_ge(hh_done, b * 2 + 2)
                for q in range(2):
                    cols = slice(F // 2 * q, F // 2 * (q + 1))
                    in_product(psum[:, (1, 7)[q], 0:F // 2], w3s, e, 2, cols).then_inc(u_ready, 1)
                pe.wait_ge(xb_in, (b + 2) * 16)
                for q in range(2):
                    pe.wait_ge(hh_done, b * 2 + (q + 3))
                    for k in range(KF // 2 * q, KF // 2 * (q + 1)):
                        last = te.transpose(psum[:, 6 + q, (k % 2 + 2) * P:(k % 2 + 3) * P], hh[:, k * P:(k + 1) * P], ident[:])
                    last.then_inc(ht_ready, 1)
                    x_transposes(q)
                pe.wait_ge(e_lo, e * NQ + NQ)
                pe.wait_ge(y_evac, b + 1)
                for q in range(2):
                    pe.wait_ge(hhT_hi, b * 2 + (q + 1))
                    ks = range(KF // 2 * q, KF // 2 * (q + 1))
                    out_part(ks, 0, 0)
                    out_part(ks, 0, 1)
                pe.wait_ge(hhT_done, b + 1)
                out_part(range(KF), 1, 0, stop=True).then_inc(y_ready, 1)
                pe.reg_add(blk, blk, 1)

            with pe.Fori(0, E) as e:
                n_more = pe.value_load(nb_i[0:1, bass.ds(e, 1)], min_val=0, max_val=NT - 1)
                with pe.Fori(0, n_more + 1) as _j:
                    block_pe(e)


def kernel(**inputs):
    import numpy as np
    import concourse.bacc as bacc
    from concourse.bass_utils import run_bass_kernel_spmd as run

    nc = bacc.Bacc("TRN2", target_bir_lowering=False, num_devices=1)
    arrays, t = {}, {}
    for name in sorted(inputs):
        arrays["in_" + name] = np.ascontiguousarray(inputs[name])
        t[name] = nc.dram_tensor("in_" + name, arrays["in_" + name].shape, F32, kind="ExternalInput").ap()
    shape = tuple(inputs["x"].shape)
    out = nc.dram_tensor("out", shape, F32, kind="ExternalOutput").ap()
    hybrid_layer(nc, t, out)
    return run(nc, [arrays], core_ids=[0]).results[0]["out"]
```
